# Optimizing a Trainium2 kernel written in Bass

```python
import math
import jax, jax.numpy as jnp
from jax import lax
import numpy as np

D_MODEL = 1024
BATCH = 1
SEQ = 512
DEPTH = 2

CHUNK = 64
Q_BLOCK = 128
EPS = 1e-6
NEG = -1e30

H_A = 8
DA_NOPE = 64
DA_ROPE = 32
DA_V = 64
Q_LORA = 256
KV_LORA = 128
ROPE_THETA = 10000.0

H_B = 8
DH_B = 64
B_LEFT_CHUNKS = 8
REL_CLIP_B = 256

H_C = 4
DH_C = 64

H_D = 8
KV_D = 2
DH_D = 64
SWA_WINDOW = 128
D_LEFT_CHUNKS = SWA_WINDOW // CHUNK - 1

N_BUCKETS = 32
T5_MAX_DIST = 1024

N_BRANCH = 4
BRANCH_W = 512

N_EXPERTS = 64
TOP_K = 6
D_EXPERT = 256
D_SHARED = 256
ROUTED_SCALE = 2.5
MOE_BLOCK = 128

kernel_name = "hybrid_chunk_causal_mla_diff_swa_moe"

def _in_sizes():
    return [Q_LORA,
            KV_LORA + DA_ROPE,
            3 * H_B * DH_B,
            3 * H_C * 2 * DH_C,
            (H_D + 2 * KV_D) * DH_D,
            N_BRANCH * D_MODEL]

def rmsnorm(x, g):
    xf = x.astype(jnp.float32)
    y = xf * lax.rsqrt(jnp.mean(xf * xf, axis=-1, keepdims=True) + EPS)
    return (y * g.astype(jnp.float32)).astype(x.dtype)

def rope(t, pos):
    d = t.shape[-1]
    inv = ROPE_THETA ** (-jnp.arange(0, d, 2, dtype=jnp.float32) / d)
    ang = pos.astype(jnp.float32)[:, None] * inv[None, :]
    cos = jnp.cos(ang)[:, None, :].astype(t.dtype)
    sin = jnp.sin(ang)[:, None, :].astype(t.dtype)
    t1, t2 = t[..., :d // 2], t[..., d // 2:]
    return jnp.concatenate([t1 * cos - t2 * sin, t2 * cos + t1 * sin], axis=-1)

def t5_bucket(rel):
    half = N_BUCKETS // 2
    max_exact = half // 2
    ret = jnp.where(rel > 0, half, 0)
    n = jnp.abs(rel)
    nf = jnp.maximum(n, 1).astype(jnp.float32)
    large = max_exact + (jnp.log(nf / max_exact) / math.log(T5_MAX_DIST / max_exact)
                         * (half - max_exact)).astype(jnp.int32)
    large = jnp.minimum(large, half - 1)
    return ret + jnp.where(n < max_exact, n, large)

def chunk_causal_mask(q_pos, k_pos):
    return (k_pos[None, :] // CHUNK) <= (q_pos[:, None] // CHUNK)

def _block_queries(q):
    b, s = q.shape[:2]
    return q.reshape(b, s // Q_BLOCK, Q_BLOCK, *q.shape[2:]).swapaxes(0, 1)

def _unblock(o):
    o = o.swapaxes(0, 1)
    return o.reshape(o.shape[0], -1, *o.shape[3:])

def _chunk_band(t, n_left):
    b, s = t.shape[:2]
    nc = s // CHUNK
    tc = t.reshape(b, nc, CHUNK, *t.shape[2:])
    tp = jnp.pad(tc, ((0, 0), (n_left, 0)) + ((0, 0),) * (tc.ndim - 2))
    return jnp.concatenate([tp[:, j:j + nc] for j in range(n_left + 1)], axis=2)

def swiglu(h, w_gu, w_down):
    gu = h @ w_gu
    g, u = jnp.split(gu, 2, axis=-1)
    return (jax.nn.silu(g) * u) @ w_down

def mla_mixer(xq, xkv, q_norm_g, w_q_up, kv_norm_g, w_kv_up):
    b, s, _ = xq.shape
    pos = jnp.arange(s)
    cq = rmsnorm(xq, q_norm_g)
    q = (cq @ w_q_up).reshape(b, s, H_A, DA_NOPE + DA_ROPE)
    q = jnp.concatenate([q[..., :DA_NOPE], rope(q[..., DA_NOPE:], pos)], axis=-1) * (DA_NOPE + DA_ROPE) ** -0.5
    ckv = rmsnorm(xkv[..., :KV_LORA], kv_norm_g)
    k_rope = rope(xkv[..., None, KV_LORA:], pos)
    kv = (ckv @ w_kv_up).reshape(b, s, H_A, DA_NOPE + DA_V)
    k = jnp.concatenate([kv[..., :DA_NOPE], jnp.broadcast_to(k_rope, (b, s, H_A, DA_ROPE))], axis=-1)
    v = kv[..., DA_NOPE:]
    k_pos = jnp.arange(s)

    def body(args):
        qb, blk = args
        q_pos = blk * Q_BLOCK + jnp.arange(Q_BLOCK)
        sc = jnp.einsum('bqhd,bkhd->bhqk', qb, k).astype(jnp.float32)
        sc = jnp.where(chunk_causal_mask(q_pos, k_pos), sc, NEG)
        p = jax.nn.softmax(sc, axis=-1).astype(v.dtype)
        return jnp.einsum('bhqk,bkhd->bqhd', p, v)

    o = _unblock(lax.map(body, (_block_queries(q), jnp.arange(s // Q_BLOCK))))
    return o.reshape(b, s, H_A * DA_V)

def chunk_relbias_mixer(xb, rel_table):
    b, s, _ = xb.shape
    nc = s // CHUNK
    w = H_B * DH_B
    q = xb[..., :w].reshape(b, nc, CHUNK, H_B, DH_B) * DH_B ** -0.5
    k = _chunk_band(xb[..., w:2 * w].reshape(b, s, H_B, DH_B), B_LEFT_CHUNKS)
    v = _chunk_band(xb[..., 2 * w:].reshape(b, s, H_B, DH_B), B_LEFT_CHUNKS)
    band = (B_LEFT_CHUNKS + 1) * CHUNK
    kk = jnp.arange(band)
    valid = (jnp.arange(nc)[:, None] - B_LEFT_CHUNKS + kk[None, :] // CHUNK) >= 0
    rel = B_LEFT_CHUNKS * CHUNK + jnp.arange(CHUNK)[:, None] - kk[None, :]
    bias = rel_table[:, jnp.clip(rel, -(CHUNK - 1), REL_CLIP_B) + CHUNK - 1].astype(jnp.float32)
    sc = jnp.einsum('bnqhd,bnkhd->bhnqk', q, k).astype(jnp.float32) + bias[None, :, None]
    sc = jnp.where(valid[None, None, :, None, :], sc, NEG)
    p = jax.nn.softmax(sc, axis=-1).astype(v.dtype)
    o = jnp.einsum('bhnqk,bnkhd->bnqhd', p, v)
    return o.reshape(b, s, w)

def diff_mixer(xc, lam, subln_g, t5_c, lambda_init):
    b, s, _ = xc.shape
    qw = H_C * 2 * DH_C
    q = xc[..., :qw].reshape(b, s, H_C, 2, DH_C) * DH_C ** -0.5
    k = xc[..., qw:2 * qw].reshape(b, s, H_C, 2, DH_C)
    v = xc[..., 2 * qw:].reshape(b, s, H_C, 2 * DH_C)
    lf = lam.astype(jnp.float32)
    lam_full = jnp.exp(jnp.sum(lf[0] * lf[1])) - jnp.exp(jnp.sum(lf[2] * lf[3])) + lambda_init
    k_pos = jnp.arange(s)

    def body(args):
        qb, blk = args
        q_pos = blk * Q_BLOCK + jnp.arange(Q_BLOCK)
        bias = t5_c[t5_bucket(k_pos[None, :] - q_pos[:, None])].astype(jnp.float32).transpose(2, 0, 1)
        sc = jnp.einsum('bqhtd,bkhtd->bthqk', qb, k).astype(jnp.float32) + bias[None, None]
        sc = jnp.where(chunk_causal_mask(q_pos, k_pos), sc, NEG)
        p = jax.nn.softmax(sc, axis=-1)
        a = p[:, 0] - lam_full * p[:, 1]
        return jnp.einsum('bhqk,bkhd->bqhd', a.astype(v.dtype), v)

    o = _unblock(lax.map(body, (_block_queries(q), jnp.arange(s // Q_BLOCK))))
    o = rmsnorm(o, subln_g) * (1.0 - lambda_init)
    return o.reshape(b, s, qw)

def swa_sink_mixer(xd, sinks, t5_d):
    b, s, _ = xd.shape
    nc = s // CHUNK
    g = H_D // KV_D
    qw, kw = H_D * DH_D, KV_D * DH_D
    q = xd[..., :qw].reshape(b, nc, CHUNK, KV_D, g, DH_D) * DH_D ** -0.5
    k = _chunk_band(xd[..., qw:qw + kw].reshape(b, s, KV_D, DH_D), D_LEFT_CHUNKS)
    v = _chunk_band(xd[..., qw + kw:].reshape(b, s, KV_D, DH_D), D_LEFT_CHUNKS)
    band = (D_LEFT_CHUNKS + 1) * CHUNK
    kk = jnp.arange(band)
    valid = (jnp.arange(nc)[:, None] - D_LEFT_CHUNKS + kk[None, :] // CHUNK) >= 0
    rel = kk[None, :] - (D_LEFT_CHUNKS * CHUNK + jnp.arange(CHUNK)[:, None])
    bias = t5_d[t5_bucket(rel)].astype(jnp.float32).transpose(2, 0, 1).reshape(KV_D, g, CHUNK, band)
    sc = jnp.einsum('bnqhgd,bnkhd->bhgnqk', q, k).astype(jnp.float32) + bias[None, :, :, None]
    sc = jnp.where(valid[None, None, None, :, None, :], sc, NEG)
    sink = jnp.broadcast_to(sinks.astype(jnp.float32).reshape(KV_D, g)[None, :, :, None, None, None],
                            sc.shape[:-1] + (1,))
    p = jax.nn.softmax(jnp.concatenate([sc, sink], axis=-1), axis=-1)[..., :-1].astype(v.dtype)
    o = jnp.einsum('bhgnqk,bnkhd->bnqhgd', p, v)
    return o.reshape(b, s, qw)

def moe_routed(h2, router_w, router_bias, w_gu, w_down):
    t = h2.shape[0]
    tk = t * TOP_K
    scores = jax.nn.sigmoid((h2 @ router_w).astype(jnp.float32))
    _, idx = lax.top_k(scores + router_bias.astype(jnp.float32), TOP_K)
    gsel = jnp.take_along_axis(scores, idx, axis=1)
    gsel = gsel / jnp.sum(gsel, axis=-1, keepdims=True) * ROUTED_SCALE
    flat_e = idx.reshape(-1)
    flat_t = jnp.repeat(jnp.arange(t, dtype=jnp.int32), TOP_K)
    flat_g = gsel.reshape(-1)
    order = jnp.argsort(flat_e)
    e_s, t_s, g_s = flat_e[order], flat_t[order], flat_g[order]
    counts = jnp.zeros((N_EXPERTS,), jnp.int32).at[flat_e].add(1)
    padded = (counts + MOE_BLOCK - 1) // MOE_BLOCK * MOE_BLOCK
    pad_end = jnp.cumsum(padded)
    pad_start = pad_end - padded
    start = jnp.cumsum(counts) - counts
    dest = pad_start[e_s] + jnp.arange(tk, dtype=jnp.int32) - start[e_s]
    n_blocks = -(-(tk + N_EXPERTS * (MOE_BLOCK - 1)) // MOE_BLOCK)
    n_rows = n_blocks * MOE_BLOCK
    row_t = jnp.full((n_rows,), t, jnp.int32).at[dest].set(t_s)
    row_g = jnp.zeros((n_rows,), jnp.float32).at[dest].set(g_s)
    blk_e = jnp.minimum(jnp.searchsorted(pad_end, jnp.arange(n_blocks) * MOE_BLOCK, side='right'),
                        N_EXPERTS - 1)
    h_pad = jnp.concatenate([h2, jnp.zeros((1, h2.shape[1]), h2.dtype)], axis=0)
    xb = h_pad[row_t].reshape(n_blocks, MOE_BLOCK, h2.shape[1])

    def expert_block(args):
        xblk, e = args
        return swiglu(xblk, w_gu[e], w_down[e])

    yb = lax.map(expert_block, (xb, blk_e)).reshape(n_rows, h2.shape[1])
    yb = yb * row_g[:, None].astype(yb.dtype)
    return jnp.zeros((t + 1, h2.shape[1]), yb.dtype).at[row_t].add(yb)[:t]

def setup_inputs(seed: int = 0) -> dict:
    key = jax.random.key(seed)
    ks = jax.random.split(key, 32)
    L, D = DEPTH, D_MODEL
    f32 = jnp.float32

    def nrm(k, shape, scale):
        return jax.random.normal(k, shape, f32) * scale

    def gain(k, shape):
        return 1.0 + 0.02 * jax.random.normal(k, shape, f32)

    in_cols = sum(_in_sizes())
    return {
        "x": nrm(ks[0], (BATCH, SEQ, D), 1.0),
        "c": nrm(ks[1], (BATCH, D), 1.0),
        "ada_w": nrm(ks[2], (L, D, 6 * D), 0.5 * D ** -0.5),
        "ada_b": nrm(ks[3], (L, 6 * D), 0.02),
        "norm_mix_g": gain(ks[4], (L, D)),
        "norm_ffn_g": gain(ks[5], (L, D)),
        "w_in": nrm(ks[6], (L, D, in_cols), D ** -0.5),
        "q_norm_g": gain(ks[7], (L, Q_LORA)),
        "w_q_up": nrm(ks[8], (L, Q_LORA, H_A * (DA_NOPE + DA_ROPE)), Q_LORA ** -0.5),
        "kv_norm_g": gain(ks[9], (L, KV_LORA)),
        "w_kv_up": nrm(ks[10], (L, KV_LORA, H_A * (DA_NOPE + DA_V)), KV_LORA ** -0.5),
        "rel_bias_b": nrm(ks[11], (L, H_B, CHUNK + REL_CLIP_B), 0.2),
        "diff_lambda": nrm(ks[12], (L, 4, DH_C), 0.1),
        "diff_subln_g": gain(ks[13], (L, 2 * DH_C)),
        "sinks_d": nrm(ks[14], (L, H_D), 0.5),
        "t5_table": nrm(ks[15], (N_BUCKETS, H_C + H_D), 0.2),
        "w_branch": nrm(ks[16], (L, N_BRANCH, BRANCH_W, D), BRANCH_W ** -0.5),
        "w_out": nrm(ks[17], (L, D, D), D ** -0.5),
        "router_w": nrm(ks[18], (L, D, N_EXPERTS), D ** -0.5),
        "router_bias": nrm(ks[19], (L, N_EXPERTS), 0.01),
        "w_shared_gu": nrm(ks[20], (L, D, 2 * D_SHARED), D ** -0.5),
        "w_shared_down": nrm(ks[21], (L, D_SHARED, D), D_SHARED ** -0.5),
        "w_exp_gu": nrm(ks[22], (L, N_EXPERTS, D, 2 * D_EXPERT), D ** -0.5),
        "w_exp_down": nrm(ks[23], (L, N_EXPERTS, D_EXPERT, D), D_EXPERT ** -0.5),
        "final_norm_g": gain(ks[24], (D,)),
    }

def reference(x, c, ada_w, ada_b, norm_mix_g, norm_ffn_g, w_in, q_norm_g, w_q_up, kv_norm_g,
              w_kv_up, rel_bias_b, diff_lambda, diff_subln_g, sinks_d, t5_table, w_branch, w_out,
              router_w, router_bias, w_shared_gu, w_shared_down, w_exp_gu, w_exp_down, final_norm_g):
    b, s, d = x.shape
    splits = [int(v) for v in np.cumsum(_in_sizes())[:-1]]
    t5_c, t5_d = t5_table[:, :H_C], t5_table[:, H_C:]
    c_act = jax.nn.silu(c)
    for l in range(DEPTH):
        lambda_init = 0.8 - 0.6 * math.exp(-0.3 * l)
        mod = c_act @ ada_w[l] + ada_b[l]
        sh1, sc1, g1, sh2, sc2, g2 = [m[:, None, :] for m in jnp.split(mod, 6, axis=-1)]

        h = rmsnorm(x, norm_mix_g[l]) * (1.0 + sc1) + sh1
        proj = h @ w_in[l]
        xa_q, xa_kv, xb, xc, xd, gates = jnp.split(proj, splits, axis=-1)
        y_a = mla_mixer(xa_q, xa_kv, q_norm_g[l], w_q_up[l], kv_norm_g[l], w_kv_up[l])
        y_b = chunk_relbias_mixer(xb, rel_bias_b[l])
        y_c = diff_mixer(xc, diff_lambda[l], diff_subln_g[l], t5_c, lambda_init)
        y_d = swa_sink_mixer(xd, sinks_d[l], t5_d)
        ys = jnp.stack([y_a, y_b, y_c, y_d], axis=2)
        branch = jnp.einsum('bsnw,nwd->bsnd', ys, w_branch[l])
        gate = jax.nn.sigmoid(gates.reshape(b, s, N_BRANCH, d))
        merged = jnp.sum(gate * branch, axis=2)
        x = x + g1 * (merged @ w_out[l])

        h = rmsnorm(x, norm_ffn_g[l]) * (1.0 + sc2) + sh2
        h2 = h.reshape(b * s, d)
        y = swiglu(h2, w_shared_gu[l], w_shared_down[l]) + moe_routed(
            h2, router_w[l], router_bias[l], w_exp_gu[l], w_exp_down[l])
        x = x + g2 * y.reshape(b, s, d)
    return rmsnorm(x, final_norm_g)


_drawn_inputs = setup_inputs


def setup_inputs(seed=0):
    import zlib

    import numpy as np

    out = dict(_drawn_inputs(seed))
    spreads = {}
    factors = {'q_norm_g': 7.285, 'kv_norm_g': 3.164, 'sinks_d': 8.0, 'final_norm_g': 2.87}
    for name, (base, spread) in spreads.items():
        noise = np.random.default_rng([zlib.crc32(name.encode()), seed]).standard_normal(out[name].shape)
        drawn = base * np.exp(spread * noise) if base else spread * noise
        out[name] = __import__('jax').numpy.asarray(drawn.astype(out[name].dtype))
    for name, factor in factors.items():
        out[name] = (out[name] * factor).astype(out[name].dtype)
    return out
```

```python
import math
from contextlib import ExitStack

import numpy as np

import concourse.bass as bass
from concourse import mybir

ALU = mybir.AluOpType
ACT = mybir.ActivationFunctionType
AX = mybir.AxisListType
F32 = mybir.dt.float32
F32R = mybir.dt.float32r
I32 = mybir.dt.int32
U32 = mybir.dt.uint32

P = 128
S = 512
D = 1024
L = 2
KD = D // P
TC = S // P
EPS = 1e-6
NEG = -1e30
BIG = 3.0e38

NOPE, ROPE, HA = 64, 32, 8
DH = 64
DQ = NOPE + ROPE
Q_LORA, KV_LORA = 256, 128
NBR = 4
BW = 512
NE = 64
TOPK = 6
DE = 256
BLK = 128
NPAIR = TC * TOPK
MAXOVF = S * TOPK // BLK + 8
SKIP = 1 << 20
VLEN = 640

C_KV = Q_LORA
C_B = Q_LORA + KV_LORA + ROPE
C_C = C_B + 3 * BW
C_D = C_C + 3 * BW
C_G = C_D + BW + 256

V_ADAB, V_GMIX, V_GFFN, V_GQ, V_GKV, V_SUB, V_SINK, V_LI, V_OML, V_RB, V_LAM = (
    0, 48, 56, 64, 66, 67, 68, 100, 101, 102, 166)
NVEC = 166

K_ID, K_UP, K_UPI, K_IOTA, K_IOTAS, K_PROT, K_IOTA32 = 0, 128, 256, 320, 384, 448, 480
NCONST = 480 + 48


def weight_tiles():
    ada = lambda a: [("ada", 8 * a + i) for i in range(8)]
    cols = lambda c0, n: [("in", c0 + P * i) for i in range(n)]
    gate_branch = lambda n: [t for i in range(KD // 2) for t in
                             cols(C_G + n * D + 2 * i * P, 2) + [("branch", n, i)]]
    phases = {
        "ada0": ada(0) + ada(1),
        "projA": cols(0, 2) + cols(C_KV, 1) + [("in", C_KV + KV_LORA - NOPE)] + [("kvup",), ("qup", 0), ("qup", 1)],
        "projB": cols(C_B, 12),
        "gbA": gate_branch(0),
        "projC": cols(C_C, 12),
        "gbB": gate_branch(1),
        "projD": cols(C_D, 6) + ada(2) + ada(3) + ada(4) + ada(5),
        "gbC": gate_branch(2),
        "gbD": gate_branch(3),
        "out": [("out", m) for m in range(KD)],
        "shared": [("sgu", 0), ("sgu", 2), ("sgu", 1), ("sgu", 3), ("sdn", 0), ("sdn", 1)],
    }
    return phases


PHASES = weight_tiles()
TILES = [t for ph in PHASES.values() for t in ph]
NTILES = len(TILES)
MIX_TILES = NTILES - len(PHASES["shared"])
RAW = 3
SPLIT = 2


class Job:

    def __init__(self, kind, tiles, out, act="h", k=KD, m=P, col=0, arg=0):
        self.kind, self.tiles, self.out, self.act, self.k, self.m, self.col, self.arg = (
            kind, tiles, out, act, k, m, col, arg)


def make_jobs():
    at, first = {}, 0
    for name, ph in PHASES.items():
        at[name] = first
        first += len(ph)
    j = {}
    a = at["ada0"]
    j["ada0"] = [Job("ada", list(range(a + 8 * i, a + 8 * i + 8)), "mod", arg=i) for i in range(2)]
    a = at["projA"]
    j["projA"] = [Job("T", [a], "cq", arg=0), Job("T", [a + 1], "cq", arg=1), Job("T", [a + 2], "ckv"),
                  Job("T", [a + 3], "krope", m=DQ)]
    j["upA"] = ([Job("T", [a + 4], "kA", act="ckv", k=1, col=P * h, arg=h) for h in range(HA)]
                + [Job("VA", [a + 4], "vA", act="ckv", k=1, arg=t) for t in range(TC)]
                + [Job("T", [a + 5 + h // 4], "qA", act="cq", k=2, m=DQ, col=DQ * (h % 4), arg=h) for h in range(HA)])
    for br in "BC":
        a = at["proj" + br]
        j["proj" + br] = ([Job("T", [a + i], "q" + br, arg=i) for i in range(4)]
                          + [Job("T", [a + 4 + i], "k" + br, arg=i) for i in range(4)]
                          + [Job("V", [a + 8 + i], "v" + br, arg=i) for i in range(4)])
    a = at["projD"]
    j["projD"] = ([Job("T", [a + i], "qD", arg=i) for i in range(4)]
                  + [Job("T", [a + 4], "kD")]
                  + [Job("V", [a + 5], "vD")]
                  + [Job("ada", list(range(a + 6 + 8 * i, a + 14 + 8 * i)), "mod", arg=2 + i) for i in range(4)])
    for n, br in enumerate("ABCD"):
        a, jobs = at["gb" + br], []
        for i in range(KD // 2):
            m = n * KD + 2 * i
            jobs += [Job("T", [a + 3 * i], "gate", arg=m), Job("T", [a + 3 * i + 1], "gate", arg=m + 1)]
            jobs += [Job("T", [a + 3 * i + 2], "branch", act="o", k=4, col=P * e, arg=m + e) for e in range(2)]
        j["gb" + br] = jobs
    a = at["out"]
    j["out"] = [Job("T", [a + m], "x", act="m", arg=m) for m in range(KD)]
    a = at["shared"]
    j["shared"] = ([Job("T", [a + i], "sg" if i % 2 == 0 else "su", arg=i // 2) for i in range(4)]
                   + [Job("T", [a + 4 + i // 4], "ys", act="s", k=2, col=P * (i % 4), arg=i) for i in range(KD)])
    return j


class Map:
    def __init__(self, br, head, qb, t=0):
        self.br, self.head, self.qb, self.t = br, head, qb, t
        self.k0 = max(qb - 1, 0) * P if br == "D" else 0
        self.nk = (qb + 1) * P - self.k0


def make_maps(br):
    if br == "C":
        return [Map(br, h, qb, t) for h in range(4) for qb in range(TC) for t in range(2)]
    return [Map(br, h, qb) for h in range(8) for qb in range(TC)]


MAPS = {br: make_maps(br) for br in "ABCD"}
MAP0 = {"A": 0, "B": 32, "C": 64, "D": 96}
GROUP0 = {"A": 0, "B": 32, "C": 64, "D": 80}
NGROUP = {"A": 32, "B": 32, "C": 16, "D": 32}
PER_SET = {"A": 8, "B": 8, "C": 4, "D": 8}
SET0 = {"A": 0, "B": 4, "C": 8, "D": 12}
FILL = {"A": "projB", "B": "projC", "C": "projD", "D": "gbC"}


def map_group(u):
    if u < 64:
        return u
    return 64 + (u - 64) // 2 if u < 96 else 80 + u - 96


def group_maps(g):
    if g < 64:
        return [g]
    return [64 + 2 * (g - 64), 65 + 2 * (g - 64)] if g < 80 else [96 + g - 80]


def hybrid_trunk(nc, xT_d, wmix_d, wexp_d, vec_d, gvec_d, rw_d, vb_d, t5_d, const_d, onehot_d, rope_d, pay_d, skip_d,
                 out_d):
    ctx = ExitStack()
    with ctx:
        base = (nc.sbuf_base + 63) // 64 * 64
        end = nc.sbuf_usable_end
        ctx.enter_context(nc.sbuf_tensor("arena", [P, (end - base) // 4 - 64], F32))
        cursor = [base]

        def place(name, shape, dt=F32, at=None):
            size = int(np.prod(shape[1:])) * 4
            size = (size + 31) // 32 * 32
            off = cursor[0] if at is None else at
            assert off + size <= end, (name, off + size, end)
            if at is None:
                cursor[0] += size
            t = nc.alloc_sbuf_tensor_at(name, shape, dt, offset=off)
            t_end[name] = off + size
            return t

        t_end = {}
        xT = place("xT", [P, KD, S])
        cst = place("cst", [P, NCONST])
        vec = place("vec", [P, NVEC])
        gvec = place("gvec", [P, 16])
        cact = place("cact", [P, KD])
        ctmp = place("ctmp", [P, 2 * KD])
        mod = place("mod", [P, 48])
        amul = place("amul", [P, KD])
        ones = place("ones", [P, P])
        mhalf = place("mhalf", [P, 8])
        stat = place("stat", [P, 8])
        rstd = place("rstd", [P, 8])
        zero = place("zero", [P, 4])
        tab = [place(f"tab{i}", [P, S]) for i in range(2)]
        tabD = [place(f"tabD{i}", [P, 2 * P]) for i in range(2)]
        keep_end = cursor[0]
        h_hi = place("h_hi", [P, KD, S], F32R)
        h_lo = place("h_lo", [P, KD, S], F32R)
        raw = [place(f"raw{i}", [P, 1024]) for i in range(RAW)]
        w_hi = [place(f"w_hi{i}", [P, 1024], F32R) for i in range(SPLIT)]
        w_lo = [place(f"w_lo{i}", [P, 1024], F32R) for i in range(SPLIT)]
        both_end = cursor[0]
        sn = [place(f"sn{i}", [P, S]) for i in range(2)]
        pr = [place(f"pr{i}", [P, S]) for i in range(4)]
        pt = [place(f"pt{i}", [P, S]) for i in range(2)]
        on = place("on", [P, TC, P])
        gt = [place(f"gt{i}", [P, S]) for i in range(2)]
        gb = place("gb", [P, S])
        negmax = place("negmax", [P, P])
        psum_of = place("psum_of", [P, P])
        rcp = place("rcp", [P, 16])
        sinkt = place("sinkt", [P, 48])
        lamt = place("lamt", [P, 8])
        lamj = place("lamj", [P, 64])
        o_hi = place("o_hi", [P, 4, S], F32R)
        o_lo = place("o_lo", [P, 4, S], F32R)
        m0 = cursor[0]
        merged = place("merged", [P, KD, S])
        rope_t = place("rope_t", [P, 2, S], at=m0)
        tabA = place("tabA", [P, S], at=m0 + 4096)
        qraw = place("qraw", [P, S], at=m0 + 6144)
        qrot = place("qrot", [P, S], at=m0 + 8192)
        lamv = place("lamv", [P, 256], at=m0 + 10240)
        r0 = cursor[0]
        qA = place("qA", [P, HA, S])
        kA = place("kA", [P, HA, S])
        vA = place("vA", [P, TC, BW])
        r1 = cursor[0]
        qB = place("qB", [P, 4, S])
        kB = place("kB", [P, 4, S])
        vB = place("vB", [P, TC, BW])
        mixer_end = cursor[0]
        cqf = place("cqf", [P, 2, S], at=r1)
        ckvf = place("ckvf", [P, 1, S], at=r1 + 4096)
        cq_hi = place("cq_hi", [P, 2, S], F32R, at=r1 + 6144)
        cq_lo = place("cq_lo", [P, 2, S], F32R, at=r1 + 10240)
        ckv_hi = place("ckv_hi", [P, 1, S], F32R, at=r1 + 14336)
        ckv_lo = place("ckv_lo", [P, 1, S], F32R, at=r1 + 16384)
        qC = place("qC", [P, 4, S], at=r0)
        kC = place("kC", [P, 4, S], at=r0 + 8192)
        vC = place("vC", [P, TC, BW], at=r0 + 16384)
        o2_hi = place("o2_hi", [P, 4, S], F32R, at=r0 + 24576)
        o2_lo = place("o2_lo", [P, 4, S], F32R, at=r0 + 32768)
        qD = place("qD", [P, 4, S], at=r1)
        kD = place("kD", [P, 2, S], at=r1 + 8192)
        vD = place("vD", [P, TC, P], at=r1 + 12288)
        cursor[0] = both_end
        hf = place("hf", [P, KD, S])
        s_hi = place("s_hi", [P, 2, S], F32R)
        s_lo = place("s_lo", [P, 2, S], F32R)
        sgt = place("sgt", [P, S])
        htok = [place(f"htok{i}", [P, D]) for i in range(2)]
        shared_end = cursor[0]
        rw = place("rw", [P, KD, NE])
        score = place("score", [P, TC, NE])
        biased = place("biased", [P, TC, NE])
        top = place("top", [P, TC, 8])
        topi = place("topi", [P, TC, 8], U32)
        topf = place("topf", [P, TC, 8])
        sel = place("sel", [P, TC, NE])
        posn = place("posn", [P, TC, NE])
        gsel = place("gsel", [P, TC, TOPK])
        gsum = place("gsum", [P, 8])
        dest = place("dest", [P, NPAIR], U32)
        destf = place("destf", [P, NPAIR])
        pay = place("pay", [P, NPAIR, 4], I32)
        cnt = place("cnt", [P, 8])
        cmpt = place("cmpt", [P, 48])
        ovf = place("ovf", [P, 2, 48], I32)
        ovff = place("ovff", [P, 3, 48])
        novf = place("novf", [P, 8], I32)
        slots = place("slots", [P, NE, 4], I32)
        idx = [place(f"idx{i}", [P, 4], I32) for i in range(8)]
        ew = [place(f"ew{i}", [P, 6144]) for i in range(3)]
        assert cursor[0] <= end, (cursor[0], end)
        onehot = place("onehot", [P, NPAIR, NE], at=t_end["ew1"])
        ohmul = place("ohmul", [P, NPAIR, NE], at=t_end["ew1"] + 4 * NPAIR * NE)
        cursor[0] = keep_end
        ew.append(place("ew3", [P, 6144]))
        xg = [place(f"xg{i}", [P, D]) for i in range(4)]
        xgT = [place(f"xgT{i}", [P, KD, BLK]) for i in range(2)]
        sil = [place(f"sil{i}", [P, 2, BLK]) for i in range(2)]
        actT = [place(f"actT{i}", [P, 2, BLK]) for i in range(2)]
        y = [place(f"y{i}", [P, D]) for i in range(4)]
        assert cursor[0] <= shared_end
        yt = [place(f"yt{i}", [P, TOPK, D], at=keep_end + 24576 * i) for i in range(2)]

        PB = [ctx.enter_context(nc.psum_tensor(f"bank{i}", [P, S], F32)) for i in range(8)]
        G, SB, TB, OB, MB = PB[0:2], PB[2:4], PB[4:6], PB[6], PB[7]

        v_d = nc.dram_tensor("v_d", [12, P, VLEN], F32, kind="Internal").ap()
        h2_d = nc.dram_tensor("h2_d", [S, D], F32, kind="Internal").ap()
        slot_d = nc.dram_tensor("slot_d", [NE * S, 4], I32, kind="Internal").ap()
        y_d = nc.dram_tensor("y_d", [S * TOPK, D], F32, kind="Internal").ap()

        sems = {}

        def sem(name):
            sems[name] = ctx.enter_context(nc.semaphore(name))
            return sems[name]

        tile_in = [sem(f"tile_in{i}") for i in range(RAW)]
        hi_done = sem("hi_done")
        lo_done = sem("lo_done")
        mark = sem("mark")
        chunk_out = [sem(f"chunk_out{i}") for i in range(2)]
        m_full, m_free = sem("m_full"), sem("m_free")
        sq_ready, sq_used = sem("sq_ready"), sem("sq_used")
        ms_ready = sem("ms_ready")
        rstd_ready = sem("rstd_ready")
        nt_ready, nhi_ready, nlo_ready = sem("nt_ready"), sem("nhi_ready"), sem("nlo_ready")
        dchain = sem("dchain")
        achain = sem("achain")
        pchain = sem("pchain")
        vecs_in, rope_in = sem("vecs_in"), sem("rope_in")
        tabA_ready = sem("tabA_ready")
        amul_ready = sem("amul_ready")
        kr_ready, kr_copied = sem("kr_ready"), sem("kr_copied")
        rot_ready = sem("rot_ready")
        tab_in = [sem(f"tab_in{i}") for i in range(2)]
        tabD_in = [sem(f"tabD_in{i}") for i in range(2)]
        sc_ready = sem("sc_ready")
        sn_ready = sem("sn_ready")
        p_ready = sem("p_ready")
        comb_ready = sem("comb_ready")
        tr_ready = sem("tr_ready")
        pt_copied = [sem(f"pt_copied{i}") for i in range(2)]
        pv_done = sem("pv_done")
        es_in, es_ready = sem("es_in"), sem("es_ready")
        ss_ready = sem("ss_ready")
        ms2_ready, rs2_ready = sem("ms2_ready"), sem("rs2_ready")
        on_ready = sem("on_ready")
        ohi_ready, olo_ready = sem("ohi_ready"), sem("olo_ready")
        merged_to = sem("merged_to")
        lam_ready, lame = sem("lam_ready"), sem("lame")
        mhi_ready, mlo_ready = sem("mhi_ready"), sem("mlo_ready")
        rw_in, h2_out = sem("rw_in"), [sem("h2_out0"), sem("h2_out1")]
        logits_ready, score_ready = sem("logits_ready"), sem("score_ready")
        sel_ready, rank_ready, dest_ready = sem("sel_ready"), sem("rank_ready"), sem("dest_ready")
        htr_ready, htr_copied = sem("htr_ready"), [sem(f"htr_copied{i}") for i in range(2)]
        sil_ready, sprod_ready, shi_ready = sem("sil_ready"), sem("sprod_ready"), sem("shi_ready")
        slo_ready = sem("slo_ready")
        slot_init, slot_out, slots_in = sem("slot_init"), sem("slot_out"), [sem(f"slots_in{i}") for i in range(4)]
        cnt_ready, cnt_read = sem("cnt_ready"), sem("cnt_read")
        settled = sem("settled")
        ew_in = [sem(f"ew_in{i}") for i in range(4)]
        xg_in = [sem(f"xg_in{i}") for i in range(4)]
        y_out = [sem(f"y_out{i}") for i in range(4)]
        xt_ready = sem("xt_ready")
        xt_copA, xt_copD = sem("xt_copA"), sem("xt_copD")
        gu_ready = sem("gu_ready")
        silu_done, act_done = sem("silu_done"), sem("act_done")
        dn_ready = sem("dn_ready")
        yA, yD = sem("yA"), sem("yD")
        o_load, o_turn, o_gat, o_put = sem("o_load"), sem("o_turn"), sem("o_gat"), sem("o_put")
        o_xt, o_xcA, o_xcD, o_gu, o_sil, o_act, o_dn, o_yA, o_yD = (
            sem("o_xt"), sem("o_xcA"), sem("o_xcD"), sem("o_gu"), sem("o_sil"), sem("o_act"), sem("o_dn"),
            sem("o_yA"), sem("o_yD"))
        yt_in = [sem("yt_in0"), sem("yt_in1")]
        ysum, ytr, yadd = sem("ysum"), sem("ytr"), [sem("yadd0"), sem("yadd1")]
        per_layer = range(min(s.num for s in sems.values()), max(s.num for s in sems.values()) + 1)
        assert len(per_layer) == len(sems)
        init_in, init_v, init_a, init_m, init_out = (ctx.enter_context(nc.semaphore(n)) for n in
                                                     ("init_in", "init_v", "init_a", "init_m", "init_out"))

        ident = cst[:, K_ID:K_ID + P]
        prot = cst[NOPE:DQ, K_PROT:K_PROT + ROPE]
        R = slice(NOPE, DQ)

        with nc.Block() as block:
            @block.sync
            def _(sp):
                sp.dma_start(xT[:], xT_d).then_inc(init_in, 16)
                sp.dma_start(cst[:], const_d).then_inc(init_in, 16)
                sp.dma_start(gvec[:], gvec_d).then_inc(init_in, 16)
                sp.dma_start(gt[0][0:32, 0:12], t5_d).then_inc(init_in, 16)
                sp.dma_start(merged[0:32, 0:2, :].rearrange("p a b -> p (a b)")[:, 0:VLEN],
                             onehot_d).then_inc(init_in, 16)
                sp.wait_ge(init_v, 4)
                v = vB[0:12, 1:3, :].rearrange("p a b -> p (a b)")[:, 0:VLEN]
                sp.dma_start(v_d, v.unsqueeze(1).broadcast_to([12, P, VLEN])).then_inc(init_out, 16)

            @block.gpsimd
            def _(pool):
                nc.gpsimd.memset(ones[:], 1.0)
                nc.gpsimd.memset(mhalf[:], -0.5)
                nc.gpsimd.memset(zero[:], 0.0)
                for t in tab + tabD:
                    nc.gpsimd.memset(t[:], NEG)

            @block.scalar
            def _(act):
                act.wait_ge(init_in, 80)
                nc.scalar.activation(ctmp[:, 0:KD], gvec[:, 0:KD], ACT.Exp, scale=-1.0).then_inc(init_a, 1)

            @block.vector
            def _(dve):
                dve.wait_ge(init_a, 1)
                nc.vector.tensor_scalar_add(ctmp[:, 0:KD], ctmp[:, 0:KD], 1.0).then_inc(init_v, 1)
                dve.wait_ge(init_v, 1)
                nc.vector.reciprocal(ctmp[:, KD:2 * KD], ctmp[:, 0:KD]).then_inc(init_v, 1)
                dve.wait_ge(init_v, 2)
                nc.vector.tensor_tensor(cact[:], gvec[:, 0:KD], ctmp[:, KD:2 * KD], ALU.mult)
                dve.wait_ge(init_m, 1)
                v = vB[0:12, 1:3, :].rearrange("p a b -> p (a b)")
                nc.vector.tensor_copy(v[:, 0:S], G[0][0:12, :]).then_inc(init_v, 1)
                nc.vector.tensor_copy(v[:, S:VLEN], G[1][0:12, 0:VLEN - S]).then_inc(init_v, 1)

            @block.tensor
            def _(pe):
                pe.wait_ge(init_in, 80)
                oh = merged[0:32, 0:2, :].rearrange("p a b -> p (a b)")
                nc.tensor.matmul(G[0][0:12, :], gt[0][0:32, 0:12], oh[:, 0:S], start=True, stop=True)
                nc.tensor.matmul(G[1][0:12, 0:VLEN - S], gt[0][0:32, 0:12], oh[:, S:VLEN], start=True,
                                 stop=True).then_inc(init_m, 1)
        nc.all_engine_barrier()

        jobs = make_jobs()
        order = ["ada0", "projA", "upA", "projB", "gbA", "projC", "gbB", "projD", "gbC", "gbD", "out"]
        mix_jobs = [j for ph in order for j in jobs[ph]]
        all_jobs = mix_jobs + jobs["shared"]
        split_no, n = {}, 0
        for u, t in enumerate(TILES):
            if t[0] != "ada":
                split_no[u] = n
                n += 1
        last_use = {}
        for c, j in enumerate(all_jobs):
            j.c = c
            for u in j.tiles:
                last_use[u] = c
        tile_mark, chunk_mark, n = {}, {}, 0
        for c, j in enumerate(all_jobs):
            for u in j.tiles:
                if last_use[u] == c and u != j.tiles[-1]:
                    n += 1
                    tile_mark[u] = n
            n += 1
            chunk_mark[c] = n
            if last_use[j.tiles[-1]] == c:
                tile_mark[j.tiles[-1]] = n
        mix_marks = chunk_mark[len(mix_jobs) - 1]
        first_of_out = {}
        for j in all_jobs:
            first_of_out.setdefault((j.out, j.arg), j.c)

        def wait_chunk_out(eng, c):
            eng.wait_ge(chunk_out[c % 2], c // 2 + 1)

        def wait_out_of(eng, name, arg=0):
            wait_chunk_out(eng, first_of_out[(name, arg)])

        def wait_tile_used(eng, u):
            eng.wait_ge(mark, tile_mark[u])

        m_use = {}
        for key in ([("st", n) for n in ("x",)] + [("rb", "x"), ("st", "cq"), ("rb", "cq"), ("st", "ckv"), ("rb", "ckv"), ("kr", 0)]
                    + [("qr", h) for h in range(HA)] + [("ot", o) for o in range(16)] + [("st", "x2"), ("rb", "x2")]):
            m_use[key] = len(m_use)

        m_keys = list(m_use)
        m_full_no = {key: i for i, key in enumerate(k for k in m_keys if k[0] != "st")}

        def wait_mb_free(eng, key):
            if not m_use[key]:
                return
            kind, n = m_keys[m_use[key] - 1]
            if kind == "rb":
                eng.wait_ge(nt_ready, norm_k0[n] + norm_k[n])
            elif kind == "ot":
                eng.wait_ge(olo_ready, n + 1)
            elif kind == "kr":
                eng.wait_ge(m_free, 1)
            elif kind == "qr":
                eng.wait_ge(m_free, n + 2)

        def wait_mb_full(eng, key):
            eng.wait_ge(m_full, m_full_no[key] + 1)

        norm_no = {"x": 0, "cq": 1, "ckv": 2, "x2": 3}
        norm_k = {"x": KD, "cq": 2, "ckv": 1, "x2": KD}
        norm_k0 = {"x": 0, "cq": KD, "ckv": KD + 2, "x2": KD + 3}

        def load_tile(sp, l, u):
            if u >= RAW:
                v = u - RAW
                if v in split_no:
                    sp.wait_ge(hi_done, split_no[v] + 1)
                    sp.wait_ge(lo_done, split_no[v] + 1)
                else:
                    wait_tile_used(sp, v)
            sp.dma_start(raw[u % RAW][:], wmix_d[l * NTILES + u]).then_inc(tile_in[u % RAW], 16)

        def wait_tile_in(eng, u):
            eng.wait_ge(tile_in[u % RAW], 16 * (u // RAW + 1))

        def split_hi(act, u):
            if u not in split_no:
                return
            q = split_no[u]
            wait_tile_in(act, u)
            if q >= SPLIT:
                wait_tile_used(act, [v for v in split_no if split_no[v] == q - SPLIT][0])
            nc.scalar.activation(w_hi[q % SPLIT][:], raw[u % RAW][:], ACT.Copy).then_inc(hi_done, 1)

        def split_lo(dve, u):
            if u not in split_no:
                return
            q = split_no[u]
            dve.wait_ge(hi_done, q + 1)
            nc.vector.tensor_tensor(w_lo[q % SPLIT][:], raw[u % RAW][:], w_hi[q % SPLIT][:].bitcast(F32),
                                    ALU.subtract).then_inc(lo_done, 1)

        acts = {"h": (h_hi, h_lo), "cq": (cq_hi, cq_lo), "ckv": (ckv_hi, ckv_lo), "m": (h_hi, h_lo),
                "s": (s_hi, s_lo), "o": (o_hi, o_lo), "o2": (o2_hi, o2_lo)}

        made = {}

        def products(j):
            if j.c not in made:
                made[j.c] = make_products(j)
            return made[j.c]

        def make_products(j):
            act = "o2" if j.act == "o" and j.arg // KD == 3 else j.act
            bank = G[j.c % 2]
            out = []
            if j.kind == "ada":
                for i, u in enumerate(j.tiles):
                    w = raw[u % RAW][:].rearrange("p (k c) -> p k c", k=KD)
                    out += [(u, k, w[:, k, :], cact[:, k:k + 1], bank[:, i:i + 1], k == 0, k == KD - 1) for k in range(KD)]
                return out
            u = j.tiles[0]
            q = split_no[u] % SPLIT
            wide = {KD: P, 4: 2 * P, 2: 384 if j.act == "cq" else S, 1: 1024}[j.k]
            W = [w[q][:, 0:j.k * wide].rearrange("p (k c) -> p k c", k=j.k) for w in (w_hi, w_lo)]
            A = acts[act]
            parts = ((0, 0), (0, 1), (1, 0))
            last = (j.k - 1, 2)
            if j.kind == "T":
                for k in range(j.k):
                    for i, (w, a) in enumerate(parts):
                        lhs = W[w][:, k, j.col:j.col + j.m]
                        out.append((u, k, lhs, A[a][:, k, :], bank[0:j.m, :], (k, i) == (0, 0), (k, i) == last))
            elif j.kind == "V":
                for t in range(TC):
                    for k in range(j.k):
                        for i, (w, a) in enumerate(parts):
                            out.append((u, k, A[a][:, k, t * P:(t + 1) * P], W[w][:, k, :], bank[:, t * P:(t + 1) * P],
                                        (k, i) == (0, 0), (k, i) == last))
            elif j.kind == "VA":
                for i, (w, a) in enumerate(parts):
                    wv = W[w][:, 0, :].rearrange("p (h c) -> p h c", h=HA)[:, :, NOPE:]
                    out.append((u, 0, A[a][:, 0, j.arg * P:(j.arg + 1) * P], wv, bank[:].rearrange("p (h c) -> p h c", h=HA),
                                i == 0, i == 2))
            return out

        def pe_products(pe, j, i0, i1):
            todo = products(j)
            for i in range(i0, min(i1, len(todo))):
                u, k, lhs, rhs, out, start, stop = todo[i]
                if i == 0:
                    if j.c >= 2:
                        wait_chunk_out(pe, j.c - 2)
                    if j.act == "cq" or j.act == "ckv":
                        pe.wait_ge(nlo_ready, norm_k0[j.act] + norm_k[j.act])
                    if j.act == "o":
                        pe.wait_ge(olo_ready, 4 * (j.arg // KD) + 4)
                    if j.act == "s":
                        pe.wait_ge(slo_ready, 2)
                if j.act == "h" and j.kind != "ada" and (j.out in ("cq", "sg")) and i % 3 == 0:
                    pe.wait_ge(nlo_ready, norm_k0["x2" if j.out == "sg" else "x"] + k + 1)
                if j.act == "m" and j.arg == 0 and i % 3 == 0:
                    pe.wait_ge(mlo_ready, k + 1)
                if i == 0 or todo[i - 1][0] != u:
                    if j.kind == "ada":
                        wait_tile_in(pe, u)
                    else:
                        pe.wait_ge(lo_done, split_no[u] + 1)
                ins = nc.tensor.matmul(out, lhs, rhs, start=start, stop=stop)
                if i == len(todo) - 1 or (todo[i + 1][0] != u and last_use[u] == j.c):
                    ins.then_inc(mark, 1)

        def n_products(j):
            return len(products(j))

        def wait_chunk_full(eng, c):
            eng.wait_ge(mark, chunk_mark[c])

        def act_out(act, j):
            b = G[j.c % 2]
            done = chunk_out[j.c % 2]
            if j.out not in ("cq", "ckv", "kA", "qA", "qB", "kB", "qC", "kC", "qD", "kD", "gate", "sg"):
                return
            if j.out == "gate" and j.arg >= 2:
                wait_out_of(act, "branch", j.arg - 2)
            wait_chunk_full(act, j.c)
            if j.out == "cq":
                nc.scalar.activation(cqf[:, j.arg, :], b[:], ACT.Copy).then_inc(done, 1)
            elif j.out == "ckv":
                nc.scalar.activation(ckvf[:, 0, :], b[:], ACT.Copy).then_inc(done, 1)
            elif j.out == "kA":
                nc.scalar.activation(kA[0:NOPE, j.arg, :], b[0:NOPE, :], ACT.Copy).then_inc(done, 1)
            elif j.out == "qA":
                nc.scalar.activation(qA[0:DQ, j.arg, :], b[0:DQ, :], ACT.Copy, scale=float(DQ) ** -0.5).then_inc(done, 1)
            elif j.out in ("qB", "qC", "qD"):
                q = {"qB": qB, "qC": qC, "qD": qD}[j.out]
                nc.scalar.activation(q[:, j.arg, :], b[:], ACT.Copy, scale=0.125).then_inc(done, 1)
            elif j.out == "kD":
                for head in range(2):
                    for half in range(2):
                        ins = nc.scalar.activation(kD[64 * half:64 * half + 64, head, :],
                                                   b[64 * head:64 * head + 64, :], ACT.Copy)
                ins.then_inc(done, 1)
            elif j.out in ("kB", "kC"):
                k = {"kB": kB, "kC": kC}[j.out]
                nc.scalar.activation(k[:, j.arg, :], b[:], ACT.Copy).then_inc(done, 1)
            elif j.out == "gate":
                nc.scalar.activation(gt[j.arg % 2][:], b[:], ACT.Tanh, scale=0.5).then_inc(done, 1)
            elif j.out == "sg":
                if j.arg:
                    act.wait_ge(slo_ready, j.arg)
                nc.scalar.activation(sgt[:], b[:], ACT.Silu).then_inc(done, 1)

        chain = [0]

        def link(dve, ins):
            chain[0] += 1
            ins.then_inc(dchain, 1)
            dve.wait_ge(dchain, chain[0])

        def dve_out(dve, j):
            b = G[j.c % 2]
            done = chunk_out[j.c % 2]
            if j.out not in ("mod", "krope", "vA", "vB", "vC", "vD", "branch", "x", "su", "ys"):
                return
            wait_chunk_full(dve, j.c)
            if j.out == "mod":
                a = j.arg * 8
                nc.vector.tensor_tensor(mod[:, a:a + 8], b[:, 0:8], vec[:, V_ADAB + a:V_ADAB + a + 8],
                                        ALU.add).then_inc(done, 1)
            elif j.out == "krope":
                nc.vector.tensor_copy(qraw[R, :], b[R, :]).then_inc(done, 1)
            elif j.out == "vA":
                nc.vector.tensor_copy(vA[:, j.arg, :], b[:]).then_inc(done, 1)
            elif j.out in ("vB", "vC"):
                v = {"vB": vB, "vC": vC}[j.out]
                nc.vector.tensor_copy(v[:, :, j.arg * P:(j.arg + 1) * P],
                                      b[:].rearrange("p (t c) -> p t c", t=TC)).then_inc(done, 1)
            elif j.out == "vD":
                nc.vector.tensor_copy(vD[:], b[:].rearrange("p (t c) -> p t c", t=TC)).then_inc(done, 1)
            elif j.out == "branch":
                m = j.arg % KD
                wait_out_of(dve, "gate", j.arg)
                dst = merged[:, m, :] if j.arg < KD else gb[:]
                nc.vector.scalar_tensor_tensor(dst, gt[j.arg % 2][:], 1.0, b[:], ALU.add, ALU.mult).then_inc(done, 1)
                if j.arg >= KD:
                    wait_chunk_out(dve, j.c)
                    nc.vector.tensor_tensor(merged[:, m, :], merged[:, m, :], gb[:], ALU.add).then_inc(merged_to, 1)
                    dve.wait_ge(merged_to, j.arg - KD + 1)
            elif j.out == "x":
                nc.vector.scalar_tensor_tensor(xT[:, j.arg, :], b[:], mod[:, 16 + j.arg:17 + j.arg], xT[:, j.arg, :],
                                               ALU.mult, ALU.add).then_inc(done, 1)
            elif j.out == "su":
                wait_out_of(dve, "sg", j.arg)
                nc.vector.tensor_tensor(sgt[:], sgt[:], b[:], ALU.mult).then_inc(done, 1)
                wait_chunk_out(dve, j.c)
                dve.wait_ge(shi_ready, j.arg + 1)
                nc.vector.tensor_tensor(s_lo[:, j.arg, :], sgt[:], s_hi[:, j.arg, :].bitcast(F32),
                                        ALU.subtract).then_inc(slo_ready, 1)
            elif j.out == "ys":
                nc.vector.scalar_tensor_tensor(xT[:, j.arg, :], b[:], mod[:, 40 + j.arg:41 + j.arg], xT[:, j.arg, :],
                                               ALU.mult, ALU.add).then_inc(done, 1)

        def act_stream(act, events, end=MIX_TILES):
            for what, v in events:
                if what == "tile":
                    split_hi(act, v + 1) if v + 1 < end else None
                else:
                    j = all_jobs[v]
                    act_out(act, j)
                    if j.out == "su":
                        wait_chunk_out(act, j.c)
                        nc.scalar.activation(s_hi[:, j.arg, :], sgt[:], ACT.Copy).then_inc(shi_ready, 1)

        def dve_stream(dve, events, end=MIX_TILES):
            for what, v in events:
                if what == "tile":
                    split_lo(dve, v + 1) if v + 1 < end else None
                else:
                    dve_out(dve, all_jobs[v])

        def spread(js, nslots):
            total = sum(n_products(j) * (0.5 if j.kind == "ada" else 1) for j in js)
            shares, at = [[] for _ in range(nslots)], 0.0
            for j in js:
                n = n_products(j)
                w = 0.5 if j.kind == "ada" else 1
                i = 0
                while i < n:
                    s = min(int(at * nslots / total + 1e-9), nslots - 1)
                    room = max(1, int(math.ceil(((s + 1) * total / nslots - at) / w - 1e-9))) if s < nslots - 1 else n
                    i1 = min(n, i + room)
                    shares[s].append((j, i, i1))
                    at += (i1 - i) * w
                    i = i1
            return shares

        def events_of(share):
            ev = []
            for j, i0, i1 in share:
                todo = products(j)
                for i in range(i0, i1):
                    u = todo[i][0]
                    if (i == 0 or todo[i - 1][0] != u) and all_jobs_first[u] == (j.c, i):
                        ev.append(("tile", u))
                    if i == len(todo) - 1:
                        ev.append(("chunk", j.c))
            return ev

        all_jobs_first = {}
        for j in all_jobs:
            for i, t in enumerate(products(j)):
                all_jobs_first.setdefault(t[0], (j.c, i))

        def whole(js):
            return [(j, 0, n_products(j)) for j in js]

        sq_bufs = {"x": sn, "cq": sn, "ckv": sn, "x2": htok, "end": sn}

        def square_buf(name, n):
            return sq_bufs[name][n % 2][:, 0:S]

        def act_norm_squares(act, name, src, ready=None):
            for k in range(norm_k[name]):
                if ready:
                    ready(act, k)
                n = norm_k0[name] + k
                if n >= 2:
                    act.wait_ge(sq_used, n - 1)
                nc.scalar.activation(square_buf(name, n), src[:, k, :], ACT.Square).then_inc(sq_ready, 1)

        def pe_norm_sums(pe, name):
            wait_mb_free(pe, ("st", name))
            K = norm_k[name]
            for k in range(K):
                n = norm_k0[name] + k
                pe.wait_ge(sq_ready, n + 1)
                for t in range(TC):
                    ins = nc.tensor.matmul(MB[:, t:t + 1], square_buf(name, n)[:, t * P:(t + 1) * P], ones[:, 0:1],
                                           start=(k == 0 and t == 0), stop=(k == K - 1), skip_group_check=True)
                ins.then_inc(sq_used, 1)

        def dve_norm_mean(dve, name):
            dve.wait_ge(sq_used, norm_k0[name] + norm_k[name])
            nc.vector.tensor_scalar(stat[:, 0:TC], MB[:, 0:TC], 1.0 / (norm_k[name] * P), EPS, ALU.mult,
                                    ALU.add).then_inc(ms_ready, 1)

        def pool_norm_root(pool, name):
            pool.wait_ge(ms_ready, norm_no[name] + 1)
            nc.gpsimd.tensor_tensor(rstd[:, 0:TC], stat[:, 0:TC], mhalf[:, 0:TC], ALU.pow).then_inc(rstd_ready, 1)

        def pe_norm_spread(pe, name):
            pe.wait_ge(rstd_ready, norm_no[name] + 1)
            for t in range(TC):
                ins = nc.tensor.matmul(MB[:, t * P:(t + 1) * P], rstd[:, t:t + 1].broadcast_to([P, P]), ident,
                                       start=True, stop=True)
            ins.then_inc(m_full, 1)

        def dve_norm_apply(dve, name, src, mul, add, hi, lo, tmp):
            K = norm_k[name]
            wait_mb_full(dve, ("rb", name))
            for k in range(K + 1):
                if k < K:
                    n = norm_k0[name] + k
                    if n >= 2 and len(tmp) == 2:
                        dve.wait_ge(nlo_ready, n - 1)
                    nc.vector.scalar_tensor_tensor(tmp[k % len(tmp)], src[:, k, :], mul[:, k:k + 1], MB[:], ALU.mult,
                                                   ALU.mult).then_inc(nt_ready, 1)
                if k >= 1:
                    n = norm_k0[name] + k
                    dve.wait_ge(nhi_ready, n)
                    t, h = tmp[(k - 1) % len(tmp)], hi[:, k - 1, :].bitcast(F32)
                    if add is None or len(tmp) > 2:
                        nc.vector.tensor_tensor(lo[:, k - 1, :], t, h, ALU.subtract).then_inc(nlo_ready, 1)
                    else:
                        nc.vector.scalar_tensor_tensor(lo[:, k - 1, :], t, add[:, k - 1:k], h, ALU.add,
                                                       ALU.subtract).then_inc(nlo_ready, 1)

        def act_norm_apply(act, name, add, hi, tmp):
            for k in range(norm_k[name]):
                n = norm_k0[name] + k
                act.wait_ge(nt_ready, n + 1)
                t = tmp[k % len(tmp)]
                if add is None:
                    nc.scalar.activation(hi[:, k, :], t, ACT.Copy).then_inc(nhi_ready, 1)
                elif len(tmp) == 2:
                    nc.scalar.activation(hi[:, k, :], t, ACT.Identity, bias=add[:, k:k + 1]).then_inc(nhi_ready, 1)
                else:
                    nc.scalar.activation(t, t, ACT.Identity, bias=add[:, k:k + 1]).then_inc(achain, 1)
                    act.wait_ge(achain, k + 1)
                    nc.scalar.activation(hi[:, k, :], t, ACT.Copy).then_inc(nhi_ready, 1)

        Q = {"A": qA, "B": qB, "C": qC, "D": qD}
        K_ = {"A": kA, "B": kB, "C": kC, "D": kD}
        V_ = {"A": vA, "B": vB, "C": vC, "D": vD}

        def score_operands(mp):
            q0 = mp.qb * P
            if mp.br == "A":
                rows, qc, kc = slice(0, DQ), mp.head, mp.head
            elif mp.br == "C":
                rows, qc, kc = slice(64 * mp.t, 64 * mp.t + 64), mp.head, mp.head
            else:
                rows, qc = slice(64 * (mp.head % 2), 64 * (mp.head % 2) + 64), mp.head // 2
                kc = mp.head // 4 if mp.br == "D" else qc
            return Q[mp.br][rows, qc, q0:q0 + P], K_[mp.br][rows, kc, mp.k0:mp.k0 + mp.nk]

        def pe_scores(pe, br, u):
            mp = MAPS[br][u - MAP0[br]]
            if u == MAP0[br]:
                last = {"A": ("qA", HA - 1), "B": ("vB", 3), "C": ("vC", 3), "D": ("vD", 0)}[br]
                c = first_of_out[last]
                wait_chunk_out(pe, c)
                wait_chunk_out(pe, c - 1)
                if br == "A":
                    pe.wait_ge(kr_copied, 1)
                    pe.wait_ge(kr_ready, 1)
            if br == "A" and mp.qb == 0:
                pe.wait_ge(rot_ready, mp.head + 1)
            if u >= 2:
                pe.wait_ge(sn_ready, u - 1)
            q, k = score_operands(mp)
            nc.tensor.matmul(SB[u % 2][:, 0:mp.nk], q, k, start=True, stop=True).then_inc(sc_ready, 1)

        def dve_bias(dve, br, u):
            mp = MAPS[br][u - MAP0[br]]
            if mp.qb == 0 and mp.t == 0:
                if br in "BC":
                    th = mp.head + (8 if br == "C" else 0)
                    dve.wait_ge(tab_in[th % 2], 32 * (th // 2 + 1))
                elif br == "D":
                    dve.wait_ge(tabD_in[mp.head % 2], 32 * (mp.head // 2 + 1))
            bias = {"A": tabA[:, S - mp.nk:], "B": tab[mp.head % 2][:, S - mp.nk:], "C": tab[mp.head % 2][:, S - mp.nk:],
                    "D": tabD[mp.head % 2][:, 2 * P - mp.nk:]}[br]
            floor = sinkt[:, u - MAP0[br]:u - MAP0[br] + 1] if br == "D" else BIG
            dve.wait_ge(sc_ready, u + 1)
            if u >= 2:
                dve.wait_ge(p_ready, u - 1)
            nc.vector.tensor_tensor_reduce(out=sn[u % 2][:, 0:mp.nk], in0=SB[u % 2][:, 0:mp.nk], in1=bias, scale=-1.0,
                                           scalar=floor, op0=ALU.add, op1=ALU.min,
                                           accum_out=negmax[:, u:u + 1]).then_inc(sn_ready, 1)

        def act_exp(act, br, u):
            mp = MAPS[br][u - MAP0[br]]
            act.wait_ge(sn_ready, u + 1)
            if u >= 4:
                act.wait_ge(tr_ready, map_group(u - 4) + 1)
            nc.scalar.activation(pr[u % 4][:, 0:mp.nk], sn[u % 2][:, 0:mp.nk], ACT.Exp, bias=negmax[:, u:u + 1],
                                 scale=-1.0, accum_out=psum_of[:, u:u + 1]).then_inc(p_ready, 1)

        def dve_combine(dve, g):
            u0, u1 = group_maps(g)
            nk = MAPS["C"][u0 - MAP0["C"]].nk
            dve.wait_ge(p_ready, u1 + 1)
            if g > GROUP0["C"]:
                dve.wait_ge(comb_ready, g - GROUP0["C"])
            link(dve, nc.vector.reciprocal(rcp[:, 8:10], psum_of[:, u0:u1 + 1]))
            link(dve, nc.vector.tensor_tensor(rcp[:, 10:11], rcp[:, 9:10], lamt[:, 5:6], ALU.mult))
            link(dve, nc.vector.tensor_scalar(pr[u1 % 4][:, 0:nk], pr[u1 % 4][:, 0:nk], rcp[:, 10:11], None, ALU.mult))
            nc.vector.scalar_tensor_tensor(pr[u0 % 4][:, 0:nk], pr[u0 % 4][:, 0:nk], rcp[:, 8:9], pr[u1 % 4][:, 0:nk],
                                           ALU.mult, ALU.add).then_inc(comb_ready, 1)

        def pe_transpose_probs(pe, br, g):
            u = group_maps(g)[0]
            mp = MAPS[br][u - MAP0[br]]
            if br == "C":
                pe.wait_ge(comb_ready, g - GROUP0["C"] + 1)
            else:
                pe.wait_ge(p_ready, u + 1)
            if g >= 2:
                pe.wait_ge(pt_copied[g % 2], g // 2)
            for b in range(mp.nk // P):
                ins = nc.tensor.transpose(TB[g % 2][:, b * P:(b + 1) * P], pr[u % 4][:, b * P:(b + 1) * P], ident)
            ins.then_inc(tr_ready, 1)

        def copy_probs(eng, g):
            u = group_maps(g)[0]
            br = "A" if g < 32 else "B" if g < 64 else "C" if g < 80 else "D"
            nk = MAPS[br][u - MAP0[br]].nk
            eng.wait_ge(tr_ready, g + 1)
            if g >= 2:
                eng.wait_ge(pv_done, g - 1)
            if g % 2 == 0:
                nc.scalar.activation(pt[0][:, 0:nk], TB[0][:, 0:nk], ACT.Copy).then_inc(pt_copied[0], 1)
            else:
                nc.vector.tensor_copy(pt[1][:, 0:nk], TB[1][:, 0:nk]).then_inc(pt_copied[1], 1)

        def pe_values(pe, br, g):
            u = group_maps(g)[0]
            mp = MAPS[br][u - MAP0[br]]
            i = g - GROUP0[br]
            o = SET0[br] + i // PER_SET[br]
            if i % PER_SET[br] == 0 and o:
                pe.wait_ge(on_ready, o)
            pe.wait_ge(pt_copied[g % 2], g // 2 + 1)
            w = 2 * DH if br == "C" else DH
            col = i % PER_SET[br] * w
            head = mp.head // 4 if br == "D" else mp.head
            nb = mp.nk // P
            for b in range(nb):
                ins = nc.tensor.matmul(OB[:, col:col + w], pt[g % 2][:, b * P:(b + 1) * P],
                                       V_[br][:, mp.k0 // P + b, head * w:(head + 1) * w], start=b == 0, stop=b == nb - 1)
            ins.then_inc(pv_done, 1)

        def set_end(br, g):
            i = g - GROUP0[br]
            return SET0[br] + i // PER_SET[br] if i >= 0 and i % PER_SET[br] == PER_SET[br] - 1 else None

        def set_maps(o):
            br = "ABCD"[o // 4]
            n = len(MAPS[br]) // 4
            return MAP0[br] + (o % 4) * n, n

        def dve_norm_set(dve, o):
            br = "ABCD"[o // 4]
            u0, n = set_maps(o)
            if br == "D":
                dve.wait_ge(p_ready, u0 + n)
                nc.vector.tensor_tensor(sinkt[:, 32:40], negmax[:, u0:u0 + n],
                                        vec[:, V_SINK + u0 - 96:V_SINK + u0 - 96 + n], ALU.add).then_inc(es_in, 1)
                dve.wait_ge(es_ready, o - 11)
                link(dve, nc.vector.tensor_tensor(psum_of[:, u0:u0 + n], psum_of[:, u0:u0 + n], sinkt[:, 40:48], ALU.add))
            if br == "C":
                dve.wait_ge(ss_ready, o - 7)
                nc.vector.tensor_scalar(stat[:, 4:8], rcp[:, 12:16], 1.0 / P, EPS, ALU.mult, ALU.add).then_inc(ms2_ready, 1)
                dve.wait_ge(rs2_ready, o - 7)
            else:
                dve.wait_ge(pv_done, GROUP0[br] + (o % 4 + 1) * PER_SET[br])
                if o:
                    dve.wait_ge(on_ready, o)
                link(dve, nc.vector.reciprocal(rcp[:, 0:8], psum_of[:, u0:u0 + n]))
            if o:
                wait_mb_full(dve, ("ot", o - 1))
            if br == "C":
                nc.vector.tensor_tensor(on[:], OB[:].rearrange("p (q c) -> p q c", q=TC),
                                        rstd[:, 4:8].unsqueeze(2).broadcast_to([P, TC, P]), ALU.mult).then_inc(on_ready, 1)
            else:
                nc.vector.tensor_tensor(on[:].rearrange("p q (h c) -> p h q c", h=2),
                                        OB[:].rearrange("p (h q c) -> p h q c", h=2, q=TC),
                                        rcp[:, 0:8].rearrange("p (h q) -> p h q", h=2).unsqueeze(3).broadcast_to(
                                            [P, 2, TC, DH]), ALU.mult).then_inc(on_ready, 1)

        def act_norm_set(act, o):
            br = "ABCD"[o // 4]
            if br == "C":
                act.wait_ge(pv_done, GROUP0[br] + (o % 4 + 1) * PER_SET[br])
                if o > 8:
                    act.wait_ge(ms2_ready, o - 8)
                for q in range(TC):
                    ins = nc.scalar.activation(gb[:, q * P:(q + 1) * P], OB[:, q * P:(q + 1) * P], ACT.Square,
                                               accum_out=rcp[:, 12 + q:13 + q])
                ins.then_inc(ss_ready, 1)
            if br == "D":
                act.wait_ge(es_in, o - 11)
                nc.scalar.activation(sinkt[:, 40:48], sinkt[:, 32:40], ACT.Exp).then_inc(es_ready, 1)

        def pe_transpose_set(pe, o):
            pe.wait_ge(on_ready, o + 1)
            wait_mb_free(pe, ("ot", o))
            for q in range(TC):
                ins = nc.tensor.transpose(MB[:, q * P:(q + 1) * P], on[:, q, :], ident)
            ins.then_inc(m_full, 1)

        def act_set_hi(act, o):
            br = "ABCD"[o // 4]
            wait_mb_full(act, ("ot", o))
            if br in "BC" and o % 4 == 0:
                wait_chunk_full(act, jobs["gb" + "ABCD"[o // 4 - 1]][-1].c)
            dst = (o2_hi if br == "D" else o_hi)[:, o % 4, :]
            if br == "C":
                nc.scalar.activation(dst, MB[:], ACT.Copy, scale=lamt[:, 6:7]).then_inc(ohi_ready, 1)
            else:
                nc.scalar.activation(dst, MB[:], ACT.Copy).then_inc(ohi_ready, 1)

        def dve_set_lo(dve, o):
            br = "ABCD"[o // 4]
            dve.wait_ge(ohi_ready, o + 1)
            hi, lo = ((o2_hi, o2_lo) if br == "D" else (o_hi, o_lo))
            if br == "C":
                nc.vector.scalar_tensor_tensor(lo[:, o % 4, :], MB[:], lamt[:, 6:7], hi[:, o % 4, :].bitcast(F32),
                                               ALU.mult, ALU.subtract).then_inc(olo_ready, 1)
            else:
                nc.vector.tensor_tensor(lo[:, o % 4, :], MB[:], hi[:, o % 4, :].bitcast(F32),
                                        ALU.subtract).then_inc(olo_ready, 1)

        shares = {br: spread(jobs[FILL[br]], NGROUP[br] + 1) for br in "ABCD"}

        def pe_attention(pe, br):
            g0, n = GROUP0[br], NGROUP[br]
            for u in group_maps(g0):
                pe_scores(pe, br, u)
            for s in range(n + 2):
                g = g0 + s
                if s + 1 < n:
                    for u in group_maps(g + 1):
                        pe_scores(pe, br, u)
                if s >= 2 and set_end(br, g - 2) is not None:
                    pe_transpose_set(pe, set_end(br, g - 2))
                if s <= n:
                    for j, i0, i1 in shares[br][s]:
                        pe_products(pe, j, i0, i1)
                if s < n:
                    pe_transpose_probs(pe, br, g)
                if 1 <= s <= n:
                    pe_values(pe, br, g - 1)

        def act_attention(act, br):
            g0, n = GROUP0[br], NGROUP[br]
            for u in group_maps(g0):
                act_exp(act, br, u)
            for s in range(n + 2):
                g = g0 + s
                if s + 1 < n:
                    for u in group_maps(g + 1):
                        act_exp(act, br, u)
                if s >= 2 and set_end(br, g - 2) is not None:
                    act_set_hi(act, set_end(br, g - 2))
                if s <= n:
                    act_stream(act, events_of(shares[br][s]))
                if s < n and g % 2 == 0:
                    copy_probs(act, g)
                if 1 <= s <= n and set_end(br, g - 1) is not None:
                    act_norm_set(act, set_end(br, g - 1))

        def dve_attention(dve, br):
            g0, n = GROUP0[br], NGROUP[br]
            for u in group_maps(g0):
                dve_bias(dve, br, u)
            for s in range(n + 2):
                g = g0 + s
                if s < n and br == "C":
                    dve_combine(dve, g)
                if s + 1 < n:
                    for u in group_maps(g + 1):
                        dve_bias(dve, br, u)
                if s >= 2 and set_end(br, g - 2) is not None:
                    dve_set_lo(dve, set_end(br, g - 2))
                if s <= n:
                    dve_stream(dve, events_of(shares[br][s]))
                if s < n and g % 2 == 1:
                    copy_probs(dve, g)
                if 1 <= s <= n and set_end(br, g - 1) is not None:
                    dve_norm_set(dve, set_end(br, g - 1))

        with nc.Fori(0, L) as l:
            with nc.Block() as block:
                @block.sync
                def _(sp):
                    sp.dma_start(vec[:], vec_d[l, :, 0:NVEC]).then_inc(vecs_in, 16)
                    sp.dma_start(lamv[:], vec_d[l, :, V_LAM:V_LAM + 256]).then_inc(vecs_in, 16)
                    for u in range(RAW):
                        load_tile(sp, l, u)
                    sp.wait_ge(init_out, 16)
                    sp.dma_start(rope_t[R, :, :], rope_d).then_inc(rope_in, 16)
                    for u in range(RAW, MIX_TILES):
                        load_tile(sp, l, u)

                @block.gpsimd
                def _(pool):
                    def load_table(th):
                        slot = tab[th % 2]
                        if th >= 2:
                            h = th - 2
                            pool.wait_ge(sn_ready, MAP0["B"] + 4 * h + 4 if h < 8 else MAP0["C"] + 8 * (h - 8) + 8)
                        for rows, nk in ((slice(0, 64), S - 64), (slice(64, P), S)):
                            if th < 8:
                                src = vb_d[l, th, rows, 0:nk]
                            else:
                                src = bass.AP(v_d.tensor, (th - 8) * P * VLEN + rows.start * (VLEN - 1) + 127,
                                              [[VLEN - 1, 64], [1, nk]])
                            pool.dma_start(slot[rows, 0:nk], src).then_inc(tab_in[th % 2], 16)

                    def load_window_table(h):
                        slot = tabD[h % 2]
                        if h >= 2:
                            pool.wait_ge(sn_ready, MAP0["D"] + 4 * (h - 2) + 4)
                        for half in range(2):
                            pool.dma_start(slot[64 * half:64 * half + 64, 64 + 64 * half:192 + 64 * half],
                                           bass.AP(v_d.tensor, (4 + h) * P * VLEN + 64 * half * VLEN + 447,
                                                   [[VLEN - 1, 64], [1, P]])
                                           ).then_inc(tabD_in[h % 2], 16)

                    nc.gpsimd.memset(tabA[:], 0.0).then_inc(pchain, 1)
                    pool.wait_ge(pchain, 1)
                    nc.gpsimd.memset(tabA[0:64, S - 64:S], NEG).then_inc(tabA_ready, 1)
                    pool_norm_root(pool, "x")
                    load_table(0)
                    load_table(1)
                    pool.wait_ge(init_out, 16)
                    load_window_table(0)
                    load_window_table(1)
                    pool_norm_root(pool, "cq")
                    pool_norm_root(pool, "ckv")
                    pool.wait_ge(kr_ready, 1)
                    nc.gpsimd.tensor_copy(kA[R, 1:HA, :], kA[R, 0:1, :].broadcast_to([ROPE, HA - 1, S])).then_inc(kr_copied, 1)
                    for th in range(2, 10):
                        load_table(th)
                    for h in range(4):
                        pool.wait_ge(ms2_ready, h + 1)
                        nc.gpsimd.tensor_tensor(rstd[:, 4:8], stat[:, 4:8], mhalf[:, 4:8], ALU.pow).then_inc(rs2_ready, 1)
                        if h < 2:
                            load_table(10 + h)
                    for h in range(2, 8):
                        load_window_table(h)
                    for i in range(2):
                        pool.wait_ge(tab_in[i], 32 * 6)
                        pool.wait_ge(tabD_in[i], 32 * 4)

                @block.scalar
                def _(act):
                    act_norm_squares(act, "x", xT)
                    act.wait_ge(lam_ready, 2)
                    nc.scalar.activation(lamt[:, 2:4], lamt[:, 0:2], ACT.Exp).then_inc(lame, 1)
                    act_stream(act, events_of(whole(jobs["ada0"])))
                    act.wait_ge(amul_ready, 1)
                    act_norm_apply(act, "x", mod[:, 0:KD], h_hi, [pr[0][:], pr[1][:]])
                    act_stream(act, events_of(whole(jobs["projA"])))
                    act_norm_squares(act, "cq", cqf, ready=lambda e, k: wait_out_of(e, "cq", k))
                    act_norm_apply(act, "cq", None, cq_hi, [pr[0][:], pr[1][:]])
                    act_norm_squares(act, "ckv", ckvf, ready=lambda e, k: wait_out_of(e, "ckv", 0))
                    act_norm_apply(act, "ckv", None, ckv_hi, [pr[0][:], pr[1][:]])
                    act_stream(act, events_of(whole(jobs["upA"])))
                    for i, br in enumerate("ABCD"):
                        act_attention(act, br)
                        if br != "C":
                            act_stream(act, events_of(whole(jobs["gb" + br])))
                    wait_chunk_full(act, jobs["gbD"][-3].c)
                    for k in range(KD):
                        act.wait_ge(merged_to, 2 * KD + k + 1)
                        nc.scalar.activation(h_hi[:, k, :], merged[:, k, :], ACT.Copy).then_inc(mhi_ready, 1)
                    act_stream(act, events_of(whole(jobs["out"])))

                @block.vector
                def _(dve):
                    chain[0] = 0
                    dve.wait_ge(vecs_in, 32)
                    for i in range(2):
                        a = 128 * i
                        ins = nc.vector.tensor_tensor_reduce(out=lamj[:, 0:64] if i == 0 else gb[:, 0:64], in0=lamv[:, a:a + 64], in1=lamv[:, a + 64:a + 128],
                                                             scale=1.0, scalar=0.0, op0=ALU.mult, op1=ALU.add,
                                                             accum_out=lamt[:, i:i + 1]).then_inc(lam_ready, 1)
                    nc.vector.tensor_tensor(lamt[:, 6:7], vec[:, V_SUB:V_SUB + 1], vec[:, V_OML:V_OML + 1], ALU.mult)
                    nc.vector.tensor_scalar(sinkt[:, 0:32], vec[:, V_SINK:V_SINK + 32], -1.0, None, ALU.mult)
                    dve.wait_ge(lame, 1)
                    link(dve, nc.vector.tensor_tensor(lamt[:, 4:5], lamt[:, 3:4], lamt[:, 2:3], ALU.subtract))
                    link(dve, nc.vector.tensor_tensor(lamt[:, 5:6], lamt[:, 4:5], vec[:, V_LI:V_LI + 1], ALU.subtract))
                    dve_norm_mean(dve, "x")
                    dve_stream(dve, events_of(whole(jobs["ada0"])))
                    wait_out_of(dve, "mod", 1)
                    nc.vector.scalar_tensor_tensor(amul[:], mod[:, 8:16], 1.0, vec[:, V_GMIX:V_GMIX + 8], ALU.add,
                                                   ALU.mult).then_inc(amul_ready, 1)
                    dve.wait_ge(amul_ready, 1)
                    wait_out_of(dve, "mod", 0)
                    dve_norm_apply(dve, "x", xT, amul, mod[:, 0:KD], h_hi, h_lo, [pr[0][:], pr[1][:]])
                    dve_stream(dve, events_of(whole(jobs["projA"])))
                    dve_norm_mean(dve, "cq")
                    dve_norm_apply(dve, "cq", cqf, vec[:, V_GQ:V_GQ + 2], None, cq_hi, cq_lo, [pr[0][:], pr[1][:]])
                    dve_norm_mean(dve, "ckv")
                    dve_norm_apply(dve, "ckv", ckvf, vec[:, V_GKV:V_GKV + 1], None, ckv_hi, ckv_lo, [pr[0][:], pr[1][:]])
                    dve.wait_ge(rope_in, 16)
                    wait_mb_full(dve, ("kr", 0))
                    nc.vector.tensor_tensor(qrot[R, :], MB[R, :], rope_t[R, 1, :], ALU.mult).then_inc(m_free, 1)
                    link(dve, nc.vector.tensor_tensor(qraw[R, :], qraw[R, :], rope_t[R, 0, :], ALU.mult))
                    nc.vector.tensor_tensor(kA[R, 0, :], qraw[R, :], qrot[R, :], ALU.add).then_inc(kr_ready, 1)

                    def rotate(h):
                        wait_mb_full(dve, ("qr", h))
                        if h:
                            dve.wait_ge(rot_ready, h)
                        else:
                            dve.wait_ge(kr_ready, 1)
                        nc.vector.tensor_tensor(qrot[R, :], MB[R, :], rope_t[R, 1, :], ALU.mult).then_inc(m_free, 1)
                        link(dve, nc.vector.tensor_tensor(qraw[R, :], qA[R, h, :], rope_t[R, 0, :], ALU.mult))
                        nc.vector.tensor_tensor(qA[R, h, :], qraw[R, :], qrot[R, :], ALU.add).then_inc(rot_ready, 1)

                    for j in jobs["upA"]:
                        dve_stream(dve, events_of([(j, 0, n_products(j))]))
                        if j.out == "qA" and j.arg:
                            rotate(j.arg - 1)
                    rotate(HA - 1)
                    dve.wait_ge(tabA_ready, 1)
                    for i, br in enumerate("ABCD"):
                        dve_attention(dve, br)
                        if br != "C":
                            dve_stream(dve, events_of(whole(jobs["gb" + br])))
                        if br == "C":
                            wait_out_of(dve, "mod", 2)
                            link(dve, nc.vector.tensor_scalar(mod[:, 16:24], mod[:, 16:24], 0.5, None, ALU.mult))
                    for k in range(KD):
                        dve.wait_ge(mhi_ready, k + 1)
                        nc.vector.tensor_tensor(h_lo[:, k, :], merged[:, k, :], h_hi[:, k, :].bitcast(F32),
                                                ALU.subtract).then_inc(mlo_ready, 1)
                    dve_stream(dve, events_of(whole(jobs["out"])))

                @block.tensor
                def _(pe):
                    pe_norm_sums(pe, "x")
                    for j in jobs["ada0"]:
                        pe_products(pe, j, 0, n_products(j))
                    pe_norm_spread(pe, "x")
                    for j in jobs["projA"]:
                        pe_products(pe, j, 0, n_products(j))
                    for name in ("cq", "ckv"):
                        pe_norm_sums(pe, name)
                        pe_norm_spread(pe, name)
                    wait_out_of(pe, "krope")
                    wait_mb_free(pe, ("kr", 0))
                    nc.tensor.matmul(MB[R, :], prot, qraw[R, :], start=True, stop=True).then_inc(m_full, 1)

                    def rotate(h):
                        wait_out_of(pe, "qA", h)
                        wait_mb_free(pe, ("qr", h))
                        nc.tensor.matmul(MB[R, :], prot, qA[R, h, :], start=True, stop=True).then_inc(m_full, 1)

                    for j in jobs["upA"]:
                        pe_products(pe, j, 0, n_products(j))
                        if j.out == "qA" and j.arg:
                            rotate(j.arg - 1)
                    rotate(HA - 1)
                    for br in "ABCD":
                        pe_attention(pe, br)
                        if br != "C":
                            for j in jobs["gb" + br]:
                                pe_products(pe, j, 0, n_products(j))
                    for j in jobs["out"]:
                        pe_products(pe, j, 0, n_products(j))

            shared_mark = chunk_mark[jobs["shared"][-1].c]
            slot_rows = slot_d.rearrange("(e s) w -> s e w", e=NE)

            def copy_half(eng, e, par):
                eng.wait_ge(xt_ready, e + 1)
                if not (isinstance(e, int) and e < 2):
                    eng.wait_ge(gu_ready, e - 1)
                if eng.engine == nc.scalar.engine:
                    nc.scalar.activation(xgT[par][:, 0:4, :], TB[0][:].rearrange("p (k t) -> p k t", k=4),
                                         ACT.Copy).then_inc(xt_copA, 1)
                else:
                    nc.vector.tensor_copy(xgT[par][:, 4:8, :], TB[1][:].rearrange("p (k t) -> p k t", k=4)
                                          ).then_inc(xt_copD, 1)

            def scale_half(eng, it, j):
                e, s = 8 * it + j, j % 4
                eng.wait_ge(dn_ready, e + 1)
                if not (isinstance(e, int) and e < 4):
                    eng.wait_ge(y_out[s], 16 * (2 * it + j // 4))
                gate = idx[j % 8][:, 2:3].bitcast(F32)
                bank = (SB, (OB, MB))[s % 2]
                if eng.engine == nc.scalar.engine:
                    nc.scalar.activation(y[s][:, 0:S], bank[0][:], ACT.Copy, scale=gate).then_inc(yA, 1)
                else:
                    nc.vector.tensor_scalar(y[s][:, S:D], bank[1][:], gate, None, ALU.mult).then_inc(yD, 1)

            with nc.Block() as block:
                @block.sync
                def _(sp):
                    sp.dma_start(rw[:], rw_d[l]).then_inc(rw_in, 16)
                    sp.dma_start(pay[:], pay_d).then_inc(rw_in, 16)
                    sp.dma_start(slot_d, skip_d).then_inc(slot_init, 16)
                    for u in range(MIX_TILES, MIX_TILES + 3):
                        load_tile(sp, l, u)
                    sp.dma_start(ew[0][:], wexp_d[l * NE]).then_inc(ew_in[0], 16)
                    for u in range(MIX_TILES + 3, NTILES):
                        load_tile(sp, l, u)
                    sp.dma_start(ew[1][:], wexp_d[l * NE + 1]).then_inc(ew_in[1], 16)
                    sp.wait_ge(dest_ready, 1)
                    sp.dma_start(ew[2][:], wexp_d[l * NE + 2]).then_inc(ew_in[2], 16)
                    sp.wait_ge(mark, shared_mark)
                    sp.dma_start(ew[3][:], wexp_d[l * NE + 3]).then_inc(ew_in[3], 16)
                    with sp.Fori(1, NE // 4) as it:
                        for j in range(4):
                            sp.wait_ge(dn_ready, 4 * it + j - 3)
                            sp.dma_start(ew[j][:], wexp_d[l * NE + 4 * it + j]).then_inc(ew_in[j], 16)

                @block.gpsimd
                def _(pool):
                    def step(it, j):
                        if not (isinstance(it, int) and 8 * it + j + 3 >= NE):
                            gather(it, j + 3)
                        if not (isinstance(it, int) and 8 * it + j == 0):
                            scatter(it, j - 1)

                    def gather(it, j):
                        e, s = 8 * it + j, j % 4
                        if not (isinstance(e, int) and e < 8):
                            pool.wait_ge(y_out[s], 16 * (2 * it + j // 4 - 1))
                        if not (isinstance(e, int) and e < 4):
                            pool.wait_ge(xt_ready, e - 3)
                        nc.gpsimd.tensor_copy(idx[j % 8][:], slots[:, e, :]).then_inc(pchain, 1)
                        pool.wait_ge(pchain, 3 + e)
                        pool.sem_inc(settled, 1)
                        nc.gpsimd.indirect_dma_start(
                            out=xg[s][:], out_offset=None, in_=h2_d,
                            in_offset=bass.IndirectOffsetOnAxis(ap=idx[j % 8][:, 0:1].bitcast(U32), axis=0),
                            bounds_check=S - 1, oob_is_err=False).then_inc(xg_in[s], 16)

                    def scatter(it, j):
                        e, s = 8 * it + j, j % 4
                        pool.wait_ge(yA, e + 1)
                        pool.wait_ge(yD, e + 1)
                        pool.sem_inc(settled, 1)
                        nc.gpsimd.indirect_dma_start(
                            out=y_d, out_offset=bass.IndirectOffsetOnAxis(ap=idx[j % 8][:, 1:2].bitcast(U32), axis=0),
                            in_=y[s][:], in_offset=None, bounds_check=S * TOPK - 1, oob_is_err=False).then_inc(y_out[s], 16)

                    pool_norm_root(pool, "x2")
                    pool.wait_ge(slot_init, 16)
                    pool.wait_ge(dest_ready, 1)
                    for i in range(NPAIR):
                        nc.gpsimd.indirect_dma_start(
                            out=slot_d, out_offset=bass.IndirectOffsetOnAxis(ap=dest[:, i:i + 1], axis=0),
                            in_=pay[:, i, :], in_offset=None, bounds_check=NE * S - 1, oob_is_err=False
                        ).then_inc(slot_out, 16)
                    pool.wait_ge(slot_out, 16 * NPAIR)
                    for i in range(4):
                        pool.dma_start(slots[:, 16 * i:16 * i + 16, :], slot_rows[0:BLK, 16 * i:16 * i + 16, :]
                                       ).then_inc(slots_in[i], 16)
                    pool.wait_ge(mark, shared_mark)
                    for i in range(4):
                        ins = nc.gpsimd.memset(xg[i][:], 0.0)
                    ins.then_inc(pchain, 1)
                    pool.wait_ge(pchain, 2)
                    for i in range(2):
                        pool.wait_ge(h2_out[i], 32)
                    for i in range(4):
                        pool.wait_ge(slots_in[i], 16)
                    for j in range(3):
                        gather(0, j)
                    for j in range(8):
                        step(0, j)
                    with pool.Fori(1, NE // 8 - 1) as it:
                        for j in range(8):
                            step(it, j)
                    for j in range(8):
                        step(NE // 8 - 1, j)
                    scatter(NE // 8 - 1, 7)
                    for s in range(4):
                        pool.wait_ge(y_out[s], 16 * (NE // 4))

                @block.scalar
                def _(act):
                    act_norm_squares(act, "x2", xT)
                    split_hi(act, MIX_TILES)
                    act_norm_apply(act, "x2", mod[:, 24:32], h_hi, [hf[:, k, :] for k in range(KD)])
                    act.wait_ge(logits_ready, 1)
                    nc.scalar.activation(score[:], OB[:, 0:TC * NE].rearrange("p (t e) -> p t e", t=TC),
                                         ACT.Sigmoid).then_inc(score_ready, 1)
                    for t in range(TC):
                        if t >= 2:
                            act.wait_ge(h2_out[t % 2], 16 * (t // 2))
                        act.wait_ge(htr_ready, 2 * t + 1)
                        nc.scalar.activation(htok[t % 2][:, 0:S], TB[0][:], ACT.Copy).then_inc(htr_copied[0], 1)
                        act.wait_ge(htr_copied[0], t + 1)
                        act.wait_ge(htr_copied[1], t + 1)
                        act.dma_start(h2_d[t * P:(t + 1) * P, :], htok[t % 2][:]).then_inc(h2_out[t % 2], 16)
                    act_stream(act, events_of(whole(jobs["shared"])), NTILES)

                    def step(it, j, first=False, last=False):
                        e = 8 * it + j
                        if not (last and j == 7):
                            copy_half(act, e + 1, (j + 1) % 2)
                        silu(e, j % 2)
                        if not (first and j == 0):
                            scale_half(act, it, j - 1)

                    def silu(e, s):
                        act.wait_ge(gu_ready, e + 1)
                        if not (isinstance(e, int) and e < 2):
                            act.wait_ge(act_done, e - 1)
                        nc.scalar.activation(sil[s][:], G[s][:, 0:2 * BLK].rearrange("p (f t) -> p f t", f=2),
                                             ACT.Silu).then_inc(silu_done, 1)

                    copy_half(act, 0, 0)
                    for j in range(8):
                        step(0, j, first=True)
                    with act.Fori(1, NE // 8 - 1) as it:
                        for j in range(8):
                            step(it, j)
                    for j in range(8):
                        step(NE // 8 - 1, j, last=True)
                    scale_half(act, NE // 8 - 1, 7)

                @block.vector
                def _(dve):
                    chain_base = chain[0]
                    dve_norm_mean(dve, "x2")
                    link(dve, nc.vector.scalar_tensor_tensor(amul[:], mod[:, 32:40], 1.0, vec[:, V_GFFN:V_GFFN + 8],
                                                             ALU.add, ALU.mult))
                    split_lo(dve, MIX_TILES)
                    dve_norm_apply(dve, "x2", xT, amul, mod[:, 24:32], h_hi, h_lo, [hf[:, k, :] for k in range(KD)])
                    dve.wait_ge(score_ready, 1)
                    link(dve, nc.vector.tensor_tensor(biased[:], score[:], vec[:, V_RB:V_RB + NE].unsqueeze(1)
                                                      .broadcast_to([P, TC, NE]), ALU.add))
                    for t in range(TC):
                        link(dve, nc.vector.max(top[:, t, :], biased[:, t, :]))
                        ins = nc.vector.max_index(topi[:, t, :], top[:, t, :], biased[:, t, :])
                    link(dve, ins)
                    link(dve, nc.vector.tensor_copy(topf[:], topi[:]))
                    four = [P, TC, TOPK, NE]
                    oh = onehot[:].rearrange("p (t k) e -> p t k e", t=TC)
                    om = ohmul[:].rearrange("p (t k) e -> p t k e", t=TC)
                    iota = cst[:, K_IOTA:K_IOTA + NE]
                    link(dve, nc.vector.tensor_tensor(oh, iota.unsqueeze(1).unsqueeze(1).broadcast_to(four),
                                                      topf[:, :, 0:TOPK].unsqueeze(3).broadcast_to(four), ALU.is_equal))
                    nc.vector.tensor_reduce(sel[:], onehot[:].rearrange("p (t k) e -> p t e k", t=TC), AX.X,
                                            ALU.add).then_inc(sel_ready, 1)
                    link(dve, nc.vector.tensor_tensor(om, oh, score[:].unsqueeze(2).broadcast_to(four), ALU.mult))
                    link(dve, nc.vector.tensor_reduce(gsel[:], om, AX.X, ALU.add))
                    for t in range(TC):
                        if t >= 2:
                            dve.wait_ge(h2_out[t % 2], 16 * (t // 2))
                        dve.wait_ge(htr_ready, 2 * t + 2)
                        nc.vector.tensor_copy(htok[t % 2][:, S:D], TB[1][:]).then_inc(htr_copied[1], 1)
                    link(dve, nc.vector.tensor_reduce(gsum[:, 0:TC], gsel[:], AX.X, ALU.add))
                    link(dve, nc.vector.reciprocal(gsum[:, 4:8], gsum[:, 0:TC]))
                    link(dve, nc.vector.tensor_tensor(gsel[:], gsel[:], gsum[:, 4:8].unsqueeze(2).broadcast_to([P, TC, TOPK]),
                                                      ALU.mult))
                    dve.wait_ge(rw_in, 32)
                    nc.vector.tensor_scalar(pay[:, :, 2].bitcast(F32), gsel[:].rearrange("p t k -> p (t k)"), 2.5, None,
                                            ALU.mult)
                    dve_stream(dve, events_of(whole(jobs["shared"][0:2])), NTILES)
                    dve.wait_ge(rank_ready, 1)
                    nc.vector.tensor_copy(cnt[0:NE, 0:1], SB[1][0:NE, 0:1]).then_inc(cnt_read, 1)
                    link(dve, nc.vector.tensor_tensor(posn[:], SB[0][:, 0:TC * NE].rearrange("p (t e) -> p t e", t=TC),
                                                      cst[:, K_IOTAS:K_IOTAS + NE].unsqueeze(1).broadcast_to([P, TC, NE]),
                                                      ALU.add))
                    link(dve, nc.vector.tensor_tensor(om, oh, posn[:].unsqueeze(2).broadcast_to(four), ALU.mult))
                    link(dve, nc.vector.tensor_reduce(destf[:].rearrange("p (t k) -> p t k", t=TC), om, AX.X, ALU.add))
                    nc.vector.tensor_copy(dest[:], destf[:]).then_inc(dest_ready, 1)
                    dve_stream(dve, events_of(whole(jobs["shared"][2:])), NTILES)

                    def step(it, j, first=False, last=False):
                        e = 8 * it + j
                        if not (last and j == 7):
                            copy_half(dve, e + 1, (j + 1) % 2)
                        gated_up(e, j % 2)
                        if not (first and j == 0):
                            scale_half(dve, it, j - 1)

                    def gated_up(e, s):
                        dve.wait_ge(silu_done, e + 1)
                        if not (isinstance(e, int) and e < 2):
                            dve.wait_ge(dn_ready, e - 1)
                        nc.vector.tensor_tensor(actT[s][:], sil[s][:], G[s][:, 2 * BLK:].rearrange("p (f t) -> p f t", f=2),
                                                ALU.mult).then_inc(act_done, 1)

                    copy_half(dve, 0, 0)
                    for j in range(8):
                        step(0, j, first=True)
                    with dve.Fori(1, NE // 8 - 1) as it:
                        for j in range(8):
                            step(it, j)
                    for j in range(8):
                        step(NE // 8 - 1, j, last=True)
                    scale_half(dve, NE // 8 - 1, 7)

                @block.tensor
                def _(pe):
                    pe_norm_sums(pe, "x2")
                    pe_norm_spread(pe, "x2")
                    pe.wait_ge(rw_in, 32)
                    for t in range(TC):
                        for k in range(KD):
                            if t == 0:
                                pe.wait_ge(nhi_ready, norm_k0["x2"] + k + 1)
                            ins = nc.tensor.matmul(OB[:, t * NE:(t + 1) * NE], hf[:, k, t * P:(t + 1) * P], rw[:, k, :],
                                                   start=k == 0, stop=k == KD - 1)
                    ins.then_inc(logits_ready, 1)
                    for t in range(TC):
                        for b in range(2):
                            if t:
                                pe.wait_ge(htr_copied[b], t)
                            for k in range(4):
                                ins = nc.tensor.transpose(TB[b][:, k * P:(k + 1) * P],
                                                          hf[:, 4 * b + k, t * P:(t + 1) * P], ident)
                            ins.then_inc(htr_ready, 1)
                    js = jobs["shared"]
                    for j in js[0:2]:
                        pe_products(pe, j, 0, n_products(j))
                    pe.wait_ge(sel_ready, 1)
                    for t in range(TC):
                        for b in range(t + 1):
                            nc.tensor.matmul(SB[0][:, t * NE:(t + 1) * NE], ones[:] if b < t else cst[:, K_UP:K_UP + P],
                                             sel[:, b, :], start=b == 0, stop=b == t)
                    for t in range(TC):
                        ins = nc.tensor.matmul(SB[1][0:NE, 0:1], sel[:, t, :], ones[:, 0:1], start=t == 0, stop=t == TC - 1)
                    ins.then_inc(rank_ready, 1)
                    for j in js[2:]:
                        pe_products(pe, j, 0, n_products(j))

                    def transposes(e, s, it):
                        pe.wait_ge(xg_in[s], 16 * (it + 1))
                        if not (isinstance(e, int) and e == 0):
                            pe.wait_ge(xt_copA, e)
                            pe.wait_ge(xt_copD, e)
                        else:
                            pe.wait_ge(htr_copied[0], TC)
                            pe.wait_ge(htr_copied[1], TC)
                        for k in range(KD):
                            ins = nc.tensor.transpose(TB[k // 4][:, k % 4 * P:(k % 4 + 1) * P],
                                                      xg[s][:, k * P:(k + 1) * P], ident)
                        ins.then_inc(xt_ready, 1)

                    def gate_up(e, s, it):
                        pe.wait_ge(xt_copA, e + 1)
                        pe.wait_ge(xt_copD, e + 1)
                        pe.wait_ge(ew_in[s], 16 * (it + 1))
                        if isinstance(e, int) and e < 2:
                            wait_chunk_out(pe, len(all_jobs) - 2 + e)
                        else:
                            pe.wait_ge(act_done, e - 1)
                        w = ew[s][:, 0:KD * 512].rearrange("p (k c) -> p k c", k=KD)
                        for f in range(4):
                            for k in range(KD):
                                ins = nc.tensor.matmul(G[s % 2][:, f * BLK:(f + 1) * BLK], w[:, k, f * P:(f + 1) * P],
                                                       xgT[s % 2][:, k, :], start=k == 0, stop=k == KD - 1)
                        ins.then_inc(gu_ready, 1)

                    def down(e, s):
                        pe.wait_ge(act_done, e + 1)
                        if not (isinstance(e, int) and e < 2):
                            pe.wait_ge(yA, e - 1)
                            pe.wait_ge(yD, e - 1)
                        else:
                            pe.wait_ge(cnt_read, 1)
                            pe.wait_ge(dest_ready, 1)
                        w = ew[s][:, KD * 512:].rearrange("p (f c) -> p f c", f=2)
                        for h, bank in enumerate((SB, (OB, MB))[s % 2]):
                            for f in range(2):
                                ins = nc.tensor.matmul(bank[:], actT[s % 2][:, f, :], w[:, f, h * S:(h + 1) * S],
                                                       start=f == 0, stop=f == 1)
                        ins.then_inc(dn_ready, 1)

                    def step(it, j, first=False, last=False):
                        e = 4 * it + j
                        if not (last and j == 3):
                            transposes(e + 1, (j + 1) % 4, it + (1 if j == 3 else 0))
                        gate_up(e, j, it)
                        if not (first and j == 0):
                            down(e - 1, (j - 1) % 4)

                    transposes(0, 0, 0)
                    for j in range(4):
                        step(0, j, first=True)
                    with pe.Fori(1, NE // 4 - 1) as it:
                        for j in range(4):
                            step(it, j)
                    for j in range(4):
                        step(NE // 4 - 1, j, last=True)
                    down(NE - 1, 3)

            with nc.Block() as block:
                def blocks(eng):
                    eng.wait_ge(cnt_ready, 2)
                    return eng.value_load(novf[0:1, 0:1], min_val=0, max_val=MAXOVF)

                @block.vector
                def _(dve):
                    n = cnt[0:NE, 0:1]
                    link(dve, nc.vector.tensor_scalar(cnt[0:NE, 1:2], n, float(BLK), None, ALU.is_gt))
                    link(dve, nc.vector.scalar_tensor_tensor(cnt[0:NE, 2:3], n, float(2 * BLK), cnt[0:NE, 1:2], ALU.is_gt, ALU.add))
                    nc.vector.scalar_tensor_tensor(cnt[0:NE, 3:4], n, float(3 * BLK), cnt[0:NE, 2:3], ALU.is_gt,
                                                   ALU.add).then_inc(cnt_ready, 1)
                    dve.wait_ge(o_xt, 1)
                    link(dve, nc.vector.tensor_copy(cnt[0:NE, 4:5], SB[0][0:NE, 0:1]))
                    nc.vector.tensor_scalar(cmpt[0:NE, :], cst[0:NE, K_IOTA32:K_IOTA32 + 48], cnt[0:NE, 4:5], None,
                                            ALU.is_ge).then_inc(o_xcD, 1)
                    dve.wait_ge(o_gu, 1)
                    f = ovff[0:1, :, :]
                    link(dve, nc.vector.tensor_scalar(f[:, 0, :], SB[1][0:1, 0:48], 512.0, None, ALU.mult))
                    link(dve, nc.vector.tensor_tensor(f[:, 1, :], cst[0:1, K_IOTA32:K_IOTA32 + 48], SB[1][0:1, 64:112],
                                                      ALU.subtract))
                    link(dve, nc.vector.tensor_scalar(f[:, 1, :], f[:, 1, :], 1.0, 128.0, ALU.add, ALU.mult))
                    nc.vector.tensor_copy(ovf[0:1, 0, :], SB[1][0:1, 0:48])
                    nc.vector.tensor_copy(novf[0:1, 0:1], SB[1][0:1, 128:129])
                    nc.vector.tensor_tensor(ovf[0:1, 1, :], f[:, 1, :], f[:, 0, :], ALU.add).then_inc(cnt_ready, 1)
                    nb = blocks(dve)
                    with dve.If(nb > 0):
                        with dve.Fori(0, nb) as i:
                            dve.wait_ge(o_xt, i + 2)
                            nc.vector.tensor_copy(xgT[0][:, 4:8, :], TB[1][:].rearrange("p (k t) -> p k t", k=4)
                                                  ).then_inc(o_xcD, 1)
                            dve.wait_ge(o_sil, i + 1)
                            nc.vector.tensor_tensor(actT[0][:], sil[0][:],
                                                    G[0][:, 2 * BLK:].rearrange("p (f t) -> p f t", f=2),
                                                    ALU.mult).then_inc(o_act, 1)
                            dve.wait_ge(o_dn, i + 1)
                            nc.vector.tensor_scalar(y[0][:, S:D], SB[1][:], idx[0][:, 2:3].bitcast(F32), None,
                                                    ALU.mult).then_inc(o_yD, 1)

                @block.tensor
                def _(pe):
                    pe.wait_ge(cnt_ready, 1)
                    nc.tensor.matmul(SB[0][0:NE, 0:1], cst[0:NE, K_UPI:K_UPI + NE], cnt[0:NE, 3:4], start=True,
                                     stop=True).then_inc(o_xt, 1)
                    pe.wait_ge(o_xcD, 1)
                    nc.tensor.matmul(SB[1][0:1, 0:48], ones[0:NE, 0:1], cmpt[0:NE, :], start=True, stop=True)
                    nc.tensor.matmul(SB[1][0:1, 64:112], cnt[0:NE, 3:4], cmpt[0:NE, :], start=True, stop=True)
                    nc.tensor.matmul(SB[1][0:1, 128:129], cnt[0:NE, 3:4], ones[0:NE, 0:1], start=True,
                                     stop=True).then_inc(o_gu, 1)
                    nb = blocks(pe)
                    w = ew[0][:, 0:KD * 512].rearrange("p (k c) -> p k c", k=KD)
                    wd = ew[0][:, KD * 512:].rearrange("p (f c) -> p f c", f=2)
                    with pe.If(nb > 0):
                        with pe.Fori(0, nb) as i:
                            pe.wait_ge(o_gat, 16 * i + 16)
                            for k in range(KD):
                                ins = nc.tensor.transpose(TB[k // 4][:, k % 4 * P:(k % 4 + 1) * P],
                                                          xg[0][:, k * P:(k + 1) * P], ident)
                            ins.then_inc(o_xt, 1)
                            pe.wait_ge(o_xcA, i + 1)
                            pe.wait_ge(o_xcD, i + 2)
                            for f in range(4):
                                for k in range(KD):
                                    ins = nc.tensor.matmul(G[0][:, f * BLK:(f + 1) * BLK], w[:, k, f * P:(f + 1) * P],
                                                           xgT[0][:, k, :], start=k == 0, stop=k == KD - 1)
                            ins.then_inc(o_gu, 1)
                            pe.wait_ge(o_act, i + 1)
                            for h in range(2):
                                for f in range(2):
                                    ins = nc.tensor.matmul(SB[h][:], actT[0][:, f, :], wd[:, f, h * S:(h + 1) * S],
                                                           start=f == 0, stop=f == 1)
                            ins.then_inc(o_dn, 1)

                @block.scalar
                def _(act):
                    nb = blocks(act)
                    with act.If(nb > 0):
                        with act.Fori(0, nb) as i:
                            act.wait_ge(o_xt, i + 2)
                            nc.scalar.activation(xgT[0][:, 0:4, :], TB[0][:].rearrange("p (k t) -> p k t", k=4),
                                                 ACT.Copy).then_inc(o_xcA, 1)
                            act.wait_ge(o_gu, i + 2)
                            nc.scalar.activation(sil[0][:], G[0][:, 0:2 * BLK].rearrange("p (f t) -> p f t", f=2),
                                                 ACT.Silu).then_inc(o_sil, 1)
                            act.wait_ge(o_dn, i + 1)
                            nc.scalar.activation(y[0][:, 0:S], SB[0][:], ACT.Copy,
                                                 scale=idx[0][:, 2:3].bitcast(F32)).then_inc(o_yA, 1)

                @block.gpsimd
                def _(pool):
                    nb = blocks(pool)
                    pool.sem_inc(o_turn, 1)
                    with pool.If(nb > 0):
                        with pool.Fori(0, nb) as i:
                            pool.wait_ge(o_load, 32 * i + 32)
                            pool.sem_inc(settled, 1)
                            nc.gpsimd.indirect_dma_start(
                                out=xg[0][:], out_offset=None, in_=h2_d,
                                in_offset=bass.IndirectOffsetOnAxis(ap=idx[0][:, 0:1].bitcast(U32), axis=0),
                                bounds_check=S - 1, oob_is_err=False).then_inc(o_gat, 16)
                            pool.wait_ge(o_yA, i + 1)
                            pool.wait_ge(o_yD, i + 1)
                            pool.sem_inc(settled, 1)
                            nc.gpsimd.indirect_dma_start(
                                out=y_d, out_offset=bass.IndirectOffsetOnAxis(ap=idx[0][:, 1:2].bitcast(U32), axis=0),
                                in_=y[0][:], in_offset=None, bounds_check=S * TOPK - 1, oob_is_err=False
                            ).then_inc(o_put, 16)
                            pool.wait_ge(o_put, 16 * i + 16)
                            pool.sem_inc(o_turn, 1)

                @block.sync
                def _(sp):
                    nb = blocks(sp)
                    with sp.If(nb > 0):
                        with sp.Fori(0, nb) as i:
                            sp.wait_ge(o_turn, i + 1)
                            e = sp.value_load(ovf[0:1, 0, bass.ds(i, 1)], min_val=0, max_val=NE - 1)
                            row = sp.value_load(ovf[0:1, 1, bass.ds(i, 1)], min_val=0, max_val=NE * S - BLK)
                            sp.dma_start(idx[0][:], slot_d[bass.ds(row, BLK), :]).then_inc(o_load, 16)
                            sp.dma_start(ew[0][:], wexp_d[l * NE + e]).then_inc(o_load, 16)

            y_rows = y_d.rearrange("(t k) d -> t k d", k=TOPK)
            with nc.Block() as block:
                @block.sync
                def _(sp):
                    for t in range(TC):
                        if t >= 2:
                            sp.wait_ge(ytr, 2 * (t - 1))
                        sp.dma_start(yt[t % 2][:], y_rows[t * P:(t + 1) * P]).then_inc(yt_in[t % 2], 16)

                @block.vector
                def _(dve):
                    def add_back(t):
                        for b in range(2):
                            dve.wait_ge(ytr, 2 * t + b + 1)
                            for k in range(4):
                                x = xT[:, 4 * b + k, t * P:(t + 1) * P]
                                ins = nc.vector.scalar_tensor_tensor(x, G[b][:, k * P:(k + 1) * P],
                                                                     mod[:, 40 + 4 * b + k:41 + 4 * b + k], x, ALU.mult, ALU.add)
                            ins.then_inc(yadd[b], 1)
                    for t in range(TC):
                        v = yt[t % 2]
                        dve.wait_ge(yt_in[t % 2], 16 * (t // 2 + 1))
                        link(dve, nc.vector.tensor_tensor(v[:, 0:3, :], v[:, 0:3, :], v[:, 3:6, :], ALU.add))
                        link(dve, nc.vector.tensor_tensor(v[:, 0, :], v[:, 0, :], v[:, 1, :], ALU.add))
                        nc.vector.tensor_tensor(v[:, 0, :], v[:, 0, :], v[:, 2, :], ALU.add).then_inc(ysum, 1)
                        if t:
                            add_back(t - 1)
                    add_back(TC - 1)

                @block.tensor
                def _(pe):
                    for t in range(TC):
                        pe.wait_ge(ysum, t + 1)
                        for b in range(2):
                            if t:
                                pe.wait_ge(yadd[b], t)
                            for k in range(4):
                                ins = nc.tensor.transpose(G[b][:, k * P:(k + 1) * P],
                                                          yt[t % 2][:, 0, (4 * b + k) * P:(4 * b + k + 1) * P], ident)
                            ins.then_inc(ytr, 1)
            nc.gpsimd.dma_reset(per_layer)
            nc.all_engine_barrier(sems_to_clear=per_layer)

        with nc.Block() as block:
            norm_no["end"], norm_k["end"], norm_k0["end"] = 0, KD, 0
            m_use[("st", "end")] = m_use[("rb", "end")] = 0
            m_full_no[("rb", "end")] = 0

            @block.sync
            def _(sp):
                for k in range(KD):
                    sp.wait_ge(nt_ready, k + 1)
                    sp.dma_start(out_d[:, k, :], hf[:, k, :]).then_inc(init_out, 16)
                sp.wait_ge(init_out, 16 + 16 * KD)

            @block.gpsimd
            def _(pool):
                pool_norm_root(pool, "end")

            @block.scalar
            def _(act):
                act_norm_squares(act, "end", xT)

            @block.tensor
            def _(pe):
                pe_norm_sums(pe, "end")
                pe_norm_spread(pe, "end")

            @block.vector
            def _(dve):
                dve_norm_mean(dve, "end")
                wait_mb_full(dve, ("rb", "end"))
                for k in range(KD):
                    nc.vector.scalar_tensor_tensor(hf[:, k, :], xT[:, k, :], gvec[:, 8 + k:9 + k], MB[:], ALU.mult,
                                                   ALU.mult).then_inc(nt_ready, 1)


def _bucket(rel):
    half, exact = 16, 8
    ret = np.where(rel > 0, half, 0)
    n = np.abs(rel)
    large = exact + (np.log(np.maximum(n, 1).astype(np.float32) / np.float32(exact)) / np.float32(math.log(1024 / exact))
                     * np.float32(half - exact)).astype(np.int32)
    return ret + np.where(n < exact, n, np.minimum(large, half - 1))


def _constants():
    c = np.zeros((P, NCONST), np.float32)
    i = np.arange(P)
    c[:, K_ID:K_ID + P] = np.eye(P)
    c[:, K_UP:K_UP + P] = i[:, None] < i[None, :]
    c[:64, K_UPI:K_UPI + 64] = i[:64, None] <= i[None, :64]
    c[:, K_IOTA:K_IOTA + 64] = np.arange(64)
    c[:, K_IOTAS:K_IOTAS + 64] = np.arange(64) * S
    h = ROPE // 2
    for m in range(h):
        c[NOPE + h + m, K_PROT + m] = -1.0
        c[NOPE + m, K_PROT + h + m] = 1.0
    c[:, K_IOTA32:K_IOTA32 + 48] = np.arange(48)
    onehot = np.zeros((32, VLEN), np.float32)
    onehot[_bucket(np.arange(VLEN) - (S - 1)), np.arange(VLEN)] = 1.0
    inv = np.float32(10000.0) ** (-np.arange(0, ROPE, 2, dtype=np.float32) / np.float32(ROPE))
    ang = np.arange(S, dtype=np.float32)[None, :] * inv[:, None]
    rope = np.stack([np.tile(np.cos(ang), (2, 1)), np.tile(np.sin(ang), (2, 1))], 1).astype(np.float32)
    pay = np.zeros((P, TC, TOPK, 4), np.int32)
    tok = np.arange(TC)[None, :, None] * P + i[:, None, None]
    pay[..., 0] = tok
    pay[..., 1] = tok * TOPK + np.arange(TOPK)
    skip = np.full((NE * S, 4), SKIP, np.int32)
    return c, onehot, rope, pay.reshape(P, NPAIR, 4), skip


def _tile(a, k):
    n = a.shape[1]
    t = a.reshape(k, P, n).transpose(1, 0, 2).reshape(P, k * n)
    return t if t.shape[1] == 1024 else np.concatenate([t, np.zeros((P, 1024 - t.shape[1]), a.dtype)], 1)


def _lay_out_tiles(w, l):
    out = []
    for t in TILES:
        if t[0] == "ada":
            out.append(_tile(w["ada_w"][l][:, t[1] * P:(t[1] + 1) * P], KD))
        elif t[0] == "in":
            out.append(_tile(w["w_in"][l][:, t[1]:t[1] + P], KD))
        elif t[0] == "kvup":
            out.append(_tile(w["w_kv_up"][l], 1))
        elif t[0] == "qup":
            out.append(_tile(w["w_q_up"][l][:, t[1] * 384:(t[1] + 1) * 384], 2))
        elif t[0] == "branch":
            out.append(_tile(w["w_branch"][l, t[1]][:, t[2] * 256:(t[2] + 1) * 256], 4))
        elif t[0] == "out":
            out.append(_tile(w["w_out"][l][:, t[1] * P:(t[1] + 1) * P], KD))
        elif t[0] == "sgu":
            out.append(_tile(w["w_shared_gu"][l][:, t[1] * P:(t[1] + 1) * P], KD))
        else:
            out.append(_tile(w["w_shared_down"][l][:, t[1] * 512:(t[1] + 1) * 512], 2))
    return np.stack(out)


def _columns(v):
    return v.reshape(-1, P).T


def kernel(**inputs):
    import concourse.bacc as bacc
    from concourse.bass_utils import run_bass_kernel_spmd

    w = {k: np.asarray(v) for k, v in inputs.items()}
    const, onehot, rope, pay, skip = _constants()
    vecs = []
    for l in range(L):
        li = 0.8 - 0.6 * math.exp(-0.3 * l)
        rep = lambda a: np.broadcast_to(a.reshape(1, -1), (P, a.size))
        vecs.append(np.concatenate([
            _columns(w["ada_b"][l]), _columns(w["norm_mix_g"][l]), _columns(w["norm_ffn_g"][l]),
            _columns(w["q_norm_g"][l]), _columns(w["kv_norm_g"][l]), _columns(w["diff_subln_g"][l]),
            rep(np.repeat(w["sinks_d"][l], TC)), np.full((P, 1), li, np.float32), np.full((P, 1), 1.0 - li, np.float32),
            rep(w["router_bias"][l]), rep(w["diff_lambda"][l])], 1))
    at = np.clip(P - 1 - np.arange(P)[:, None] + np.arange(S)[None, :], 0, VLEN - 1)
    at = np.clip(S - 1 - at, -63, 256) + 63
    arrays = {
        "xT": np.ascontiguousarray(w["x"][0].T.reshape(KD, P, S).transpose(1, 0, 2)),
        "wmix": np.concatenate([_lay_out_tiles(w, l) for l in range(L)]),
        "wexp": np.concatenate([
            w["w_exp_gu"].reshape(L * NE, KD, P, 512).transpose(0, 2, 1, 3).reshape(L * NE, P, KD * 512),
            w["w_exp_down"].reshape(L * NE, 2, P, D).transpose(0, 2, 1, 3).reshape(L * NE, P, 2 * D)], 2),
        "vec": np.stack(vecs),
        "gvec": np.concatenate([_columns(w["c"][0]), _columns(w["final_norm_g"])], 1),
        "rw": np.ascontiguousarray(w["router_w"].reshape(L, KD, P, NE).transpose(0, 2, 1, 3)),
        "vb": np.ascontiguousarray(w["rel_bias_b"][:, :, at]),
        "t5": w["t5_table"], "const": const, "onehot": onehot, "rope": rope, "pay": pay, "skip": skip,
    }
    nc = bacc.Bacc("TRN2", target_bir_lowering=False, num_devices=1)
    aps = [nc.dram_tensor(f"in_{n}", a.shape, mybir.dt.from_np(a.dtype), kind="ExternalInput").ap() for n, a in arrays.items()]
    out = nc.dram_tensor("out", [P, KD, S], F32, kind="ExternalOutput").ap()
    hybrid_trunk(nc, *aps, out)
    r = run_bass_kernel_spmd(nc, [{f"in_{n}": np.ascontiguousarray(a) for n, a in arrays.items()}], core_ids=[0])
    o = np.asarray(r.results[0]["out"])
    return np.ascontiguousarray(o.transpose(2, 1, 0).reshape(1, S, D))
```

```python
import math
from contextlib import ExitStack

import numpy as np

import concourse.bass as bass
from concourse import mybir

ALU = mybir.AluOpType
ACT = mybir.ActivationFunctionType
AX = mybir.AxisListType
F32 = mybir.dt.float32
F32R = mybir.dt.float32r
I32 = mybir.dt.int32
U32 = mybir.dt.uint32

P = 128
S = 512
D = 1024
L = 2
KD = D // P
TC = S // P
EPS = 1e-6
NEG = -1e30
BIG = 3.0e38

NOPE, ROPE, HA = 64, 32, 8
DH = 64
DQ = NOPE + ROPE
Q_LORA, KV_LORA = 256, 128
BW = 512
NE = 64
TOPK = 6
BLK = 128
NPAIR = TC * TOPK
MAXOVF = S * TOPK // BLK + 8
SKIP = 1 << 20
VLEN = 640

C_KV = Q_LORA
C_B = Q_LORA + KV_LORA + ROPE
C_C = C_B + 3 * BW
C_D = C_C + 3 * BW
C_G = C_D + BW + 256

V_ADAB, V_GMIX, V_GFFN, V_GQ, V_GKV, V_SUB, V_SINK, V_LI, V_OML, V_RB, V_LAM = (
    0, 48, 56, 64, 66, 67, 68, 100, 101, 102, 166)
NVEC = 166

K_ID, K_PROT, NCONST = 0, 128, 160
K_UP, K_UPI, K_IOTA, K_IOTA32, NROUTE = 0, 128, 192, 256, 304


RAW = 3
SPLIT = 2


class Job:

    def __init__(self, kind, tiles, out, act="h", k=KD, m=P, col=0, arg=0):
        self.kind, self.tiles, self.out, self.act, self.k, self.m, self.col, self.arg = (
            kind, tiles, out, act, k, m, col, arg)
        self.after = []


def place_ada(phases):
    jobs = [job for jobs in phases for job in jobs[:-1] if job.kind == "T"]
    for i in range(48):
        jobs[i * len(jobs) // 48].after.append(("ada", (16 + i) % 48))


def with_turns(jobs, turns):
    out = []
    for i, job in enumerate(jobs):
        out.append(job)
        if i:
            out += turns[i - 1:i]
    return out + turns[len(jobs) - 1:]


def make_jobs():
    j = {}
    tile = lambda c: [("in", c)]
    j["projA"] = [Job("T", tile(0), "cq", arg=0), Job("T", tile(P), "cq", arg=1), Job("T", tile(C_KV), "ckv"),
                  Job("T", tile(C_KV + KV_LORA - NOPE), "krope", m=DQ)]
    j["upA"] = ([Job("T", [("kvup",)], "kA", act="ckv", k=1, col=P * h, arg=h) for h in range(HA)]
                + [Job("VA", [("kvup",)], "vA", act="ckv", k=1, arg=t) for t in range(TC)]
                + [Job("T", [("qup", h // 4)], "qA", act="cq", k=2, m=DQ, col=DQ * (h % 4), arg=h) for h in range(HA)])
    for br, c in (("B", C_B), ("C", C_C)):
        j["proj" + br] = ([Job("T", tile(c + P * i), "q" + br, arg=i) for i in range(4)]
                          + [Job("T", tile(c + P * (4 + i)), "k" + br, arg=i) for i in range(4)]
                          + with_turns([Job("T", tile(c + P * (8 + i)), "vt", arg=4 * (br == "C") + i) for i in range(4)],
                                       [Job("turn", [], "v" + br, arg=i) for i in range(4)]))
    j["projD"] = ([Job("T", tile(C_D + P * i), "qD", arg=i) for i in range(4)]
                  + with_turns([Job("T", tile(C_D + P * 5), "vt", arg=8), Job("T", tile(C_D + P * 4), "kD")],
                               [Job("turn", [], "vD")]))
    for n, br in enumerate("ABCD"):
        jobs = []
        for i in range(KD // 2):
            m = n * KD + 2 * i
            jobs += [Job("T", tile(C_G + m * P), "gate", arg=m), Job("T", tile(C_G + (m + 1) * P), "gate", arg=m + 1)]
            jobs += [Job("T", [("branch", n, i)], "branch", act="o", k=4, col=P * e, arg=m + e) for e in range(2)]
        j["gb" + br] = jobs
    place_ada([j[phase] for phase in ("projB", "gbA", "projC", "gbB", "projD", "gbC", "gbD")])
    j["out"] = [Job("T", [("out", m)], "x", act="m", arg=m) for m in range(KD)]
    j["shared"] = ([Job("T", [("sgu", t)], "sg" if i % 2 == 0 else "su", arg=i // 2) for i, t in enumerate((0, 2, 1, 3))]
                   + [Job("T", [("sdn", i // 4)], "ys", act="s", k=2, col=P * (i % 4), arg=i) for i in range(KD)])
    return j


ORDER = ("projA", "upA", "projB", "gbA", "projC", "gbB", "projD", "gbC", "gbD", "out", "shared")


def tile_stream():
    names, jobs = [], make_jobs()
    for phase in ORDER:
        if phase == "shared":
            mixer = len(names)
        for job in jobs[phase]:
            names += [t for t in job.tiles if t not in names] + job.after
    return names, mixer


TILES, MIX_TILES = tile_stream()
NTILES = len(TILES)


class Map:
    def __init__(self, br, head, qb, t=0):
        self.br, self.head, self.qb, self.t = br, head, qb, t
        self.k0 = max(qb - 1, 0) * P if br == "D" else 0
        self.nk = (qb + 1) * P - self.k0


def make_maps(br):
    if br == "C":
        return [Map(br, h, qb, t) for h in range(4) for qb in range(TC) for t in range(2)]
    return [Map(br, h, qb) for h in range(8) for qb in range(TC)]


MAPS = {br: make_maps(br) for br in "ABCD"}
MAP0 = {"A": 0, "B": 32, "C": 64, "D": 96}
GROUP0 = {"A": 0, "B": 32, "C": 64, "D": 80}
NGROUP = {"A": 32, "B": 32, "C": 16, "D": 32}
PER_SET = {"A": 8, "B": 8, "C": 4, "D": 8}
SET0 = {"A": 0, "B": 4, "C": 8, "D": 12}
FILL = {"A": "projB", "B": "projC", "C": "projD", "D": "gbC"}


def map_group(u):
    if u < 64:
        return u
    return 64 + (u - 64) // 2 if u < 96 else 80 + u - 96


def group_maps(g):
    if g < 64:
        return [g]
    return [64 + 2 * (g - 64), 65 + 2 * (g - 64)] if g < 80 else [96 + g - 80]


def hybrid_trunk(nc, xT_d, wmix_d, wexp_d, vec_d, gvec_d, cb_d, ada0_d, rw_d, vb_d, t5_d, const_d, rcst_d, onehot_d,
                 rope_d, pay_d, skip_d,
                 out_d):
    ctx = ExitStack()
    with ctx:
        base = (nc.sbuf_base + 63) // 64 * 64
        end = nc.sbuf_usable_end
        ctx.enter_context(nc.sbuf_tensor("arena", [P, (end - base) // 4 - 64], F32))
        cursor = [base]

        def place(name, shape, dt=F32, at=None):
            size = int(np.prod(shape[1:])) * 4
            size = (size + 31) // 32 * 32
            off = cursor[0] if at is None else at
            assert off + size <= end, (name, off + size, end)
            if at is None:
                cursor[0] += size
            t = nc.alloc_sbuf_tensor_at(name, shape, dt, offset=off)
            t_end[name] = off + size
            return t

        t_end = {}
        xT = place("xT", [P, KD, S])
        cst = place("cst", [P, NCONST])
        vec = place("vec", [P, NVEC])
        gvec = place("gvec", [P, 24])
        cb = place("cb", [P, D])
        mod = place("mod", [P, 48])
        amul = place("amul", [P, KD])
        ones = place("ones", [P, P])
        mhalf = place("mhalf", [P, 8])
        stat = place("stat", [P, 8])
        rstd = place("rstd", [P, 8])
        zero = place("zero", [P, 4])
        tab = [place(f"tab{i}", [P, S]) for i in range(2)]
        tabD = [place(f"tabD{i}", [P, 2 * P]) for i in range(2)]
        keep_end = cursor[0]
        h_hi = place("h_hi", [P, KD, S], F32R)
        h_lo = place("h_lo", [P, KD, S], F32R)
        raw = [place(f"raw{i}", [P, 1024]) for i in range(RAW)]
        w_hi = [place(f"w_hi{i}", [P, 1024], F32R) for i in range(SPLIT)]
        w_lo = [place(f"w_lo{i}", [P, 1024], F32R) for i in range(SPLIT)]
        both_end = cursor[0]
        ctmp = place("ctmp", [P, 2, D], at=keep_end + 65536)
        ada0 = place("ada0", [P, 16, D], at=keep_end)
        sn = [place(f"sn{i}", [P, S]) for i in range(2)]
        pr = [place(f"pr{i}", [P, S]) for i in range(4)]
        pt = [place(f"pt{i}", [P, S]) for i in range(2)]
        on = place("on", [P, TC, P])
        gt = [place(f"gt{i}", [P, S]) for i in range(2)]
        negmax = place("negmax", [P, P])
        psum_of = place("psum_of", [P, P])
        rcp = place("rcp", [P, 16])
        sinkt = place("sinkt", [P, 48])
        lamt = place("lamt", [P, 8])
        o_hi = place("o_hi", [P, 4, S], F32R)
        o_lo = place("o_lo", [P, 4, S], F32R)
        m0 = cursor[0]
        merged = place("merged", [P, KD, S])
        rope_t = place("rope_t", [P, 2, S], at=m0)
        tabA = place("tabA", [P, S], at=m0 + 4096)
        qraw = place("qraw", [P, S], at=m0 + 6144)
        qrot = place("qrot", [P, S], at=m0 + 8192)
        lamv = place("lamv", [P, 256], at=m0 + 10240)
        r0 = cursor[0]
        qA = place("qA", [P, HA, S])
        kA = place("kA", [P, HA, S])
        vA = place("vA", [P, TC, BW])
        r1 = cursor[0]
        qB = place("qB", [P, 4, S])
        kB = place("kB", [P, 4, S])
        vB = place("vB", [P, TC, BW])
        cqf = place("cqf", [P, 2, S], at=r1)
        ckvf = place("ckvf", [P, 1, S], at=r1 + 4096)
        cq_hi = place("cq_hi", [P, 2, S], F32R, at=r1 + 6144)
        cq_lo = place("cq_lo", [P, 2, S], F32R, at=r1 + 10240)
        ckv_hi = place("ckv_hi", [P, 1, S], F32R, at=r1 + 14336)
        ckv_lo = place("ckv_lo", [P, 1, S], F32R, at=r1 + 16384)
        qC = place("qC", [P, 4, S], at=r0)
        kC = place("kC", [P, 4, S], at=r0 + 8192)
        vC = place("vC", [P, TC, BW], at=r0 + 16384)
        o2_hi = place("o2_hi", [P, 4, S], F32R, at=r0 + 24576)
        o2_lo = place("o2_lo", [P, 4, S], F32R, at=r0 + 32768)
        qD = place("qD", [P, 4, S], at=r1)
        kD = place("kD", [P, 2, S], at=r1 + 8192)
        vD = place("vD", [P, TC, P], at=r1 + 12288)
        cursor[0] = both_end
        hf = place("hf", [P, KD, S])
        s_hi = place("s_hi", [P, 2, S], F32R)
        s_lo = place("s_lo", [P, 2, S], F32R)
        sgt = place("sgt", [P, S])
        htok = [place(f"htok{i}", [P, D]) for i in range(2)]
        shared_end = cursor[0]
        rcst = place("rcst", [P, NROUTE])
        rw = place("rw", [P, KD, NE])
        score = place("score", [P, TC, NE])
        biased = place("biased", [P, TC, NE])
        top = place("top", [P, TC, 8])
        topi = place("topi", [P, TC, 8], U32)
        topf = place("topf", [P, TC, 8])
        sel = place("sel", [P, TC, NE])
        posn = place("posn", [P, TC, NE])
        gsel = place("gsel", [P, TC, TOPK])
        gsum = place("gsum", [P, 8])
        dest = place("dest", [P, NPAIR], U32)
        destf = place("destf", [P, NPAIR])
        pay = place("pay", [P, NPAIR, 4], I32)
        cnt = place("cnt", [P, 8])
        cmpt = place("cmpt", [P, 48])
        ovf = place("ovf", [P, 2, 48], I32)
        ovff = place("ovff", [P, 3, 48])
        novf = place("novf", [P, 8], I32)
        cntrow = place("cntrow", [P, NE], I32)
        slots = place("slots", [P, NE, 4], I32)
        idx = [place(f"idx{i}", [P, 4], I32) for i in range(8)]
        ew = [place(f"ew{i}", [P, 6144]) for i in range(3)]
        assert cursor[0] <= end, (cursor[0], end)
        onehot = place("onehot", [P, NPAIR, NE], at=t_end["ew1"])
        ohmul = place("ohmul", [P, NPAIR, NE], at=t_end["ew1"] + 4 * NPAIR * NE)
        cursor[0] = keep_end
        ew.append(place("ew3", [P, 6144]))
        xg = [place(f"xg{i}", [P, D]) for i in range(4)]
        xgT = [place(f"xgT{i}", [P, KD, BLK]) for i in range(2)]
        sil = [place(f"sil{i}", [P, 2, BLK]) for i in range(2)]
        actT = [place(f"actT{i}", [P, 2, BLK]) for i in range(2)]
        y = [place(f"y{i}", [P, D]) for i in range(4)]
        a_hi = [place(f"a_hi{i}", [P, 2, BLK], F32R) for i in range(2)]
        a_lo = [place(f"a_lo{i}", [P, 2, BLK], F32R) for i in range(2)]
        d_hi, d_lo = place("d_hi", [P, 2, D], F32R), place("d_lo", [P, 2, D], F32R)
        assert cursor[0] <= shared_end
        yt = [place(f"yt{i}", [P, TOPK, D], at=keep_end + 24576 * i) for i in range(2)]

        PB = [ctx.enter_context(nc.psum_tensor(f"bank{i}", [P, S], F32)) for i in range(8)]
        G, SB, TB, OB, MB = PB[0:2], PB[2:4], PB[4:6], PB[6], PB[7]

        v_d = nc.dram_tensor("v_d", [12, P, VLEN], F32, kind="Internal").ap()
        h2_d = nc.dram_tensor("h2_d", [S, D], F32, kind="Internal").ap()
        slot_d = nc.dram_tensor("slot_d", [NE * S, 4], I32, kind="Internal").ap()
        y_d = nc.dram_tensor("y_d", [S * TOPK, D], F32, kind="Internal").ap()

        sems = {}

        def sem(name):
            sems[name] = ctx.enter_context(nc.semaphore(name))
            return sems[name]

        tile_in = [sem(f"tile_in{i}") for i in range(RAW)]
        ada_done = sem("ada_done")
        hi_done = sem("hi_done")
        lo_done = sem("lo_done")
        mark = sem("mark")
        chunk_out = [sem(f"chunk_out{i}") for i in range(2)]
        m_full, m_free = sem("m_full"), sem("m_free")
        sq_ready, sq_used = [sem(f"sq_ready{i}") for i in range(2)], sem("sq_used")
        ms_ready = sem("ms_ready")
        rstd_ready = sem("rstd_ready")
        nt_ready, nhi_ready, nlo_ready = sem("nt_ready"), sem("nhi_ready"), sem("nlo_ready")
        dchain = sem("dchain")
        achain = sem("achain")
        pchain = sem("pchain")
        vecs_in, rope_in = sem("vecs_in"), sem("rope_in")
        tabA_ready = sem("tabA_ready")
        amul_ready = sem("amul_ready")
        kr_ready, kr_copied = sem("kr_ready"), sem("kr_copied")
        rot_ready = sem("rot_ready")
        tab_in = [sem(f"tab_in{i}") for i in range(2)]
        tabD_in = [sem(f"tabD_in{i}") for i in range(2)]
        sc_ready = sem("sc_ready")
        sn_ready = sem("sn_ready")
        p_ready = sem("p_ready")
        comb_ready = sem("comb_ready")
        tr_ready = sem("tr_ready")
        pt_copied = [sem(f"pt_copied{i}") for i in range(2)]
        pv_done = sem("pv_done")
        es_in, es_ready = sem("es_in"), sem("es_ready")
        ss_ready = sem("ss_ready")
        ms2_ready, rs2_ready = sem("ms2_ready"), sem("rs2_ready")
        on_ready = sem("on_ready")
        ohi_ready, olo_ready = sem("ohi_ready"), sem("olo_ready")
        merged_to = sem("merged_to")
        lam_ready, lame = sem("lam_ready"), sem("lame")
        mhi_ready, mlo_ready = sem("mhi_ready"), sem("mlo_ready")
        rw_in, h2_out = sem("rw_in"), [sem("h2_out0"), sem("h2_out1")]
        logits_ready, score_ready = sem("logits_ready"), sem("score_ready")
        sel_ready, rank_ready, dest_ready = sem("sel_ready"), sem("rank_ready"), sem("dest_ready")
        htr_ready, htr_copied = sem("htr_ready"), [sem(f"htr_copied{i}") for i in range(2)]
        shi_ready = sem("shi_ready")
        slo_ready = sem("slo_ready")
        slot_init, slot_out, slots_in = sem("slot_init"), sem("slot_out"), sem("slots_in")
        cnt_ready, cnt_read = sem("cnt_ready"), sem("cnt_read")
        o_wfree = sem("o_wfree")
        o_list, cmp_ready = sem("o_list"), sem("cmp_ready")
        settled = sem("settled")
        ew_in = [sem(f"ew_in{i}") for i in range(4)]
        xg_in = [sem(f"xg_in{i}") for i in range(4)]
        y_out = [sem(f"y_out{i}") for i in range(4)]
        xt_ready = sem("xt_ready")
        xt_copA, xt_copD = sem("xt_copA"), sem("xt_copD")
        gu_ready = sem("gu_ready")
        silu_done, act_done = sem("silu_done"), sem("act_done")
        ahi_ready, alo_ready = sem("ahi_ready"), sem("alo_ready")
        dhi_ready, dlo_ready = sem("dhi_ready"), sem("dlo_ready")
        dn_ready = sem("dn_ready")
        yA, yD = sem("yA"), sem("yD")
        o_load, o_turn, o_gat, o_put = sem("o_load"), sem("o_turn"), sem("o_gat"), sem("o_put")
        o_xt, o_xcA, o_xcD, o_gu, o_sil, o_act, o_dn, o_yA, o_yD = (
            sem("o_xt"), sem("o_xcA"), sem("o_xcD"), sem("o_gu"), sem("o_sil"), sem("o_act"), sem("o_dn"),
            sem("o_yA"), sem("o_yD"))
        yt_in = [sem("yt_in0"), sem("yt_in1")]
        ysum, ytr, yadd = sem("ysum"), sem("ytr"), [sem("yadd0"), sem("yadd1")]
        per_layer = range(min(s.num for s in sems.values()), max(s.num for s in sems.values()) + 1)
        assert len(per_layer) == len(sems)
        init_w = [ctx.enter_context(nc.semaphore(f"init_w{i}")) for i in range(4)]
        init_in, init_v, init_a, init_m, init_out, init_c = (ctx.enter_context(nc.semaphore(n)) for n in
                                                     ("init_in", "init_v", "init_a", "init_m", "init_out", "init_c"))

        ident = cst[:, K_ID:K_ID + P]
        prot = cst[NOPE:DQ, K_PROT:K_PROT + ROPE]
        R = slice(NOPE, DQ)

        with nc.Block() as block:
            @block.sync
            def _(sp):
                sp.dma_start(xT[:], xT_d).then_inc(init_in, 16)
                sp.dma_start(cst[:], const_d).then_inc(init_in, 16)
                sp.dma_start(gvec[:], gvec_d).then_inc(init_in, 16)
                sp.dma_start(cb[:], cb_d).then_inc(init_in, 16)
                sp.dma_start(gt[0][0:32, 0:12], t5_d).then_inc(init_in, 16)
                sp.dma_start(merged[0:32, 0:2, :].rearrange("p a b -> p (a b)")[:, 0:VLEN],
                             onehot_d).then_inc(init_in, 16)
                for i in range(4):
                    sp.dma_start(ada0[:, 4 * i:4 * i + 4, :], ada0_d[:, 4 * i:4 * i + 4, :]).then_inc(init_w[i], 16)
                sp.wait_ge(init_v, 4)
                v = vB[0:12, 1:3, :].rearrange("p a b -> p (a b)")[:, 0:VLEN]
                sp.dma_start(v_d, v.unsqueeze(1).broadcast_to([12, P, VLEN])).then_inc(init_out, 16)

            @block.gpsimd
            def _(pool):
                nc.gpsimd.memset(ones[:], 1.0)
                nc.gpsimd.memset(mhalf[:], -0.5)
                nc.gpsimd.memset(zero[:], 0.0)
                for t in tab + tabD:
                    nc.gpsimd.memset(t[:], NEG)

            @block.scalar
            def _(act):
                act.wait_ge(init_in, 96)
                nc.scalar.activation(ctmp[:, 0, :], cb[:], ACT.Exp, scale=-1.0).then_inc(init_a, 1)

            @block.vector
            def _(dve):
                dve.wait_ge(init_a, 1)
                nc.vector.tensor_scalar_add(ctmp[:, 0, :], ctmp[:, 0, :], 1.0).then_inc(init_v, 1)
                dve.wait_ge(init_v, 1)
                nc.vector.reciprocal(ctmp[:, 1, :], ctmp[:, 0, :]).then_inc(init_v, 1)
                dve.wait_ge(init_v, 2)
                nc.vector.tensor_tensor(cb[:], cb[:], ctmp[:, 1, :], ALU.mult).then_inc(init_c, 1)
                dve.wait_ge(init_m, 1)
                v = vB[0:12, 1:3, :].rearrange("p a b -> p (a b)")
                nc.vector.tensor_copy(v[:, 0:S], G[0][0:12, :]).then_inc(init_v, 1)
                nc.vector.tensor_copy(v[:, S:VLEN], G[1][0:12, 0:VLEN - S]).then_inc(init_v, 1)
                dve.wait_ge(init_c, 1)
                for i in range(16):
                    if i % 4 == 0:
                        dve.wait_ge(init_w[i // 4], 16)
                    nc.vector.tensor_tensor_reduce(out=ada0[:, i, :], in0=ada0[:, i, :], in1=cb[:], scale=1.0,
                                                   scalar=gvec[:, 8 + i:9 + i], op0=ALU.mult, op1=ALU.add,
                                                   accum_out=mod[:, i:i + 1])

            @block.tensor
            def _(pe):
                pe.wait_ge(init_in, 96)
                oh = merged[0:32, 0:2, :].rearrange("p a b -> p (a b)")
                nc.tensor.matmul(G[0][0:12, :], gt[0][0:32, 0:12], oh[:, 0:S], start=True, stop=True)
                nc.tensor.matmul(G[1][0:12, 0:VLEN - S], gt[0][0:32, 0:12], oh[:, S:VLEN], start=True,
                                 stop=True).then_inc(init_m, 1)
        nc.all_engine_barrier()

        jobs = make_jobs()
        mix_jobs = [j for ph in ORDER[:-1] for j in jobs[ph]]
        all_jobs = mix_jobs + jobs["shared"]
        for j in all_jobs:
            j.tiles = [TILES.index(t) for t in j.tiles]
            j.after = [TILES.index(t) for t in j.after]
        ada_no = {u: i for i, u in enumerate(u for u, t in enumerate(TILES) if t[0] == "ada")}
        split_no, n = {}, 0
        for u, t in enumerate(TILES):
            if t[0] != "ada":
                split_no[u] = n
                n += 1
        split_at = {}
        for u in split_no:
            before = max((v for v in split_no if v < u), default=None)
            if before is not None:
                assert before >= u - RAW
                split_at[before] = u
        last_use = {}
        for c, j in enumerate(all_jobs):
            j.c = c
            for u in j.tiles:
                last_use[u] = c
        tile_mark, chunk_mark, n = {}, {}, 0
        for c, j in enumerate(all_jobs):
            for u in j.tiles[:-1]:
                if last_use[u] == c:
                    n += 1
                    tile_mark[u] = n
            n += 1
            chunk_mark[c] = n
            if j.tiles and last_use[j.tiles[-1]] == c:
                tile_mark[j.tiles[-1]] = n
        first_of_out = {}
        for j in all_jobs:
            first_of_out.setdefault((j.out, j.arg), j.c)

        def wait_chunk_out(eng, c):
            eng.wait_ge(chunk_out[c % 2], c // 2 + 1)

        def wait_out_of(eng, name, arg=0):
            wait_chunk_out(eng, first_of_out[(name, arg)])

        def wait_tile_used(eng, u):
            eng.wait_ge(mark, tile_mark[u])

        m_use = {}
        for key in ([("st", n) for n in ("x",)] + [("rb", "x"), ("st", "cq"), ("rb", "cq"), ("st", "ckv"), ("rb", "ckv"), ("kr", 0)]
                    + [("qr", h) for h in range(HA)] + [("ot", o) for o in range(16)] + [("st", "x2"), ("rb", "x2")]):
            m_use[key] = len(m_use)

        m_keys = list(m_use)
        m_full_no = {key: i for i, key in enumerate(k for k in m_keys if k[0] != "st")}

        def wait_mb_free(eng, key):
            if not m_use[key]:
                return
            kind, n = m_keys[m_use[key] - 1]
            if kind == "rb":
                eng.wait_ge(nt_ready, norm_k0[n] + norm_k[n])
            elif kind == "ot":
                eng.wait_ge(olo_ready, n + 1)
            elif kind == "kr":
                eng.wait_ge(m_free, 1)
            elif kind == "qr":
                eng.wait_ge(m_free, n + 2)

        def wait_mb_full(eng, key):
            eng.wait_ge(m_full, m_full_no[key] + 1)

        norm_no = {"x": 0, "cq": 1, "ckv": 2, "x2": 3}
        norm_k = {"x": KD, "cq": 2, "ckv": 1, "x2": KD}
        norm_k0 = {"x": 0, "cq": KD, "ckv": KD + 2, "x2": KD + 3}

        def load_tile(sp, l, u):
            if u >= RAW:
                v = u - RAW
                if v in split_no:
                    sp.wait_ge(hi_done, split_no[v] + 1)
                    sp.wait_ge(lo_done, split_no[v] + 1)
                else:
                    sp.wait_ge(ada_done, ada_no[v] + 1)
            sp.dma_start(raw[u % RAW][:], wmix_d[l * NTILES + u]).then_inc(tile_in[u % RAW], 16)

        def wait_tile_in(eng, u):
            eng.wait_ge(tile_in[u % RAW], 16 * (u // RAW + 1))

        def split_hi(act, u):
            if u not in split_no:
                return
            q = split_no[u]
            wait_tile_in(act, u)
            if q >= SPLIT:
                wait_tile_used(act, [v for v in split_no if split_no[v] == q - SPLIT][0])
            nc.scalar.activation(w_hi[q % SPLIT][:], raw[u % RAW][:], ACT.Copy).then_inc(hi_done, 1)

        def split_lo(dve, u):
            if u not in split_no:
                return
            q = split_no[u]
            dve.wait_ge(hi_done, q + 1)
            nc.vector.tensor_tensor(w_lo[q % SPLIT][:], raw[u % RAW][:], w_hi[q % SPLIT][:].bitcast(F32),
                                    ALU.subtract).then_inc(lo_done, 1)

        acts = {"h": (h_hi, h_lo), "cq": (cq_hi, cq_lo), "ckv": (ckv_hi, ckv_lo), "m": (h_hi, h_lo),
                "s": (s_hi, s_lo), "o": (o_hi, o_lo), "o2": (o2_hi, o2_lo)}

        made = {}

        def products(j):
            if j.c not in made:
                made[j.c] = make_products(j)
            return made[j.c]

        def make_products(j):
            act = "o2" if j.act == "o" and j.arg // KD == 3 else j.act
            bank = G[j.c % 2]
            out = []
            if j.kind == "turn":
                return [(None, 0, None, gt[j.arg % 2][:, t * P:(t + 1) * P], bank[:, t * P:(t + 1) * P], True, True)
                        for t in range(TC)]
            u = j.tiles[0]
            q = split_no[u] % SPLIT
            wide = {KD: P, 4: 2 * P, 2: 384 if j.act == "cq" else S, 1: 1024}[j.k]
            W = [w[q][:, 0:j.k * wide].rearrange("p (k c) -> p k c", k=j.k) for w in (w_hi, w_lo)]
            A = acts[act]
            parts = ((0, 0), (0, 1), (1, 0))
            last = (j.k - 1, 2)
            if j.kind == "T":
                for k in range(j.k):
                    for i, (w, a) in enumerate(parts):
                        lhs = W[w][:, k, j.col:j.col + j.m]
                        out.append((u, k, lhs, A[a][:, k, :], bank[0:j.m, :], (k, i) == (0, 0), (k, i) == last))
            elif j.kind == "VA":
                for i, (w, a) in enumerate(parts):
                    wv = W[w][:, 0, :].rearrange("p (h c) -> p h c", h=HA)[:, :, NOPE:]
                    out.append((u, 0, A[a][:, 0, j.arg * P:(j.arg + 1) * P], wv, bank[:].rearrange("p (h c) -> p h c", h=HA),
                                i == 0, i == 2))
            return out

        def pe_products(pe, j, i0, i1):
            todo = products(j)
            for i in range(i0, min(i1, len(todo))):
                u, k, lhs, rhs, out, start, stop = todo[i]
                if i == 0:
                    if j.c >= 2:
                        wait_chunk_out(pe, j.c - 2)
                    if j.act == "cq" or j.act == "ckv":
                        pe.wait_ge(nlo_ready, norm_k0[j.act] + norm_k[j.act])
                    if j.act == "o":
                        pe.wait_ge(olo_ready, 4 * (j.arg // KD) + 4)
                    if j.act == "s":
                        pe.wait_ge(slo_ready, 2)
                if j.act == "h" and (j.out in ("cq", "sg")) and i % 3 == 0:
                    pe.wait_ge(nlo_ready, norm_k0["x2" if j.out == "sg" else "x"] + k + 1)
                if j.act == "m" and j.arg == 0 and i % 3 == 0:
                    pe.wait_ge(mlo_ready, k + 1)
                if i == 0 or todo[i - 1][0] != u:
                    if j.kind == "turn":
                        wait_out_of(pe, "vt", {"vB": 0, "vC": 4, "vD": 8}[j.out] + j.arg)
                    else:
                        pe.wait_ge(lo_done, split_no[u] + 1)
                if j.kind == "turn":
                    ins = nc.tensor.transpose(out, rhs, ident)
                else:
                    ins = nc.tensor.matmul(out, lhs, rhs, start=start, stop=stop)
                if i == len(todo) - 1 or (todo[i + 1][0] != u and last_use[u] == j.c):
                    ins.then_inc(mark, 1)

        def n_products(j):
            return len(products(j))

        def wait_chunk_full(eng, c):
            eng.wait_ge(mark, chunk_mark[c])

        def act_out(act, j):
            b = G[j.c % 2]
            done = chunk_out[j.c % 2]
            if j.out not in ("cq", "ckv", "kA", "qA", "qB", "kB", "qC", "kC", "qD", "kD", "gate", "sg", "vt"):
                return
            if j.out == "gate" and j.arg >= 2:
                if j.arg - 2 < KD:
                    wait_out_of(act, "branch", j.arg - 2)
                else:
                    act.wait_ge(merged_to, j.arg - 2 - KD + 1)
            wait_chunk_full(act, j.c)
            if j.out == "cq":
                nc.scalar.activation(cqf[:, j.arg, :], b[:], ACT.Copy).then_inc(done, 1)
            elif j.out == "ckv":
                nc.scalar.activation(ckvf[:, 0, :], b[:], ACT.Copy).then_inc(done, 1)
            elif j.out == "kA":
                nc.scalar.activation(kA[0:NOPE, j.arg, :], b[0:NOPE, :], ACT.Copy).then_inc(done, 1)
            elif j.out == "qA":
                nc.scalar.activation(qA[0:DQ, j.arg, :], b[0:DQ, :], ACT.Copy, scale=float(DQ) ** -0.5).then_inc(done, 1)
            elif j.out in ("qB", "qC", "qD"):
                q = {"qB": qB, "qC": qC, "qD": qD}[j.out]
                nc.scalar.activation(q[:, j.arg, :], b[:], ACT.Copy, scale=0.125).then_inc(done, 1)
            elif j.out == "kD":
                for head in range(2):
                    for half in range(2):
                        ins = nc.scalar.activation(kD[64 * half:64 * half + 64, head, :],
                                                   b[64 * head:64 * head + 64, :], ACT.Copy)
                ins.then_inc(done, 1)
            elif j.out == "vt":
                if j.arg % 4 >= 2:
                    wait_chunk_full(act, first_of_out[("vB" if j.arg < 4 else "vC", j.arg % 4 - 2)])
                if j.arg == 8:
                    act.wait_ge(merged_to, KD)
                nc.scalar.activation(gt[j.arg % 2][:], b[:], ACT.Copy).then_inc(done, 1)
            elif j.out in ("kB", "kC"):
                k = {"kB": kB, "kC": kC}[j.out]
                nc.scalar.activation(k[:, j.arg, :], b[:], ACT.Copy).then_inc(done, 1)
            elif j.out == "gate":
                nc.scalar.activation(gt[j.arg % 2][:], b[:], ACT.Tanh, scale=0.5).then_inc(done, 1)
            elif j.out == "sg":
                if j.arg:
                    act.wait_ge(slo_ready, j.arg)
                nc.scalar.activation(sgt[:], b[:], ACT.Silu).then_inc(done, 1)

        chain = [0]

        def link(dve, ins):
            chain[0] += 1
            ins.then_inc(dchain, 1)
            dve.wait_ge(dchain, chain[0])

        def dve_out(dve, j):
            b = G[j.c % 2]
            done = chunk_out[j.c % 2]
            if j.out not in ("krope", "vA", "vB", "vC", "vD", "branch", "x", "su", "ys"):
                return
            wait_chunk_full(dve, j.c)
            if j.out == "krope":
                nc.vector.tensor_copy(qraw[R, :], b[R, :]).then_inc(done, 1)
            elif j.out == "vA":
                nc.vector.tensor_copy(vA[:, j.arg, :], b[:]).then_inc(done, 1)
            elif j.out in ("vB", "vC"):
                v = {"vB": vB, "vC": vC}[j.out]
                nc.vector.tensor_copy(v[:, :, j.arg * P:(j.arg + 1) * P],
                                      b[:].rearrange("p (t c) -> p t c", t=TC)).then_inc(done, 1)
            elif j.out == "vD":
                nc.vector.tensor_copy(vD[:], b[:].rearrange("p (t c) -> p t c", t=TC)).then_inc(done, 1)
            elif j.out == "branch":
                m = j.arg % KD
                wait_out_of(dve, "gate", j.arg)
                dst = merged[:, m, :] if j.arg < KD else gt[j.arg % 2][:]
                nc.vector.scalar_tensor_tensor(dst, gt[j.arg % 2][:], 1.0, b[:], ALU.add, ALU.mult).then_inc(done, 1)
                if j.arg >= KD:
                    wait_chunk_out(dve, j.c)
                    nc.vector.tensor_tensor(merged[:, m, :], merged[:, m, :], gt[j.arg % 2][:], ALU.add
                                            ).then_inc(merged_to, 1)
            elif j.out == "x":
                nc.vector.scalar_tensor_tensor(xT[:, j.arg, :], b[:], mod[:, 16 + j.arg:17 + j.arg], xT[:, j.arg, :],
                                               ALU.mult, ALU.add).then_inc(done, 1)
            elif j.out == "su":
                wait_out_of(dve, "sg", j.arg)
                nc.vector.tensor_tensor(sgt[:], sgt[:], b[:], ALU.mult).then_inc(done, 1)
                wait_chunk_out(dve, j.c)
                dve.wait_ge(shi_ready, j.arg + 1)
                nc.vector.tensor_tensor(s_lo[:, j.arg, :], sgt[:], s_hi[:, j.arg, :].bitcast(F32),
                                        ALU.subtract).then_inc(slo_ready, 1)
            elif j.out == "ys":
                nc.vector.scalar_tensor_tensor(xT[:, j.arg, :], b[:], mod[:, 40 + j.arg:41 + j.arg], xT[:, j.arg, :],
                                               ALU.mult, ALU.add).then_inc(done, 1)

        def act_stream(act, events, end=MIX_TILES):
            for what, v in events:
                if what == "tile":
                    if split_at.get(v, end) < end:
                        split_hi(act, split_at[v])
                elif what == "chunk":
                    j = all_jobs[v]
                    act_out(act, j)
                    if j.out == "su":
                        wait_chunk_out(act, j.c)
                        nc.scalar.activation(s_hi[:, j.arg, :], sgt[:], ACT.Copy).then_inc(shi_ready, 1)

        def dve_stream(dve, events, end=MIX_TILES):
            for what, v in events:
                if what == "tile":
                    if split_at.get(v, end) < end:
                        split_lo(dve, split_at[v])
                elif what == "ada":
                    ada(dve, v)
                else:
                    dve_out(dve, all_jobs[v])

        def ada(dve, u):
            i = TILES[u][1]
            wait_tile_in(dve, u)
            if ada_no[u]:
                dve.wait_ge(ada_done, ada_no[u])
            nc.vector.tensor_tensor_reduce(out=raw[u % RAW][:], in0=raw[u % RAW][:], in1=cb[:], scale=1.0,
                                           scalar=vec[:, V_ADAB + i:V_ADAB + i + 1], op0=ALU.mult, op1=ALU.add,
                                           accum_out=mod[:, i:i + 1]).then_inc(ada_done, 1)

        def spread(js, nslots):
            total = sum(n_products(j) for j in js)
            shares, at = [[] for _ in range(nslots)], 0.0
            for j in js:
                n = n_products(j)
                i = 0
                while i < n:
                    s = min(int(at * nslots / total + 1e-9), nslots - 1)
                    room = max(1, int(math.ceil((s + 1) * total / nslots - at - 1e-9))) if s < nslots - 1 else n
                    i1 = min(n, i + room)
                    shares[s].append((j, i, i1))
                    at += i1 - i
                    i = i1
            return shares

        def events_of(share):
            ev = []
            for j, i0, i1 in share:
                todo = products(j)
                for i in range(i0, i1):
                    u = todo[i][0]
                    if u is not None and (i == 0 or todo[i - 1][0] != u) and all_jobs_first[u] == (j.c, i):
                        ev.append(("tile", u))
                    if i == len(todo) - 1:
                        ev.append(("chunk", j.c))
                        ev += [("ada", u) for u in j.after]
            return ev

        all_jobs_first = {}
        for j in all_jobs:
            for i, t in enumerate(products(j)):
                all_jobs_first.setdefault(t[0], (j.c, i))

        def whole(js):
            return [(j, 0, n_products(j)) for j in js]

        sq_bufs = {"x": sn, "cq": sn, "ckv": sn, "x2": htok, "end": sn}

        def square_buf(name, n):
            return sq_bufs[name][n % 2][:, 0:S]

        def norm_squares(eng, name, src, ready=None):
            for k in range(norm_k[name]):
                n = norm_k0[name] + k
                if n % 2 != (0 if eng.engine == nc.scalar.engine else 1):
                    continue
                if ready:
                    ready(eng, k)
                if n >= 2:
                    eng.wait_ge(sq_used, n - 1)
                if n % 2 == 0:
                    nc.scalar.activation(square_buf(name, n), src[:, k, :], ACT.Square).then_inc(sq_ready[0], 1)
                else:
                    nc.vector.tensor_tensor(square_buf(name, n), src[:, k, :], src[:, k, :], ALU.mult
                                            ).then_inc(sq_ready[1], 1)

        def pe_norm_sums(pe, name):
            wait_mb_free(pe, ("st", name))
            K = norm_k[name]
            for k in range(K):
                n = norm_k0[name] + k
                pe.wait_ge(sq_ready[n % 2], n // 2 + 1)
                for t in range(TC):
                    ins = nc.tensor.matmul(MB[:, t:t + 1], square_buf(name, n)[:, t * P:(t + 1) * P], ones[:, 0:1],
                                           start=(k == 0 and t == 0), stop=(k == K - 1), skip_group_check=True)
                ins.then_inc(sq_used, 1)

        def dve_norm_mean(dve, name):
            dve.wait_ge(sq_used, norm_k0[name] + norm_k[name])
            nc.vector.tensor_scalar(stat[:, 0:TC], MB[:, 0:TC], 1.0 / (norm_k[name] * P), EPS, ALU.mult,
                                    ALU.add).then_inc(ms_ready, 1)

        def pool_norm_root(pool, name):
            pool.wait_ge(ms_ready, norm_no[name] + 1)
            nc.gpsimd.tensor_tensor(rstd[:, 0:TC], stat[:, 0:TC], mhalf[:, 0:TC], ALU.pow).then_inc(rstd_ready, 1)

        def pe_norm_spread(pe, name):
            pe.wait_ge(rstd_ready, norm_no[name] + 1)
            for t in range(TC):
                ins = nc.tensor.matmul(MB[:, t * P:(t + 1) * P], rstd[:, t:t + 1].broadcast_to([P, P]), ident,
                                       start=True, stop=True)
            ins.then_inc(m_full, 1)

        def dve_norm_apply(dve, name, src, mul, add, hi, lo, tmp):
            K = norm_k[name]
            wait_mb_full(dve, ("rb", name))
            for k in range(K + 1):
                if k < K:
                    n = norm_k0[name] + k
                    if n >= 2 and len(tmp) == 2:
                        dve.wait_ge(nlo_ready, n - 1)
                    nc.vector.scalar_tensor_tensor(tmp[k % len(tmp)], src[:, k, :], mul[:, k:k + 1], MB[:], ALU.mult,
                                                   ALU.mult).then_inc(nt_ready, 1)
                if k >= 1:
                    n = norm_k0[name] + k
                    dve.wait_ge(nhi_ready, n)
                    t, h = tmp[(k - 1) % len(tmp)], hi[:, k - 1, :].bitcast(F32)
                    if add is None or len(tmp) > 2:
                        nc.vector.tensor_tensor(lo[:, k - 1, :], t, h, ALU.subtract).then_inc(nlo_ready, 1)
                    else:
                        nc.vector.scalar_tensor_tensor(lo[:, k - 1, :], t, add[:, k - 1:k], h, ALU.add,
                                                       ALU.subtract).then_inc(nlo_ready, 1)

        def act_norm_apply(act, name, add, hi, tmp):
            for k in range(norm_k[name]):
                n = norm_k0[name] + k
                act.wait_ge(nt_ready, n + 1)
                t = tmp[k % len(tmp)]
                if add is None:
                    nc.scalar.activation(hi[:, k, :], t, ACT.Copy).then_inc(nhi_ready, 1)
                elif len(tmp) == 2:
                    nc.scalar.activation(hi[:, k, :], t, ACT.Identity, bias=add[:, k:k + 1]).then_inc(nhi_ready, 1)
                else:
                    nc.scalar.activation(t, t, ACT.Identity, bias=add[:, k:k + 1]).then_inc(achain, 1)
                    act.wait_ge(achain, k + 1)
                    nc.scalar.activation(hi[:, k, :], t, ACT.Copy).then_inc(nhi_ready, 1)

        Q = {"A": qA, "B": qB, "C": qC, "D": qD}
        K_ = {"A": kA, "B": kB, "C": kC, "D": kD}
        V_ = {"A": vA, "B": vB, "C": vC, "D": vD}

        def score_operands(mp):
            q0 = mp.qb * P
            if mp.br == "A":
                rows, qc, kc = slice(0, DQ), mp.head, mp.head
            elif mp.br == "C":
                rows, qc, kc = slice(64 * mp.t, 64 * mp.t + 64), mp.head, mp.head
            else:
                rows, qc = slice(64 * (mp.head % 2), 64 * (mp.head % 2) + 64), mp.head // 2
                kc = mp.head // 4 if mp.br == "D" else qc
            return Q[mp.br][rows, qc, q0:q0 + P], K_[mp.br][rows, kc, mp.k0:mp.k0 + mp.nk]

        def pe_scores(pe, br, u):
            mp = MAPS[br][u - MAP0[br]]
            if u == MAP0[br]:
                last = {"A": ("qA", HA - 1), "B": ("vB", 3), "C": ("vC", 3), "D": ("vD", 0)}[br]
                c = first_of_out[last]
                wait_chunk_out(pe, c)
                wait_chunk_out(pe, c - 1)
                if br == "A":
                    pe.wait_ge(kr_copied, 1)
                    pe.wait_ge(kr_ready, 1)
            if br == "A" and mp.qb == 0:
                pe.wait_ge(rot_ready, mp.head + 1)
            if u >= 2:
                pe.wait_ge(sn_ready, u - 1)
            q, k = score_operands(mp)
            nc.tensor.matmul(SB[u % 2][:, 0:mp.nk], q, k, start=True, stop=True).then_inc(sc_ready, 1)

        def dve_bias(dve, br, u):
            mp = MAPS[br][u - MAP0[br]]
            if mp.qb == 0 and mp.t == 0:
                if br in "BC":
                    th = mp.head + (8 if br == "C" else 0)
                    dve.wait_ge(tab_in[th % 2], 32 * (th // 2 + 1))
                elif br == "D":
                    dve.wait_ge(tabD_in[mp.head % 2], 32 * (mp.head // 2 + 1))
            bias = {"A": tabA[:, S - mp.nk:], "B": tab[mp.head % 2][:, S - mp.nk:], "C": tab[mp.head % 2][:, S - mp.nk:],
                    "D": tabD[mp.head % 2][:, 2 * P - mp.nk:]}[br]
            floor = sinkt[:, u - MAP0[br]:u - MAP0[br] + 1] if br == "D" else BIG
            dve.wait_ge(sc_ready, u + 1)
            if u >= 2:
                dve.wait_ge(p_ready, u - 1)
            nc.vector.tensor_tensor_reduce(out=sn[u % 2][:, 0:mp.nk], in0=SB[u % 2][:, 0:mp.nk], in1=bias, scale=-1.0,
                                           scalar=floor, op0=ALU.add, op1=ALU.min,
                                           accum_out=negmax[:, u:u + 1]).then_inc(sn_ready, 1)

        def act_exp(act, br, u):
            mp = MAPS[br][u - MAP0[br]]
            act.wait_ge(sn_ready, u + 1)
            if u >= 4:
                act.wait_ge(tr_ready, map_group(u - 4) + 1)
            nc.scalar.activation(pr[u % 4][:, 0:mp.nk], sn[u % 2][:, 0:mp.nk], ACT.Exp, bias=negmax[:, u:u + 1],
                                 scale=-1.0, accum_out=psum_of[:, u:u + 1]).then_inc(p_ready, 1)

        def dve_combine(dve, g):
            u0, u1 = group_maps(g)
            nk = MAPS["C"][u0 - MAP0["C"]].nk
            dve.wait_ge(p_ready, u1 + 1)
            if g > GROUP0["C"]:
                dve.wait_ge(comb_ready, g - GROUP0["C"])
            link(dve, nc.vector.reciprocal(rcp[:, 8:10], psum_of[:, u0:u1 + 1]))
            link(dve, nc.vector.tensor_tensor(rcp[:, 10:11], rcp[:, 9:10], lamt[:, 5:6], ALU.mult))
            link(dve, nc.vector.tensor_scalar(pr[u1 % 4][:, 0:nk], pr[u1 % 4][:, 0:nk], rcp[:, 10:11], None, ALU.mult))
            nc.vector.scalar_tensor_tensor(pr[u0 % 4][:, 0:nk], pr[u0 % 4][:, 0:nk], rcp[:, 8:9], pr[u1 % 4][:, 0:nk],
                                           ALU.mult, ALU.add).then_inc(comb_ready, 1)

        def pe_transpose_probs(pe, br, g):
            u = group_maps(g)[0]
            mp = MAPS[br][u - MAP0[br]]
            if br == "C":
                pe.wait_ge(comb_ready, g - GROUP0["C"] + 1)
            else:
                pe.wait_ge(p_ready, u + 1)
            if g >= 2:
                pe.wait_ge(pt_copied[g % 2], g // 2)
            for b in range(mp.nk // P):
                ins = nc.tensor.transpose(TB[g % 2][:, b * P:(b + 1) * P], pr[u % 4][:, b * P:(b + 1) * P], ident)
            ins.then_inc(tr_ready, 1)

        def copy_probs(eng, g):
            u = group_maps(g)[0]
            br = "A" if g < 32 else "B" if g < 64 else "C" if g < 80 else "D"
            nk = MAPS[br][u - MAP0[br]].nk
            eng.wait_ge(tr_ready, g + 1)
            if g >= 2:
                eng.wait_ge(pv_done, g - 1)
            if g % 2 == 0:
                nc.scalar.activation(pt[0][:, 0:nk], TB[0][:, 0:nk], ACT.Copy).then_inc(pt_copied[0], 1)
            else:
                nc.vector.tensor_copy(pt[1][:, 0:nk], TB[1][:, 0:nk]).then_inc(pt_copied[1], 1)

        def pe_values(pe, br, g):
            u = group_maps(g)[0]
            mp = MAPS[br][u - MAP0[br]]
            i = g - GROUP0[br]
            o = SET0[br] + i // PER_SET[br]
            if i % PER_SET[br] == 0 and o:
                pe.wait_ge(on_ready, o)
            pe.wait_ge(pt_copied[g % 2], g // 2 + 1)
            w = 2 * DH if br == "C" else DH
            col = i % PER_SET[br] * w
            head = mp.head // 4 if br == "D" else mp.head
            nb = mp.nk // P
            for b in range(nb):
                ins = nc.tensor.matmul(OB[:, col:col + w], pt[g % 2][:, b * P:(b + 1) * P],
                                       V_[br][:, mp.k0 // P + b, head * w:(head + 1) * w], start=b == 0, stop=b == nb - 1)
            ins.then_inc(pv_done, 1)

        def set_end(br, g):
            i = g - GROUP0[br]
            return SET0[br] + i // PER_SET[br] if i >= 0 and i % PER_SET[br] == PER_SET[br] - 1 else None

        def set_maps(o):
            br = "ABCD"[o // 4]
            n = len(MAPS[br]) // 4
            return MAP0[br] + (o % 4) * n, n

        def dve_norm_set(dve, o):
            br = "ABCD"[o // 4]
            u0, n = set_maps(o)
            if br == "D":
                dve.wait_ge(p_ready, u0 + n)
                nc.vector.tensor_tensor(sinkt[:, 32:40], negmax[:, u0:u0 + n],
                                        vec[:, V_SINK + u0 - 96:V_SINK + u0 - 96 + n], ALU.add).then_inc(es_in, 1)
                dve.wait_ge(es_ready, o - 11)
                link(dve, nc.vector.tensor_tensor(psum_of[:, u0:u0 + n], psum_of[:, u0:u0 + n], sinkt[:, 40:48], ALU.add))
            if br == "C":
                dve.wait_ge(ss_ready, o - 7)
                nc.vector.tensor_scalar(stat[:, 4:8], rcp[:, 12:16], 1.0 / P, EPS, ALU.mult, ALU.add).then_inc(ms2_ready, 1)
                dve.wait_ge(rs2_ready, o - 7)
            else:
                dve.wait_ge(pv_done, GROUP0[br] + (o % 4 + 1) * PER_SET[br])
                if o:
                    dve.wait_ge(on_ready, o)
                link(dve, nc.vector.reciprocal(rcp[:, 0:8], psum_of[:, u0:u0 + n]))
            if o:
                wait_mb_full(dve, ("ot", o - 1))
            if br == "C":
                nc.vector.tensor_tensor(on[:], OB[:].rearrange("p (q c) -> p q c", q=TC),
                                        rstd[:, 4:8].unsqueeze(2).broadcast_to([P, TC, P]), ALU.mult).then_inc(on_ready, 1)
            else:
                nc.vector.tensor_tensor(on[:].rearrange("p q (h c) -> p h q c", h=2),
                                        OB[:].rearrange("p (h q c) -> p h q c", h=2, q=TC),
                                        rcp[:, 0:8].rearrange("p (h q) -> p h q", h=2).unsqueeze(3).broadcast_to(
                                            [P, 2, TC, DH]), ALU.mult).then_inc(on_ready, 1)

        def act_norm_set(act, o):
            br = "ABCD"[o // 4]
            if br == "C":
                act.wait_ge(pv_done, GROUP0[br] + (o % 4 + 1) * PER_SET[br])
                if o > 8:
                    act.wait_ge(ms2_ready, o - 8)
                wait_mb_full(act, ("ot", o - 1))
                for q in range(TC):
                    ins = nc.scalar.activation(on[:, q, :], OB[:, q * P:(q + 1) * P], ACT.Square,
                                               accum_out=rcp[:, 12 + q:13 + q])
                ins.then_inc(ss_ready, 1)
            if br == "D":
                act.wait_ge(es_in, o - 11)
                nc.scalar.activation(sinkt[:, 40:48], sinkt[:, 32:40], ACT.Exp).then_inc(es_ready, 1)

        def pe_transpose_set(pe, o):
            pe.wait_ge(on_ready, o + 1)
            wait_mb_free(pe, ("ot", o))
            for q in range(TC):
                ins = nc.tensor.transpose(MB[:, q * P:(q + 1) * P], on[:, q, :], ident)
            ins.then_inc(m_full, 1)

        def act_set_hi(act, o):
            br = "ABCD"[o // 4]
            wait_mb_full(act, ("ot", o))
            if br in "BC" and o % 4 == 0:
                wait_chunk_full(act, jobs["gb" + "ABCD"[o // 4 - 1]][-1].c)
            dst = (o2_hi if br == "D" else o_hi)[:, o % 4, :]
            if br == "C":
                nc.scalar.activation(dst, MB[:], ACT.Copy, scale=lamt[:, 6:7]).then_inc(ohi_ready, 1)
            else:
                nc.scalar.activation(dst, MB[:], ACT.Copy).then_inc(ohi_ready, 1)

        def dve_set_lo(dve, o):
            br = "ABCD"[o // 4]
            dve.wait_ge(ohi_ready, o + 1)
            hi, lo = ((o2_hi, o2_lo) if br == "D" else (o_hi, o_lo))
            if br == "C":
                nc.vector.scalar_tensor_tensor(lo[:, o % 4, :], MB[:], lamt[:, 6:7], hi[:, o % 4, :].bitcast(F32),
                                               ALU.mult, ALU.subtract).then_inc(olo_ready, 1)
            else:
                nc.vector.tensor_tensor(lo[:, o % 4, :], MB[:], hi[:, o % 4, :].bitcast(F32),
                                        ALU.subtract).then_inc(olo_ready, 1)

        shares = {br: spread(jobs[FILL[br]], NGROUP[br] + 1) for br in "ABCD"}

        def pe_attention(pe, br):
            g0, n = GROUP0[br], NGROUP[br]
            for u in group_maps(g0):
                pe_scores(pe, br, u)
            for s in range(n + 2):
                g = g0 + s
                if s + 1 < n:
                    for u in group_maps(g + 1):
                        pe_scores(pe, br, u)
                if s <= n:
                    for j, i0, i1 in shares[br][s]:
                        pe_products(pe, j, i0, i1)
                if s >= 2 and set_end(br, g - 2) is not None:
                    pe_transpose_set(pe, set_end(br, g - 2))
                if s < n:
                    pe_transpose_probs(pe, br, g)
                if 1 <= s <= n:
                    pe_values(pe, br, g - 1)

        def act_attention(act, br):
            g0, n = GROUP0[br], NGROUP[br]
            for u in group_maps(g0):
                act_exp(act, br, u)
            for s in range(n + 2):
                g = g0 + s
                if s + 1 < n:
                    for u in group_maps(g + 1):
                        act_exp(act, br, u)
                if s <= n:
                    act_stream(act, events_of(shares[br][s]))
                if s >= 2 and set_end(br, g - 2) is not None:
                    act_set_hi(act, set_end(br, g - 2))
                if s < n and g % 2 == 0:
                    copy_probs(act, g)
                if 1 <= s <= n and set_end(br, g - 1) is not None:
                    act_norm_set(act, set_end(br, g - 1))

        def dve_attention(dve, br):
            g0, n = GROUP0[br], NGROUP[br]
            for u in group_maps(g0):
                dve_bias(dve, br, u)
            for s in range(n + 2):
                g = g0 + s
                if s < n and br == "C":
                    dve_combine(dve, g)
                if s + 1 < n:
                    for u in group_maps(g + 1):
                        dve_bias(dve, br, u)
                if s <= n:
                    dve_stream(dve, events_of(shares[br][s]))
                if s >= 2 and set_end(br, g - 2) is not None:
                    dve_set_lo(dve, set_end(br, g - 2))
                if s < n and g % 2 == 1:
                    copy_probs(dve, g)
                if 1 <= s <= n and set_end(br, g - 1) is not None:
                    dve_norm_set(dve, set_end(br, g - 1))

        with nc.Fori(0, L) as l:
            with nc.Block() as block:
                @block.sync
                def _(sp):
                    sp.dma_start(vec[:], vec_d[l, :, 0:NVEC]).then_inc(vecs_in, 16)
                    sp.dma_start(lamv[:], vec_d[l, :, V_LAM:V_LAM + 256]).then_inc(vecs_in, 16)
                    for u in range(RAW):
                        load_tile(sp, l, u)
                    sp.wait_ge(init_out, 16)
                    sp.dma_start(rope_t[R, :, :], rope_d).then_inc(rope_in, 16)
                    for u in range(RAW, MIX_TILES):
                        load_tile(sp, l, u)

                @block.gpsimd
                def _(pool):
                    def load_table(th):
                        slot = tab[th % 2]
                        if th >= 2:
                            h = th - 2
                            pool.wait_ge(sn_ready, MAP0["B"] + 4 * h + 4 if h < 8 else MAP0["C"] + 8 * (h - 8) + 8)
                        for rows, nk in ((slice(0, 64), S - 64), (slice(64, P), S)):
                            if th < 8:
                                src = vb_d[l, th, rows, 0:nk]
                            else:
                                src = bass.AP(v_d.tensor, (th - 8) * P * VLEN + rows.start * (VLEN - 1) + 127,
                                              [[VLEN - 1, 64], [1, nk]])
                            pool.dma_start(slot[rows, 0:nk], src).then_inc(tab_in[th % 2], 16)

                    def load_window_table(h):
                        slot = tabD[h % 2]
                        if h >= 2:
                            pool.wait_ge(sn_ready, MAP0["D"] + 4 * (h - 2) + 4)
                        for half in range(2):
                            pool.dma_start(slot[64 * half:64 * half + 64, 64 + 64 * half:192 + 64 * half],
                                           bass.AP(v_d.tensor, (4 + h) * P * VLEN + 64 * half * VLEN + 447,
                                                   [[VLEN - 1, 64], [1, P]])
                                           ).then_inc(tabD_in[h % 2], 16)

                    nc.gpsimd.memset(tabA[:], 0.0).then_inc(pchain, 1)
                    pool.wait_ge(pchain, 1)
                    nc.gpsimd.memset(tabA[0:64, S - 64:S], NEG).then_inc(tabA_ready, 1)
                    pool_norm_root(pool, "x")
                    load_table(0)
                    load_table(1)
                    pool.wait_ge(init_out, 16)
                    load_window_table(0)
                    load_window_table(1)
                    pool_norm_root(pool, "cq")
                    pool_norm_root(pool, "ckv")
                    pool.wait_ge(kr_ready, 1)
                    nc.gpsimd.tensor_copy(kA[R, 1:HA, :], kA[R, 0:1, :].broadcast_to([ROPE, HA - 1, S])).then_inc(kr_copied, 1)
                    for th in range(2, 10):
                        load_table(th)
                    for h in range(4):
                        pool.wait_ge(ms2_ready, h + 1)
                        nc.gpsimd.tensor_tensor(rstd[:, 4:8], stat[:, 4:8], mhalf[:, 4:8], ALU.pow).then_inc(rs2_ready, 1)
                        if h < 2:
                            load_table(10 + h)
                    for h in range(2, 8):
                        load_window_table(h)
                    for i in range(2):
                        pool.wait_ge(tab_in[i], 32 * 6)
                        pool.wait_ge(tabD_in[i], 32 * 4)

                @block.scalar
                def _(act):
                    norm_squares(act, "x", xT)
                    act.wait_ge(lam_ready, 2)
                    nc.scalar.activation(lamt[:, 2:4], lamt[:, 0:2], ACT.Exp).then_inc(lame, 1)
                    split_hi(act, 0)
                    act_norm_apply(act, "x", mod[:, 0:KD], h_hi, [pr[0][:], pr[1][:]])
                    act_stream(act, events_of(whole(jobs["projA"])))
                    norm_squares(act, "cq", cqf, ready=lambda e, k: wait_out_of(e, "cq", k))
                    act_norm_apply(act, "cq", None, cq_hi, [pr[0][:], pr[1][:]])
                    norm_squares(act, "ckv", ckvf, ready=lambda e, k: wait_out_of(e, "ckv", 0))
                    act_norm_apply(act, "ckv", None, ckv_hi, [pr[0][:], pr[1][:]])
                    act_stream(act, events_of(whole(jobs["upA"])))
                    for i, br in enumerate("ABCD"):
                        act_attention(act, br)
                        if br != "C":
                            act_stream(act, events_of(whole(jobs["gb" + br])))
                    wait_chunk_full(act, jobs["gbD"][-3].c)
                    for k in range(KD):
                        act.wait_ge(merged_to, 2 * KD + k + 1)
                        nc.scalar.activation(h_hi[:, k, :], merged[:, k, :], ACT.Copy).then_inc(mhi_ready, 1)
                    act_stream(act, events_of(whole(jobs["out"])))

                @block.vector
                def _(dve):
                    chain[0] = 0
                    norm_squares(dve, "x", xT)
                    dve.wait_ge(vecs_in, 32)
                    for i in range(2):
                        a = 128 * i
                        ins = nc.vector.tensor_tensor_reduce(out=on[:, i, 0:64], in0=lamv[:, a:a + 64], in1=lamv[:, a + 64:a + 128],
                                                             scale=1.0, scalar=0.0, op0=ALU.mult, op1=ALU.add,
                                                             accum_out=lamt[:, i:i + 1]).then_inc(lam_ready, 1)
                    nc.vector.tensor_tensor(lamt[:, 6:7], vec[:, V_SUB:V_SUB + 1], vec[:, V_OML:V_OML + 1], ALU.mult)
                    nc.vector.tensor_scalar(sinkt[:, 0:32], vec[:, V_SINK:V_SINK + 32], -1.0, None, ALU.mult)
                    dve.wait_ge(lame, 1)
                    link(dve, nc.vector.tensor_tensor(lamt[:, 4:5], lamt[:, 3:4], lamt[:, 2:3], ALU.subtract))
                    link(dve, nc.vector.tensor_tensor(lamt[:, 5:6], lamt[:, 4:5], vec[:, V_LI:V_LI + 1], ALU.subtract))
                    dve_norm_mean(dve, "x")
                    split_lo(dve, 0)
                    nc.vector.scalar_tensor_tensor(amul[:], mod[:, 8:16], 1.0, vec[:, V_GMIX:V_GMIX + 8], ALU.add,
                                                   ALU.mult).then_inc(amul_ready, 1)
                    dve.wait_ge(amul_ready, 1)
                    dve_norm_apply(dve, "x", xT, amul, mod[:, 0:KD], h_hi, h_lo, [pr[0][:], pr[1][:]])
                    dve_stream(dve, events_of(whole(jobs["projA"])))
                    norm_squares(dve, "cq", cqf, ready=lambda e, k: wait_out_of(e, "cq", k))
                    dve_norm_mean(dve, "cq")
                    dve_norm_apply(dve, "cq", cqf, vec[:, V_GQ:V_GQ + 2], None, cq_hi, cq_lo, [pr[0][:], pr[1][:]])
                    dve_norm_mean(dve, "ckv")
                    dve_norm_apply(dve, "ckv", ckvf, vec[:, V_GKV:V_GKV + 1], None, ckv_hi, ckv_lo, [pr[0][:], pr[1][:]])
                    dve.wait_ge(rope_in, 16)
                    wait_mb_full(dve, ("kr", 0))
                    nc.vector.tensor_tensor(qrot[R, :], MB[R, :], rope_t[R, 1, :], ALU.mult).then_inc(m_free, 1)
                    link(dve, nc.vector.tensor_tensor(qraw[R, :], qraw[R, :], rope_t[R, 0, :], ALU.mult))
                    nc.vector.tensor_tensor(kA[R, 0, :], qraw[R, :], qrot[R, :], ALU.add).then_inc(kr_ready, 1)

                    def rotate(h):
                        wait_mb_full(dve, ("qr", h))
                        if h:
                            dve.wait_ge(rot_ready, h)
                        else:
                            dve.wait_ge(kr_ready, 1)
                        nc.vector.tensor_tensor(qrot[R, :], MB[R, :], rope_t[R, 1, :], ALU.mult).then_inc(m_free, 1)
                        link(dve, nc.vector.tensor_tensor(qraw[R, :], qA[R, h, :], rope_t[R, 0, :], ALU.mult))
                        nc.vector.tensor_tensor(qA[R, h, :], qraw[R, :], qrot[R, :], ALU.add).then_inc(rot_ready, 1)

                    for j in jobs["upA"]:
                        dve_stream(dve, events_of([(j, 0, n_products(j))]))
                        if j.out == "qA" and j.arg:
                            rotate(j.arg - 1)
                    rotate(HA - 1)
                    dve.wait_ge(tabA_ready, 1)
                    for i, br in enumerate("ABCD"):
                        dve_attention(dve, br)
                        if br != "C":
                            dve_stream(dve, events_of(whole(jobs["gb" + br])))
                        if br == "C":
                            dve.wait_ge(ada_done, 8)
                            link(dve, nc.vector.tensor_scalar(mod[:, 16:24], mod[:, 16:24], 0.5, None, ALU.mult))
                    for k in range(KD):
                        dve.wait_ge(mhi_ready, k + 1)
                        nc.vector.tensor_tensor(h_lo[:, k, :], merged[:, k, :], h_hi[:, k, :].bitcast(F32),
                                                ALU.subtract).then_inc(mlo_ready, 1)
                    dve_stream(dve, events_of(whole(jobs["out"])))

                @block.tensor
                def _(pe):
                    pe_norm_sums(pe, "x")
                    pe_norm_spread(pe, "x")
                    for j in jobs["projA"]:
                        pe_products(pe, j, 0, n_products(j))
                    for name in ("cq", "ckv"):
                        pe_norm_sums(pe, name)
                        pe_norm_spread(pe, name)
                    wait_out_of(pe, "krope")
                    wait_mb_free(pe, ("kr", 0))
                    nc.tensor.matmul(MB[R, :], prot, qraw[R, :], start=True, stop=True).then_inc(m_full, 1)

                    def rotate(h):
                        wait_out_of(pe, "qA", h)
                        wait_mb_free(pe, ("qr", h))
                        nc.tensor.matmul(MB[R, :], prot, qA[R, h, :], start=True, stop=True).then_inc(m_full, 1)

                    for j in jobs["upA"]:
                        pe_products(pe, j, 0, n_products(j))
                        if j.out == "qA" and j.arg:
                            rotate(j.arg - 1)
                    rotate(HA - 1)
                    for br in "ABCD":
                        pe_attention(pe, br)
                        if br != "C":
                            for j in jobs["gb" + br]:
                                pe_products(pe, j, 0, n_products(j))
                    for j in jobs["out"]:
                        pe_products(pe, j, 0, n_products(j))

            shared_mark = chunk_mark[jobs["shared"][-1].c]
            slot_rows = slot_d.rearrange("(s e) w -> s e w", e=NE)

            def blocks(eng):
                eng.wait_ge(cnt_ready, 2)
                return eng.value_load(novf[0:1, 0:1], min_val=0, max_val=MAXOVF)

            def copy_half(eng, e, par):
                eng.wait_ge(xt_ready, e + 1)
                if not (isinstance(e, int) and e < 2):
                    eng.wait_ge(gu_ready, e - 1)
                if eng.engine == nc.scalar.engine:
                    nc.scalar.activation(xgT[par][:, 0:4, :], TB[0][:].rearrange("p (k t) -> p k t", k=4),
                                         ACT.Copy).then_inc(xt_copA, 1)
                else:
                    nc.vector.tensor_copy(xgT[par][:, 4:8, :], TB[1][:].rearrange("p (k t) -> p k t", k=4)
                                          ).then_inc(xt_copD, 1)

            def scale_half(eng, it, j):
                e, s = 8 * it + j, j % 4
                eng.wait_ge(dn_ready, e + 1)
                if not (isinstance(e, int) and e < 4):
                    eng.wait_ge(y_out[s], 16 * (2 * it + j // 4))
                gate = idx[j % 8][:, 2:3].bitcast(F32)
                bank = (SB, (OB, MB))[s % 2]
                if eng.engine == nc.scalar.engine:
                    nc.scalar.activation(y[s][:, 0:S], bank[0][:], ACT.Copy, scale=gate).then_inc(yA, 1)
                else:
                    nc.vector.tensor_scalar(y[s][:, S:D], bank[1][:], gate, None, ALU.mult).then_inc(yD, 1)

            with nc.Block() as block:
                @block.sync
                def _(sp):
                    sp.dma_start(rw[:], rw_d[l]).then_inc(rw_in, 16)
                    sp.dma_start(rcst[:], rcst_d).then_inc(rw_in, 16)
                    sp.dma_start(pay[:], pay_d).then_inc(rw_in, 16)
                    sp.dma_start(slot_d, skip_d).then_inc(slot_init, 16)
                    for u in range(MIX_TILES, MIX_TILES + 3):
                        load_tile(sp, l, u)
                    sp.dma_start(ew[0][:], wexp_d[l * NE]).then_inc(ew_in[0], 16)
                    for u in range(MIX_TILES + 3, NTILES):
                        load_tile(sp, l, u)
                    sp.dma_start(ew[1][:], wexp_d[l * NE + 1]).then_inc(ew_in[1], 16)
                    sp.wait_ge(dest_ready, 1)
                    sp.dma_start(ew[2][:], wexp_d[l * NE + 2]).then_inc(ew_in[2], 16)
                    sp.wait_ge(mark, shared_mark)
                    sp.dma_start(ew[3][:], wexp_d[l * NE + 3]).then_inc(ew_in[3], 16)
                    with sp.Fori(1, NE // 4) as it:
                        for j in range(4):
                            sp.wait_ge(dn_ready, 4 * it + j - 3)
                            sp.dma_start(ew[j][:], wexp_d[l * NE + 4 * it + j]).then_inc(ew_in[j], 16)
                    nb = blocks(sp)
                    sp.wait_ge(dn_ready, NE - 3)
                    sp.sem_inc(o_wfree, 1)
                    sp.sem_inc(o_turn, 1)
                    with sp.If(nb > 0):
                        with sp.Fori(0, nb) as i:
                            e = sp.value_load(ovf[0:1, 0, bass.ds(i, 1)], min_val=0, max_val=NE - 1)
                            row = sp.value_load(ovf[0:1, 1, bass.ds(i, 1)], min_val=0, max_val=S - BLK)
                            sp.wait_ge(o_wfree, i + 1)
                            sp.dma_start(ew[0][:], wexp_d[l * NE + e]).then_inc(o_load, 16)
                            sp.wait_ge(y_out[0], 16 * (NE // 4))
                            sp.wait_ge(o_turn, i + 1)
                            sp.dma_start(idx[0][:].unsqueeze(1), slot_rows[bass.ds(row, BLK), bass.ds(e, 1), :]
                                         ).then_inc(o_load, 16)

                @block.gpsimd
                def _(pool):
                    def step(it, j):
                        if not (isinstance(it, int) and 8 * it + j + 3 >= NE):
                            gather(it, j + 3)
                        if not (isinstance(it, int) and 8 * it + j == 0):
                            scatter(it, j - 1)

                    def gather(it, j):
                        e, s = 8 * it + j, j % 4
                        if not (isinstance(e, int) and e < 8):
                            pool.wait_ge(y_out[s], 16 * (2 * it + j // 4 - 1))
                        if not (isinstance(e, int) and e < 4):
                            pool.wait_ge(xt_ready, e - 3)
                        nc.gpsimd.tensor_copy(idx[j % 8][:], slots[:, e, :]).then_inc(pchain, 1)
                        pool.wait_ge(pchain, 3 + e)
                        pool.sem_inc(settled, 1)

                        def rows(n):
                            nc.gpsimd.indirect_dma_start(
                                out=xg[s][0:n, :], out_offset=None, in_=h2_d,
                                in_offset=bass.IndirectOffsetOnAxis(ap=idx[j % 8][0:n, 0:1].bitcast(U32), axis=0),
                                bounds_check=S - 1, oob_is_err=False).then_inc(xg_in[s], 16)

                        by_count(e, rows)

                    def by_count(e, rows):
                        if isinstance(e, int) and e < 8:
                            rows(BLK)
                            return
                        n = pool.value_load(cntrow[0:1, bass.ds(e, 1)], min_val=0, max_val=S)
                        with pool.If(n > BLK // 2):
                            rows(BLK)
                        with pool.Else():
                            rows(BLK // 2)

                    def scatter(it, j):
                        e, s = 8 * it + j, j % 4
                        pool.wait_ge(yA, e + 1)
                        pool.wait_ge(yD, e + 1)
                        pool.sem_inc(settled, 1)

                        def rows(n):
                            nc.gpsimd.indirect_dma_start(
                                out=y_d,
                                out_offset=bass.IndirectOffsetOnAxis(ap=idx[j % 8][0:n, 1:2].bitcast(U32), axis=0),
                                in_=y[s][0:n, :], in_offset=None, bounds_check=S * TOPK - 1, oob_is_err=False
                            ).then_inc(y_out[s], 16)

                        by_count(e, rows)

                    pool_norm_root(pool, "x2")
                    pool.wait_ge(slot_init, 16)
                    pool.wait_ge(dest_ready, 1)
                    for i in range(NPAIR):
                        nc.gpsimd.indirect_dma_start(
                            out=slot_d, out_offset=bass.IndirectOffsetOnAxis(ap=dest[:, i:i + 1], axis=0),
                            in_=pay[:, i, :], in_offset=None, bounds_check=NE * S - 1, oob_is_err=False
                        ).then_inc(slot_out, 16)
                    pool.wait_ge(mark, shared_mark)
                    for i in range(4):
                        ins = nc.gpsimd.memset(xg[i][:], 0.0)
                    ins.then_inc(pchain, 1)
                    pool.wait_ge(slot_out, 16 * NPAIR)
                    pool.dma_start(slots[:], slot_rows[0:BLK]).then_inc(slots_in, 16)
                    pool.wait_ge(pchain, 2)
                    for i in range(2):
                        pool.wait_ge(h2_out[i], 32)
                    pool.wait_ge(slots_in, 16)
                    pool.wait_ge(cnt_ready, 2)
                    for j in range(3):
                        gather(0, j)
                    for j in range(8):
                        step(0, j)
                    with pool.Fori(1, NE // 8 - 1) as it:
                        for j in range(8):
                            step(it, j)
                    for j in range(8):
                        step(NE // 8 - 1, j)
                    scatter(NE // 8 - 1, 7)
                    nb = blocks(pool)
                    with pool.If(nb > 0):
                        with pool.Fori(0, nb) as i:
                            pool.wait_ge(o_load, 32 * i + 32)
                            pool.sem_inc(settled, 1)
                            nc.gpsimd.indirect_dma_start(
                                out=xg[0][:], out_offset=None, in_=h2_d,
                                in_offset=bass.IndirectOffsetOnAxis(ap=idx[0][:, 0:1].bitcast(U32), axis=0),
                                bounds_check=S - 1, oob_is_err=False).then_inc(o_gat, 16)
                            pool.wait_ge(o_yA, i + 1)
                            pool.wait_ge(o_yD, i + 1)
                            pool.sem_inc(settled, 1)
                            nc.gpsimd.indirect_dma_start(
                                out=y_d, out_offset=bass.IndirectOffsetOnAxis(ap=idx[0][:, 1:2].bitcast(U32), axis=0),
                                in_=y[0][:], in_offset=None, bounds_check=S * TOPK - 1, oob_is_err=False
                            ).then_inc(o_put, 16)
                            pool.wait_ge(o_put, 16 * i + 16)
                            pool.sem_inc(o_turn, 1)
                    for s in range(4):
                        pool.wait_ge(y_out[s], 16 * (NE // 4))

                @block.scalar
                def _(act):
                    norm_squares(act, "x2", xT)
                    split_hi(act, MIX_TILES)
                    act_norm_apply(act, "x2", mod[:, 24:32], h_hi, [hf[:, k, :] for k in range(KD)])
                    act.wait_ge(logits_ready, 1)
                    nc.scalar.activation(sgt[0:NE, :], OB[0:NE, :], ACT.Sigmoid).then_inc(score_ready, 1)
                    for t in range(TC):
                        for b in range(2):
                            act.wait_ge(htr_ready, 2 * t + b + 1)
                            if t >= 2:
                                act.wait_ge(h2_out[t % 2], 16 * (t // 2))
                            nc.scalar.activation(htok[t % 2][:, b * S:(b + 1) * S], TB[b][:], ACT.Copy
                                                 ).then_inc(htr_copied[b], 1)
                        act.wait_ge(htr_copied[0], t + 1)
                        act.wait_ge(htr_copied[1], t + 1)
                        act.dma_start(h2_d[t * P:(t + 1) * P, :], htok[t % 2][:]).then_inc(h2_out[t % 2], 16)
                    act_stream(act, events_of(whole(jobs["shared"])), NTILES)

                    def step(it, j, first=False, last=False):
                        e = 8 * it + j
                        if not (last and j == 7):
                            copy_half(act, e + 1, (j + 1) % 2)
                        silu(e, j % 2)
                        act.wait_ge(act_done, e + 1)
                        if not (isinstance(e, int) and e < 2):
                            act.wait_ge(dn_ready, e - 1)
                        nc.scalar.activation(a_hi[j % 2][:], actT[j % 2][:], ACT.Copy).then_inc(ahi_ready, 1)
                        if not (first and j == 0):
                            scale_half(act, it, j - 1)
                        act.wait_ge(ew_in[j % 4], 16 * (2 * it + j // 4 + 1))
                        nc.scalar.activation(d_hi[:], ew[j % 4][:, KD * 512:].rearrange("p (f c) -> p f c", f=2),
                                             ACT.Copy).then_inc(dhi_ready, 1)

                    def silu(e, s):
                        act.wait_ge(gu_ready, e + 1)
                        if not (isinstance(e, int) and e < 2):
                            act.wait_ge(act_done, e - 1)
                        nc.scalar.activation(sil[s][:], G[s][:, 0:2 * BLK].rearrange("p (f t) -> p f t", f=2),
                                             ACT.Silu).then_inc(silu_done, 1)

                    copy_half(act, 0, 0)
                    for j in range(8):
                        step(0, j, first=True)
                    with act.Fori(1, NE // 8 - 1) as it:
                        for j in range(8):
                            step(it, j)
                    for j in range(8):
                        step(NE // 8 - 1, j, last=True)
                    scale_half(act, NE // 8 - 1, 7)
                    nb = blocks(act)
                    with act.If(nb > 0):
                        with act.Fori(0, nb) as i:
                            act.wait_ge(o_xt, i + 1)
                            nc.scalar.activation(xgT[0][:, 0:4, :], TB[0][:].rearrange("p (k t) -> p k t", k=4),
                                                 ACT.Copy).then_inc(o_xcA, 1)
                            act.wait_ge(o_gu, i + 1)
                            nc.scalar.activation(sil[0][:], G[0][:, 0:2 * BLK].rearrange("p (f t) -> p f t", f=2),
                                                 ACT.Silu).then_inc(o_sil, 1)
                            act.wait_ge(o_dn, i + 1)
                            nc.scalar.activation(y[0][:, 0:S], SB[0][:], ACT.Copy,
                                                 scale=idx[0][:, 2:3].bitcast(F32)).then_inc(o_yA, 1)

                @block.vector
                def _(dve):
                    norm_squares(dve, "x2", xT)
                    dve_norm_mean(dve, "x2")
                    link(dve, nc.vector.scalar_tensor_tensor(amul[:], mod[:, 32:40], 1.0, vec[:, V_GFFN:V_GFFN + 8],
                                                             ALU.add, ALU.mult))
                    split_lo(dve, MIX_TILES)
                    dve_norm_apply(dve, "x2", xT, amul, mod[:, 24:32], h_hi, h_lo, [hf[:, k, :] for k in range(KD)])
                    dve.wait_ge(logits_ready, 2)
                    link(dve, nc.vector.tensor_copy(score[:], SB[0][:, 0:TC * NE].rearrange("p (t e) -> p t e", t=TC)))
                    link(dve, nc.vector.tensor_tensor(biased[:], score[:], vec[:, V_RB:V_RB + NE].unsqueeze(1)
                                                      .broadcast_to([P, TC, NE]), ALU.add))
                    for t in range(TC):
                        link(dve, nc.vector.max(top[:, t, :], biased[:, t, :]))
                        ins = nc.vector.max_index(topi[:, t, :], top[:, t, :], biased[:, t, :])
                    link(dve, ins)
                    link(dve, nc.vector.tensor_copy(topf[:], topi[:]))
                    four = [P, TC, TOPK, NE]
                    oh = onehot[:].rearrange("p (t k) e -> p t k e", t=TC)
                    om = ohmul[:].rearrange("p (t k) e -> p t k e", t=TC)
                    iota = rcst[:, K_IOTA:K_IOTA + NE]
                    link(dve, nc.vector.tensor_tensor(oh, iota.unsqueeze(1).unsqueeze(1).broadcast_to(four),
                                                      topf[:, :, 0:TOPK].unsqueeze(3).broadcast_to(four), ALU.is_equal))
                    nc.vector.tensor_reduce(sel[:], onehot[:].rearrange("p (t k) e -> p t e k", t=TC), AX.X,
                                            ALU.add).then_inc(sel_ready, 1)
                    link(dve, nc.vector.tensor_tensor(om, oh, score[:].unsqueeze(2).broadcast_to(four), ALU.mult))
                    link(dve, nc.vector.tensor_reduce(gsel[:], om, AX.X, ALU.add))
                    link(dve, nc.vector.tensor_reduce(gsum[:, 0:TC], gsel[:], AX.X, ALU.add))
                    link(dve, nc.vector.reciprocal(gsum[:, 4:8], gsum[:, 0:TC]))
                    link(dve, nc.vector.tensor_tensor(gsel[:], gsel[:], gsum[:, 4:8].unsqueeze(2).broadcast_to([P, TC, TOPK]),
                                                      ALU.mult))
                    dve.wait_ge(rw_in, 48)
                    nc.vector.tensor_scalar(pay[:, :, 2].bitcast(F32), gsel[:].rearrange("p t k -> p (t k)"), 2.5, None,
                                            ALU.mult)
                    dve.wait_ge(rank_ready, 1)
                    nc.vector.tensor_copy(cnt[0:NE, 0:1], SB[1][0:NE, 0:1]).then_inc(cnt_read, 1)
                    link(dve, nc.vector.scalar_tensor_tensor(
                        posn[:], SB[0][:, 0:TC * NE].rearrange("p (t e) -> p t e", t=TC), float(NE),
                        iota.unsqueeze(1).broadcast_to([P, TC, NE]), ALU.mult, ALU.add))
                    link(dve, nc.vector.tensor_tensor(om, oh, posn[:].unsqueeze(2).broadcast_to(four), ALU.mult))
                    link(dve, nc.vector.tensor_reduce(destf[:].rearrange("p (t k) -> p t k", t=TC), om, AX.X, ALU.add))
                    nc.vector.tensor_copy(dest[:], destf[:]).then_inc(dest_ready, 1)
                    dve.wait_ge(cnt_read, 1)
                    n = cnt[0:NE, 0:1]
                    link(dve, nc.vector.tensor_scalar(cnt[0:NE, 1:2], n, float(BLK), None, ALU.is_gt))
                    link(dve, nc.vector.scalar_tensor_tensor(cnt[0:NE, 2:3], n, float(2 * BLK), cnt[0:NE, 1:2], ALU.is_gt, ALU.add))
                    nc.vector.scalar_tensor_tensor(cnt[0:NE, 3:4], n, float(3 * BLK), cnt[0:NE, 2:3], ALU.is_gt,
                                                   ALU.add).then_inc(cnt_ready, 1)
                    dve_stream(dve, events_of(whole(jobs["shared"])), NTILES)
                    dve.wait_ge(o_list, 1)
                    link(dve, nc.vector.tensor_copy(cnt[0:NE, 4:5], SB[0][0:NE, 0:1]))
                    nc.vector.tensor_scalar(cmpt[0:NE, :], rcst[0:NE, K_IOTA32:K_IOTA32 + 48], cnt[0:NE, 4:5], None,
                                            ALU.is_ge).then_inc(cmp_ready, 1)
                    dve.wait_ge(o_list, 2)
                    f = ovff[0:1, :, :]
                    link(dve, nc.vector.tensor_tensor(f[:, 1, :], rcst[0:1, K_IOTA32:K_IOTA32 + 48], SB[1][0:1, 64:112],
                                                      ALU.subtract))
                    link(dve, nc.vector.tensor_scalar(f[:, 1, :], f[:, 1, :], 1.0, 128.0, ALU.add, ALU.mult))
                    nc.vector.tensor_copy(ovf[0:1, 0, :], SB[1][0:1, 0:48])
                    nc.vector.tensor_copy(novf[0:1, 0:1], SB[1][0:1, 128:129])
                    nc.vector.tensor_copy(cntrow[0:1, :], SB[1][0:1, 192:192 + NE])
                    nc.vector.tensor_copy(ovf[0:1, 1, :], f[:, 1, :]).then_inc(cnt_ready, 1)

                    def step(it, j, first=False, last=False):
                        e = 8 * it + j
                        if not (last and j == 7):
                            copy_half(dve, e + 1, (j + 1) % 2)
                        gated_up(e, j % 2)
                        dve.wait_ge(ahi_ready, e + 1)
                        nc.vector.tensor_tensor(a_lo[j % 2][:], actT[j % 2][:], a_hi[j % 2][:].bitcast(F32),
                                                ALU.subtract).then_inc(alo_ready, 1)
                        if not (first and j == 0):
                            scale_half(dve, it, j - 1)
                        dve.wait_ge(dhi_ready, e + 1)
                        nc.vector.tensor_tensor(d_lo[:], ew[j % 4][:, KD * 512:].rearrange("p (f c) -> p f c", f=2),
                                                d_hi[:].bitcast(F32), ALU.subtract).then_inc(dlo_ready, 1)

                    def gated_up(e, s):
                        dve.wait_ge(silu_done, e + 1)
                        if not (isinstance(e, int) and e < 2):
                            dve.wait_ge(ahi_ready, e - 1)
                            dve.wait_ge(alo_ready, e - 1)
                        nc.vector.tensor_tensor(actT[s][:], sil[s][:], G[s][:, 2 * BLK:].rearrange("p (f t) -> p f t", f=2),
                                                ALU.mult).then_inc(act_done, 1)

                    copy_half(dve, 0, 0)
                    for j in range(8):
                        step(0, j, first=True)
                    with dve.Fori(1, NE // 8 - 1) as it:
                        for j in range(8):
                            step(it, j)
                    for j in range(8):
                        step(NE // 8 - 1, j, last=True)
                    scale_half(dve, NE // 8 - 1, 7)
                    nb = blocks(dve)
                    with dve.If(nb > 0):
                        with dve.Fori(0, nb) as i:
                            dve.wait_ge(o_xt, i + 1)
                            nc.vector.tensor_copy(xgT[0][:, 4:8, :], TB[1][:].rearrange("p (k t) -> p k t", k=4)
                                                  ).then_inc(o_xcD, 1)
                            dve.wait_ge(o_sil, i + 1)
                            nc.vector.tensor_tensor(actT[0][:], sil[0][:],
                                                    G[0][:, 2 * BLK:].rearrange("p (f t) -> p f t", f=2),
                                                    ALU.mult).then_inc(o_act, 1)
                            dve.wait_ge(o_dn, i + 1)
                            dve.sem_inc(o_wfree, 1)
                            nc.vector.tensor_scalar(y[0][:, S:D], SB[1][:], idx[0][:, 2:3].bitcast(F32), None,
                                                    ALU.mult).then_inc(o_yD, 1)

                @block.tensor
                def _(pe):
                    pe_norm_sums(pe, "x2")
                    pe_norm_spread(pe, "x2")
                    pe.wait_ge(rw_in, 48)
                    for k in range(KD):
                        pe.wait_ge(nhi_ready, norm_k0["x2"] + k + 1)
                        ins = nc.tensor.matmul(OB[0:NE, :], rw[:, k, :], hf[:, k, :], start=k == 0, stop=k == KD - 1)
                    ins.then_inc(logits_ready, 1)

                    def rows(t):
                        for b in range(2):
                            if t:
                                pe.wait_ge(htr_copied[b], t)
                            for k in range(4):
                                ins = nc.tensor.transpose(TB[b][:, k * P:(k + 1) * P],
                                                          hf[:, 4 * b + k, t * P:(t + 1) * P], ident)
                            ins.then_inc(htr_ready, 1)

                    rows(0)
                    pe.wait_ge(score_ready, 1)
                    for t in range(TC):
                        ins = nc.tensor.transpose(SB[0][:, t * NE:(t + 1) * NE], sgt[0:NE, t * P:(t + 1) * P],
                                                  ident[0:NE, 0:NE])
                    ins.then_inc(logits_ready, 1)
                    for t in range(1, TC):
                        rows(t)
                    pe.wait_ge(sel_ready, 1)
                    for t in range(TC):
                        for b in range(t + 1):
                            nc.tensor.matmul(SB[0][:, t * NE:(t + 1) * NE], ones[:] if b < t else rcst[:, K_UP:K_UP + P],
                                             sel[:, b, :], start=b == 0, stop=b == t)
                    for t in range(TC):
                        ins = nc.tensor.matmul(SB[1][0:NE, 0:1], sel[:, t, :], ones[:, 0:1], start=t == 0, stop=t == TC - 1)
                    ins.then_inc(rank_ready, 1)
                    for j in jobs["shared"]:
                        pe_products(pe, j, 0, n_products(j))
                    pe.wait_ge(cnt_ready, 1)
                    nc.tensor.matmul(SB[0][0:NE, 0:1], rcst[0:NE, K_UPI:K_UPI + NE], cnt[0:NE, 3:4], start=True,
                                     stop=True).then_inc(o_list, 1)
                    pe.wait_ge(cmp_ready, 1)
                    nc.tensor.matmul(SB[1][0:1, 0:48], ones[0:NE, 0:1], cmpt[0:NE, :], start=True, stop=True)
                    nc.tensor.matmul(SB[1][0:1, 64:112], cnt[0:NE, 3:4], cmpt[0:NE, :], start=True, stop=True)
                    nc.tensor.matmul(SB[1][0:1, 192:192 + NE], cnt[0:NE, 0:1], ident[0:NE, 0:NE], start=True, stop=True)
                    nc.tensor.matmul(SB[1][0:1, 128:129], cnt[0:NE, 3:4], ones[0:NE, 0:1], start=True,
                                     stop=True).then_inc(o_list, 1)

                    def transposes(e, s, it):
                        pe.wait_ge(xg_in[s], 16 * (it + 1))
                        if not (isinstance(e, int) and e == 0):
                            pe.wait_ge(xt_copA, e)
                            pe.wait_ge(xt_copD, e)
                        else:
                            pe.wait_ge(htr_copied[0], TC)
                            pe.wait_ge(htr_copied[1], TC)
                        for k in range(KD):
                            ins = nc.tensor.transpose(TB[k // 4][:, k % 4 * P:(k % 4 + 1) * P],
                                                      xg[s][:, k * P:(k + 1) * P], ident)
                        ins.then_inc(xt_ready, 1)

                    def gate_up(e, s, it):
                        pe.wait_ge(xt_copA, e + 1)
                        pe.wait_ge(xt_copD, e + 1)
                        pe.wait_ge(ew_in[s], 16 * (it + 1))
                        if isinstance(e, int) and e < 2:
                            wait_chunk_out(pe, len(all_jobs) - 2 + e)
                        else:
                            pe.wait_ge(act_done, e - 1)
                        w = ew[s][:, 0:KD * 512].rearrange("p (k c) -> p k c", k=KD)
                        for f in range(4):
                            for k in range(KD):
                                ins = nc.tensor.matmul(G[s % 2][:, f * BLK:(f + 1) * BLK], w[:, k, f * P:(f + 1) * P],
                                                       xgT[s % 2][:, k, :], start=k == 0, stop=k == KD - 1)
                        ins.then_inc(gu_ready, 1)

                    def down(e, s):
                        pe.wait_ge(alo_ready, e + 1)
                        pe.wait_ge(dlo_ready, e + 1)
                        if not (isinstance(e, int) and e < 2):
                            pe.wait_ge(yA, e - 1)
                            pe.wait_ge(yD, e - 1)
                        else:
                            pe.wait_ge(cnt_ready, 2)
                        for h, bank in enumerate((SB, (OB, MB))[s % 2]):
                            for f in range(2):
                                for i, (a, w) in enumerate(((a_hi, d_hi), (a_hi, d_lo), (a_lo, d_hi))):
                                    ins = nc.tensor.matmul(bank[:], a[s % 2][:, f, :], w[:, f, h * S:(h + 1) * S],
                                                           start=(f, i) == (0, 0), stop=(f, i) == (1, 2))
                        ins.then_inc(dn_ready, 1)

                    def step(it, j, first=False, last=False):
                        e = 4 * it + j
                        if not (last and j == 3):
                            transposes(e + 1, (j + 1) % 4, it + (1 if j == 3 else 0))
                        gate_up(e, j, it)
                        if not (first and j == 0):
                            down(e - 1, (j - 1) % 4)

                    transposes(0, 0, 0)
                    for j in range(4):
                        step(0, j, first=True)
                    with pe.Fori(1, NE // 4 - 1) as it:
                        for j in range(4):
                            step(it, j)
                    for j in range(4):
                        step(NE // 4 - 1, j, last=True)
                    down(NE - 1, 3)
                    nb = blocks(pe)
                    pe.wait_ge(yA, NE)
                    pe.wait_ge(yD, NE)
                    w = ew[0][:, 0:KD * 512].rearrange("p (k c) -> p k c", k=KD)
                    wd = ew[0][:, KD * 512:].rearrange("p (f c) -> p f c", f=2)
                    with pe.If(nb > 0):
                        with pe.Fori(0, nb) as i:
                            pe.wait_ge(o_gat, 16 * i + 16)
                            for k in range(KD):
                                ins = nc.tensor.transpose(TB[k // 4][:, k % 4 * P:(k % 4 + 1) * P],
                                                          xg[0][:, k * P:(k + 1) * P], ident)
                            ins.then_inc(o_xt, 1)
                            pe.wait_ge(o_xcA, i + 1)
                            pe.wait_ge(o_xcD, i + 1)
                            for f in range(4):
                                for k in range(KD):
                                    ins = nc.tensor.matmul(G[0][:, f * BLK:(f + 1) * BLK], w[:, k, f * P:(f + 1) * P],
                                                           xgT[0][:, k, :], start=k == 0, stop=k == KD - 1)
                            ins.then_inc(o_gu, 1)
                            pe.wait_ge(o_act, i + 1)
                            for h in range(2):
                                for f in range(2):
                                    ins = nc.tensor.matmul(SB[h][:], actT[0][:, f, :], wd[:, f, h * S:(h + 1) * S],
                                                           start=f == 0, stop=f == 1)
                            ins.then_inc(o_dn, 1)

            y_rows = y_d.rearrange("(t k) d -> t k d", k=TOPK)
            with nc.Block() as block:
                @block.sync
                def _(sp):
                    for t in range(TC):
                        if t >= 2:
                            sp.wait_ge(ytr, 2 * (t - 1))
                        sp.dma_start(yt[t % 2][:], y_rows[t * P:(t + 1) * P]).then_inc(yt_in[t % 2], 16)

                @block.vector
                def _(dve):
                    def add_back(t):
                        for b in range(2):
                            dve.wait_ge(ytr, 2 * t + b + 1)
                            for k in range(4):
                                x = xT[:, 4 * b + k, t * P:(t + 1) * P]
                                ins = nc.vector.scalar_tensor_tensor(x, G[b][:, k * P:(k + 1) * P],
                                                                     mod[:, 40 + 4 * b + k:41 + 4 * b + k], x, ALU.mult, ALU.add)
                            ins.then_inc(yadd[b], 1)
                    for t in range(TC):
                        v = yt[t % 2]
                        dve.wait_ge(yt_in[t % 2], 16 * (t // 2 + 1))
                        link(dve, nc.vector.tensor_tensor(v[:, 0:3, :], v[:, 0:3, :], v[:, 3:6, :], ALU.add))
                        link(dve, nc.vector.tensor_tensor(v[:, 0, :], v[:, 0, :], v[:, 1, :], ALU.add))
                        nc.vector.tensor_tensor(v[:, 0, :], v[:, 0, :], v[:, 2, :], ALU.add).then_inc(ysum, 1)
                        if t:
                            add_back(t - 1)
                    add_back(TC - 1)

                @block.tensor
                def _(pe):
                    for t in range(TC):
                        pe.wait_ge(ysum, t + 1)
                        for b in range(2):
                            if t:
                                pe.wait_ge(yadd[b], t)
                            for k in range(4):
                                ins = nc.tensor.transpose(G[b][:, k * P:(k + 1) * P],
                                                          yt[t % 2][:, 0, (4 * b + k) * P:(4 * b + k + 1) * P], ident)
                            ins.then_inc(ytr, 1)
            nc.gpsimd.dma_reset(per_layer)
            nc.all_engine_barrier(sems_to_clear=per_layer)

        with nc.Block() as block:
            norm_no["end"], norm_k["end"], norm_k0["end"] = 0, KD, 0
            m_use[("st", "end")] = m_use[("rb", "end")] = 0
            m_full_no[("rb", "end")] = 0

            @block.sync
            def _(sp):
                for k in range(KD):
                    sp.wait_ge(nt_ready, k + 1)
                    sp.dma_start(out_d[:, k, :], hf[:, k, :]).then_inc(init_out, 16)
                sp.wait_ge(init_out, 16 + 16 * KD)

            @block.gpsimd
            def _(pool):
                pool_norm_root(pool, "end")

            @block.scalar
            def _(act):
                norm_squares(act, "end", xT)

            @block.tensor
            def _(pe):
                pe_norm_sums(pe, "end")
                pe_norm_spread(pe, "end")

            @block.vector
            def _(dve):
                norm_squares(dve, "end", xT)
                dve_norm_mean(dve, "end")
                wait_mb_full(dve, ("rb", "end"))
                for k in range(KD):
                    nc.vector.scalar_tensor_tensor(hf[:, k, :], xT[:, k, :], gvec[:, k:k + 1], MB[:], ALU.mult,
                                                   ALU.mult).then_inc(nt_ready, 1)


def _bucket(rel):
    half, exact = 16, 8
    ret = np.where(rel > 0, half, 0)
    n = np.abs(rel)
    large = exact + (np.log(np.maximum(n, 1).astype(np.float32) / np.float32(exact)) / np.float32(math.log(1024 / exact))
                     * np.float32(half - exact)).astype(np.int32)
    return ret + np.where(n < exact, n, np.minimum(large, half - 1))


def _constants():
    c, rc = np.zeros((P, NCONST), np.float32), np.zeros((P, NROUTE), np.float32)
    i = np.arange(P)
    c[:, K_ID:K_ID + P] = np.eye(P)
    rc[:, K_UP:K_UP + P] = i[:, None] < i[None, :]
    rc[:64, K_UPI:K_UPI + 64] = i[:64, None] <= i[None, :64]
    rc[:, K_IOTA:K_IOTA + 64] = np.arange(64)
    h = ROPE // 2
    for m in range(h):
        c[NOPE + h + m, K_PROT + m] = -1.0
        c[NOPE + m, K_PROT + h + m] = 1.0
    rc[:, K_IOTA32:K_IOTA32 + 48] = np.arange(48)
    onehot = np.zeros((32, VLEN), np.float32)
    onehot[_bucket(np.arange(VLEN) - (S - 1)), np.arange(VLEN)] = 1.0
    inv = np.float32(10000.0) ** (-np.arange(0, ROPE, 2, dtype=np.float32) / np.float32(ROPE))
    ang = np.arange(S, dtype=np.float32)[None, :] * inv[:, None]
    rope = np.stack([np.tile(np.cos(ang), (2, 1)), np.tile(np.sin(ang), (2, 1))], 1).astype(np.float32)
    pay = np.zeros((P, TC, TOPK, 4), np.int32)
    tok = np.arange(TC)[None, :, None] * P + i[:, None, None]
    pay[..., 0] = tok
    pay[..., 1] = tok * TOPK + np.arange(TOPK)
    skip = np.full((NE * S, 4), SKIP, np.int32)
    return c, rc, onehot, rope, pay.reshape(P, NPAIR, 4), skip


def _tile(a, k):
    n = a.shape[1]
    t = a.reshape(k, P, n).transpose(1, 0, 2).reshape(P, k * n)
    return t if t.shape[1] == 1024 else np.concatenate([t, np.zeros((P, 1024 - t.shape[1]), a.dtype)], 1)


def _ada_tile(w, l, i):
    return w["ada_w"][l][:, i * P:(i + 1) * P].T


def _lay_out_tiles(w, l):
    out = []
    for t in TILES:
        if t[0] == "ada":
            out.append(_ada_tile(w, l if t[1] >= 16 else (l + 1) % L, t[1]))
        elif t[0] == "in":
            out.append(_tile(w["w_in"][l][:, t[1]:t[1] + P], KD))
        elif t[0] == "kvup":
            out.append(_tile(w["w_kv_up"][l], 1))
        elif t[0] == "qup":
            out.append(_tile(w["w_q_up"][l][:, t[1] * 384:(t[1] + 1) * 384], 2))
        elif t[0] == "branch":
            out.append(_tile(w["w_branch"][l, t[1]][:, t[2] * 256:(t[2] + 1) * 256], 4))
        elif t[0] == "out":
            out.append(_tile(w["w_out"][l][:, t[1] * P:(t[1] + 1) * P], KD))
        elif t[0] == "sgu":
            out.append(_tile(w["w_shared_gu"][l][:, t[1] * P:(t[1] + 1) * P], KD))
        else:
            out.append(_tile(w["w_shared_down"][l][:, t[1] * 512:(t[1] + 1) * 512], 2))
    return np.stack(out)


def _columns(v):
    return v.reshape(-1, P).T


def kernel(**inputs):
    import concourse.bacc as bacc
    from concourse.bass_utils import run_bass_kernel_spmd

    w = {k: np.asarray(v) for k, v in inputs.items()}
    const, rcst, onehot, rope, pay, skip = _constants()
    vecs = []
    for l in range(L):
        li = 0.8 - 0.6 * math.exp(-0.3 * l)
        rep = lambda a: np.broadcast_to(a.reshape(1, -1), (P, a.size))
        vecs.append(np.concatenate([
            _columns(w["ada_b"][(l + 1) % L])[:, 0:16], _columns(w["ada_b"][l])[:, 16:], _columns(w["norm_mix_g"][l]), _columns(w["norm_ffn_g"][l]),
            _columns(w["q_norm_g"][l]), _columns(w["kv_norm_g"][l]), _columns(w["diff_subln_g"][l]),
            rep(np.repeat(w["sinks_d"][l], TC)), np.full((P, 1), li, np.float32), np.full((P, 1), 1.0 - li, np.float32),
            rep(w["router_bias"][l]), rep(w["diff_lambda"][l])], 1))
    at = np.clip(P - 1 - np.arange(P)[:, None] + np.arange(S)[None, :], 0, VLEN - 1)
    at = np.clip(S - 1 - at, -63, 256) + 63
    arrays = {
        "xT": np.ascontiguousarray(w["x"][0].T.reshape(KD, P, S).transpose(1, 0, 2)),
        "wmix": np.concatenate([_lay_out_tiles(w, l) for l in range(L)]),
        "wexp": np.concatenate([
            w["w_exp_gu"].reshape(L * NE, KD, P, 512).transpose(0, 2, 1, 3).reshape(L * NE, P, KD * 512),
            w["w_exp_down"].reshape(L * NE, 2, P, D).transpose(0, 2, 1, 3).reshape(L * NE, P, 2 * D)], 2),
        "vec": np.stack(vecs),
        "gvec": np.concatenate([_columns(w["final_norm_g"]), _columns(w["ada_b"][0])[:, 0:16]], 1),
        "cb": np.broadcast_to(w["c"], (P, D)),
        "ada0": np.stack([_ada_tile(w, 0, i) for i in range(16)], 1),
        "rw": np.ascontiguousarray(w["router_w"].reshape(L, KD, P, NE).transpose(0, 2, 1, 3)),
        "vb": np.ascontiguousarray(w["rel_bias_b"][:, :, at]),
        "t5": w["t5_table"], "const": const, "rcst": rcst, "onehot": onehot, "rope": rope, "pay": pay, "skip": skip,
    }
    nc = bacc.Bacc("TRN2", target_bir_lowering=False, num_devices=1)
    aps = [nc.dram_tensor(f"in_{n}", a.shape, mybir.dt.from_np(a.dtype), kind="ExternalInput").ap() for n, a in arrays.items()]
    out = nc.dram_tensor("out", [P, KD, S], F32, kind="ExternalOutput").ap()
    hybrid_trunk(nc, *aps, out)
    r = run_bass_kernel_spmd(nc, [{f"in_{n}": np.ascontiguousarray(a) for n, a in arrays.items()}], core_ids=[0])
    o = np.asarray(r.results[0]["out"])
    return np.ascontiguousarray(o.transpose(2, 1, 0).reshape(1, S, D))
```
